# Optimizing a Trainium2 kernel written in Bass

```python
import math
import jax, jax.numpy as jnp
from jax import lax
import numpy as np

D_MODEL = 1024
BATCH = 1
SEQ = 256
DEPTH = 2

CHUNK = 64
Q_BLOCK = 128
MEM_LEN = 256

A_HEADS = 8
A_HEAD_DIM = 64
A_LEFT_CHUNKS = 8
A_BAND = (A_LEFT_CHUNKS + 1) * CHUNK
A_REL_MIN = -(CHUNK - 1)
A_REL_MAX = 256
A_REL_SIZE = A_REL_MAX - A_REL_MIN + 1

B_HEADS = 8
B_Q_LORA = 384
B_KV_LORA = 256
B_NOPE = 64
B_ROPE = 32
B_V = 64
ROPE_BASE = 10000.0

C_HEADS = 8
C_HEAD_DIM = 64

N_BRANCHES = 3
BRANCH_WIDTH = 512

A_COLS = 3 * A_HEADS * A_HEAD_DIM
B_COLS = B_Q_LORA + B_KV_LORA + B_ROPE
C_COLS = 3 * C_HEADS * C_HEAD_DIM
GATE_COLS = N_BRANCHES * D_MODEL
IN_COLS = A_COLS + B_COLS + C_COLS + C_HEADS + GATE_COLS

XA_HEADS = 4
XA_HEAD_DIM = 128

FFN_HIDDEN = ((8 * D_MODEL // 3 + 255) // 256) * 256

LN_EPS = 1e-5
RMS_EPS = 1e-6


def layer_norm(x, g, b):
    xf = x.astype(jnp.float32)
    mu = jnp.mean(xf, axis=-1, keepdims=True)
    var = jnp.mean(jnp.square(xf - mu), axis=-1, keepdims=True)
    return ((xf - mu) * lax.rsqrt(var + LN_EPS) * g.astype(jnp.float32) + b.astype(jnp.float32)).astype(x.dtype)

def rms_norm(x, g):
    xf = x.astype(jnp.float32)
    ms = jnp.mean(jnp.square(xf), axis=-1, keepdims=True)
    return (xf * lax.rsqrt(ms + RMS_EPS) * g.astype(jnp.float32)).astype(x.dtype)

def rope(x, pos):
    half = x.shape[-1] // 2
    inv_freq = ROPE_BASE ** (-jnp.arange(half, dtype=jnp.float32) / half)
    ang = pos.astype(jnp.float32)[..., None] * inv_freq
    ang = ang.reshape(ang.shape[:2] + (1,) * (x.ndim - 3) + (half,))
    cos, sin = jnp.cos(ang), jnp.sin(ang)
    x1 = x[..., :half].astype(jnp.float32)
    x2 = x[..., half:].astype(jnp.float32)
    return jnp.concatenate([x1 * cos - x2 * sin, x2 * cos + x1 * sin], axis=-1).astype(x.dtype)

def split_cols(h, widths):
    out, off = [], 0
    for w in widths:
        out.append(h[..., off:off + w])
        off += w
    return out

def chunked_relpos_attention(q, k, v, rel_bias):
    B, S, H, Dh = q.shape
    nc = S // CHUNK
    pad = A_LEFT_CHUNKS * CHUNK
    kp = jnp.pad(k, ((0, 0), (pad, 0), (0, 0), (0, 0))).reshape(B, nc + A_LEFT_CHUNKS, CHUNK, H, Dh)
    vp = jnp.pad(v, ((0, 0), (pad, 0), (0, 0), (0, 0))).reshape(B, nc + A_LEFT_CHUNKS, CHUNK, H, Dh)
    k_band = jnp.concatenate([kp[:, j:j + nc] for j in range(A_LEFT_CHUNKS + 1)], axis=2)
    v_band = jnp.concatenate([vp[:, j:j + nc] for j in range(A_LEFT_CHUNKS + 1)], axis=2)
    qc = q.reshape(B, nc, CHUNK, H, Dh)
    s = jnp.einsum('bcqhd,bckhd->bchqk', qc, k_band).astype(jnp.float32) * (Dh ** -0.5)
    qi = jnp.arange(CHUNK)[:, None]
    kj = jnp.arange(A_BAND)[None, :]
    rel = pad + qi - kj
    idx = jnp.clip(rel, A_REL_MIN, A_REL_MAX) - A_REL_MIN
    bias = rel_bias.astype(jnp.float32)[:, idx]
    s = s + bias[None, None]
    chunk_ids = jnp.arange(nc)[:, None]
    valid = (chunk_ids * CHUNK - pad + kj) >= 0
    s = jnp.where(valid[None, :, None, None, :], s, -jnp.inf)
    p = jax.nn.softmax(s, axis=-1).astype(v.dtype)
    o = jnp.einsum('bchqk,bckhd->bcqhd', p, v_band)
    return o.reshape(B, S, H * Dh)

def mla_attention(c_q, c_kv, k_rope_in, pos, q_norm_g, kv_norm_g, w_uq, w_ukv):
    B, S, _ = c_q.shape
    q = (rms_norm(c_q, q_norm_g) @ w_uq).reshape(B, S, B_HEADS, B_NOPE + B_ROPE)
    q_nope = q[..., :B_NOPE]
    q_pe = rope(q[..., B_NOPE:], pos)
    kv = (rms_norm(c_kv, kv_norm_g) @ w_ukv).reshape(B, S, B_HEADS, B_NOPE + B_V)
    k_nope, v = kv[..., :B_NOPE], kv[..., B_NOPE:]
    k_pe = rope(k_rope_in, pos)
    scale = (B_NOPE + B_ROPE) ** -0.5
    key_chunk = jnp.arange(S) // CHUNK

    def block(i):
        start = i * Q_BLOCK
        qn = lax.dynamic_slice_in_dim(q_nope, start, Q_BLOCK, axis=1)
        qp = lax.dynamic_slice_in_dim(q_pe, start, Q_BLOCK, axis=1)
        s = (jnp.einsum('bqhd,bkhd->bhqk', qn, k_nope).astype(jnp.float32)
             + jnp.einsum('bqhr,bkr->bhqk', qp, k_pe).astype(jnp.float32)) * scale
        q_chunk = (start + jnp.arange(Q_BLOCK)) // CHUNK
        mask = key_chunk[None, :] <= q_chunk[:, None]
        s = jnp.where(mask, s, -jnp.inf)
        p = jax.nn.softmax(s, axis=-1).astype(v.dtype)
        return jnp.einsum('bhqk,bkhd->bqhd', p, v)

    o = lax.map(block, jnp.arange(S // Q_BLOCK))
    return o.transpose(1, 0, 2, 3, 4).reshape(B, S, B_HEADS * B_V)

def forgetting_attention(q, k, v, f_logit):
    B, S, H, Dh = q.shape
    log_f = jax.nn.log_sigmoid(f_logit.astype(jnp.float32))
    F = jnp.cumsum(log_f, axis=1).transpose(0, 2, 1)
    scale = Dh ** -0.5
    key_pos = jnp.arange(S)

    def block(i):
        start = i * Q_BLOCK
        qb = lax.dynamic_slice_in_dim(q, start, Q_BLOCK, axis=1)
        Fq = lax.dynamic_slice_in_dim(F, start, Q_BLOCK, axis=2)
        s = jnp.einsum('bqhd,bkhd->bhqk', qb, k).astype(jnp.float32) * scale
        s = s + Fq[..., :, None] - F[..., None, :]
        mask = key_pos[None, :] <= (start + jnp.arange(Q_BLOCK))[:, None]
        s = jnp.where(mask, s, -jnp.inf)
        p = jax.nn.softmax(s, axis=-1).astype(v.dtype)
        return jnp.einsum('bhqk,bkhd->bqhd', p, v)

    o = lax.map(block, jnp.arange(S // Q_BLOCK))
    return o.transpose(1, 0, 2, 3, 4).reshape(B, S, H * Dh)

def hybrid_mixer(x, pos, w_in, b_gate, b_forget, a_rel_bias, b_q_norm, b_kv_norm,
                 b_w_uq, b_w_ukv, w_branch, w_out):
    B, S, _ = x.shape
    h = x @ w_in
    a_qkv, b_cq, b_ckv, b_kr, c_qkv, c_f, g = split_cols(
        h, [A_COLS, B_Q_LORA, B_KV_LORA, B_ROPE, C_COLS, C_HEADS, GATE_COLS])
    a_qkv = a_qkv.reshape(B, S, 3, A_HEADS, A_HEAD_DIM)
    y_a = chunked_relpos_attention(a_qkv[:, :, 0], a_qkv[:, :, 1], a_qkv[:, :, 2], a_rel_bias)
    y_b = mla_attention(b_cq, b_ckv, b_kr, pos, b_q_norm, b_kv_norm, b_w_uq, b_w_ukv)
    c_qkv = c_qkv.reshape(B, S, 3, C_HEADS, C_HEAD_DIM)
    y_c = forgetting_attention(c_qkv[:, :, 0], c_qkv[:, :, 1], c_qkv[:, :, 2], c_f + b_forget)
    branches = jnp.stack([y_a, y_b, y_c], axis=2)
    proj = jnp.einsum('bsnw,nwd->bsnd', branches, w_branch)
    gates = jax.nn.sigmoid(g.reshape(B, S, N_BRANCHES, D_MODEL) + b_gate)
    merged = jnp.sum(gates * proj, axis=2)
    return merged @ w_out

def memory_cross_attention(x, mem, w_q, w_kv, w_o):
    B, S, _ = x.shape
    M = mem.shape[1]
    q = (x @ w_q).reshape(B, S, XA_HEADS, XA_HEAD_DIM)
    kv = (mem @ w_kv).reshape(B, M, 2, XA_HEADS, XA_HEAD_DIM)
    s = jnp.einsum('bqhd,bkhd->bhqk', q, kv[:, :, 0]).astype(jnp.float32) * (XA_HEAD_DIM ** -0.5)
    p = jax.nn.softmax(s, axis=-1).astype(x.dtype)
    o = jnp.einsum('bhqk,bkhd->bqhd', p, kv[:, :, 1]).reshape(B, S, XA_HEADS * XA_HEAD_DIM)
    return o @ w_o

def swiglu_ffn(x, w_gu, w_down):
    gu = x @ w_gu
    g, u = gu[..., :FFN_HIDDEN], gu[..., FFN_HIDDEN:]
    return (jax.nn.silu(g) * u) @ w_down

def first_inputs(seed: int = 0) -> dict:
    key = jax.random.key(seed)
    ks = jax.random.split(key, 24)
    f32 = jnp.float32
    L = DEPTH
    beta = (8 * DEPTH) ** -0.25

    def w(k, shape, fan_in, scale=1.0):
        return jax.random.normal(k, shape, f32) * (scale * fan_in ** -0.5)

    def gain(k, shape):
        return 1.0 + 0.05 * jax.random.normal(k, shape, f32)

    def small(k, shape, s=0.02):
        return s * jax.random.normal(k, shape, f32)

    x = jax.random.normal(ks[0], (BATCH, SEQ, D_MODEL), f32)
    mem = jax.random.normal(ks[1], (BATCH, MEM_LEN, D_MODEL), f32)
    offs = jax.random.randint(ks[2], (BATCH, 1), 0, 16) * CHUNK
    positions = (jnp.arange(SEQ, dtype=jnp.int32)[None, :] + offs).astype(jnp.int32)

    return {
        "x": x,
        "mem": mem,
        "positions": positions,
        "ln_mix_g": gain(ks[3], (L, D_MODEL)),
        "ln_mix_b": small(ks[4], (L, D_MODEL)),
        "w_in": w(ks[5], (L, D_MODEL, IN_COLS), D_MODEL),
        "b_gate": small(ks[6], (L, N_BRANCHES, D_MODEL)),
        "b_forget": 3.0 + 0.5 * jax.random.normal(ks[7], (L, C_HEADS), f32),
        "a_rel_bias": small(ks[8], (L, A_HEADS, A_REL_SIZE), 0.5),
        "b_q_norm": gain(ks[9], (L, B_Q_LORA)),
        "b_kv_norm": gain(ks[10], (L, B_KV_LORA)),
        "b_w_uq": w(ks[11], (L, B_Q_LORA, B_HEADS * (B_NOPE + B_ROPE)), B_Q_LORA),
        "b_w_ukv": w(ks[12], (L, B_KV_LORA, B_HEADS * (B_NOPE + B_V)), B_KV_LORA),
        "w_branch": w(ks[13], (L, N_BRANCHES, BRANCH_WIDTH, D_MODEL), BRANCH_WIDTH),
        "w_mix_out": w(ks[14], (L, D_MODEL, D_MODEL), D_MODEL, beta),
        "ln_xa_g": gain(ks[15], (L, D_MODEL)),
        "ln_xa_b": small(ks[16], (L, D_MODEL)),
        "xa_w_q": w(ks[17], (L, D_MODEL, XA_HEADS * XA_HEAD_DIM), D_MODEL),
        "xa_w_kv": w(ks[18], (L, D_MODEL, 2 * XA_HEADS * XA_HEAD_DIM), D_MODEL),
        "xa_w_o": w(ks[19], (L, XA_HEADS * XA_HEAD_DIM, D_MODEL), XA_HEADS * XA_HEAD_DIM, beta),
        "ln_ffn_g": gain(ks[20], (L, D_MODEL)),
        "ln_ffn_b": small(ks[21], (L, D_MODEL)),
        "ffn_w_gu": w(ks[22], (L, D_MODEL, 2 * FFN_HIDDEN), D_MODEL),
        "ffn_w_down": w(ks[23], (L, FFN_HIDDEN, D_MODEL), FFN_HIDDEN, beta),
    }

def first_block(x, mem, positions, ln_mix_g, ln_mix_b, w_in, b_gate, b_forget, a_rel_bias,
              b_q_norm, b_kv_norm, b_w_uq, b_w_ukv, w_branch, w_mix_out, ln_xa_g, ln_xa_b,
              xa_w_q, xa_w_kv, xa_w_o, ln_ffn_g, ln_ffn_b, ffn_w_gu, ffn_w_down):
    alpha = (2 * DEPTH) ** 0.25
    for l in range(DEPTH):
        y = hybrid_mixer(x, positions, w_in[l], b_gate[l], b_forget[l], a_rel_bias[l],
                         b_q_norm[l], b_kv_norm[l], b_w_uq[l], b_w_ukv[l], w_branch[l], w_mix_out[l])
        x = layer_norm(alpha * x + y, ln_mix_g[l], ln_mix_b[l])
        y = memory_cross_attention(x, mem, xa_w_q[l], xa_w_kv[l], xa_w_o[l])
        x = layer_norm(alpha * x + y, ln_xa_g[l], ln_xa_b[l])
        y = swiglu_ffn(x, ffn_w_gu[l], ffn_w_down[l])
        x = layer_norm(alpha * x + y, ln_ffn_g[l], ln_ffn_b[l])
    return x


HEAD_DIM = 64
SB_HEADS = 4
DIL_HEADS = 4
HGRN_HEADS = 4
HGRN_DK = 128
HGRN_DV = 128
SB_WIDTH = SB_HEADS * HEAD_DIM
DIL_WIDTH = DIL_HEADS * HEAD_DIM
HGRN_WIDTH = HGRN_HEADS * HGRN_DV
HGRN_KDIM = HGRN_HEADS * HGRN_DK
MIX_WIDTH = SB_WIDTH + DIL_WIDTH + HGRN_WIDTH
IN_SPLITS = (SB_WIDTH, SB_WIDTH, SB_WIDTH, DIL_WIDTH, DIL_WIDTH, DIL_WIDTH, HGRN_KDIM, HGRN_KDIM, HGRN_WIDTH, HGRN_WIDTH)
IN_WIDTH = 3 * SB_WIDTH + 3 * DIL_WIDTH + 2 * HGRN_KDIM + 2 * HGRN_WIDTH
D_FF = 2816
QBLK = 128
HGRN_CHUNK = 64
DIL_PATTERNS = ((128, 1), (512, 4), (2048, 16))
ROPE_THETA = 10000.0
EPS = 1e-6
LB_FLOOR = 1e-30
NEG_BIG = -1e30
N_MOD = 9
HALF_STEP = 0.5


def _rmsnorm(x):
    xf = x.astype(jnp.float32)
    return (xf * lax.rsqrt(jnp.mean(xf * xf, axis=-1, keepdims=True) + EPS)).astype(x.dtype)

def _split_heads(x, n_heads):
    b, s, w = x.shape
    return x.reshape(b, s, n_heads, w // n_heads).transpose(0, 2, 1, 3)

def _merge_heads(x):
    b, h, s, d = x.shape
    return x.transpose(0, 2, 1, 3).reshape(b, s, h * d)

def _rope(x):
    s, d = x.shape[2], x.shape[3]
    half = d // 2
    inv_freq = ROPE_THETA ** (-jnp.arange(half, dtype=jnp.float32) * 2.0 / d)
    ang = jnp.arange(s, dtype=jnp.float32)[:, None] * inv_freq[None, :]
    cos, sin = jnp.cos(ang), jnp.sin(ang)
    xf = x.astype(jnp.float32)
    x1, x2 = xf[..., :half], xf[..., half:]
    return jnp.concatenate([x1 * cos - x2 * sin, x2 * cos + x1 * sin], axis=-1).astype(x.dtype)

def _swiglu(h, w_gate, w_up, w_down):
    return (jax.nn.silu(h @ w_gate) * (h @ w_up)) @ w_down

def _stick_breaking(q, k, v):
    b, h, s, d = q.shape
    nb = s // QBLK
    qf = q.astype(jnp.float32) * (d ** -0.5)
    kf = k.astype(jnp.float32)
    vf = v.astype(jnp.float32)
    q_blocks = qf.reshape(b, h, nb, QBLK, d).transpose(2, 0, 1, 3, 4)
    starts = jnp.arange(nb, dtype=jnp.int32) * QBLK
    kpos = jnp.arange(s, dtype=jnp.int32)

    def block(args):
        qb, start = args
        z = jnp.einsum('bhqd,bhkd->bhqk', qb, kf)
        qpos = start + jnp.arange(QBLK, dtype=jnp.int32)
        causal = kpos[None, :] < qpos[:, None]
        log_not_beta = jnp.where(causal, jax.nn.log_sigmoid(-z), 0.0)
        tail = lax.cumsum(log_not_beta, axis=3, reverse=True) - log_not_beta
        log_w = jnp.where(causal, jax.nn.log_sigmoid(z) + tail, NEG_BIG)
        w = jnp.exp(log_w)
        return jnp.einsum('bhqk,bhkd->bhqd', w, vf)

    out = lax.map(block, (q_blocks, starts))
    return out.transpose(1, 2, 0, 3, 4).reshape(b, h, s, d)

def _dilated_partial(q, k, v, window, dilation):
    b, h, s, d = q.shape
    steps = window // dilation
    sub_len = -(-s // (QBLK * dilation)) * QBLK
    pad = sub_len * dilation - s
    nb = sub_len // QBLK

    def to_residue(x):
        x = jnp.pad(x.astype(jnp.float32), ((0, 0), (0, 0), (0, pad), (0, 0)))
        x = x.reshape(b, h, sub_len, dilation, d).transpose(0, 1, 3, 2, 4)
        return x.reshape(b, h, dilation, nb, QBLK, d)

    qr, kr, vr = to_residue(q), to_residue(k), to_residue(v)

    def with_prev_block(x):
        prev = jnp.pad(x, ((0, 0), (0, 0), (0, 0), (1, 0), (0, 0), (0, 0)))[:, :, :, :-1]
        return jnp.concatenate([prev, x], axis=4)

    kw, vw = with_prev_block(kr), with_prev_block(vr)
    scores = jnp.einsum('bhrnqd,bhrnkd->bhrnqk', qr, kw)
    a_idx = jnp.arange(QBLK)[:, None]
    k_idx = jnp.arange(2 * QBLK)[None, :]
    dist = a_idx + QBLK - k_idx
    band = (dist >= 0) & (dist <= steps)
    valid = band[None] & ((jnp.arange(nb)[:, None, None] > 0) | (k_idx[None] >= QBLK))
    scores = jnp.where(valid, scores, NEG_BIG)
    mx = jnp.max(scores, axis=-1)
    p = jnp.where(valid, jnp.exp(scores - mx[..., None]), 0.0)
    den = jnp.sum(p, axis=-1)
    num = jnp.einsum('bhrnqk,bhrnkd->bhrnqd', p, vw)

    def back(x):
        x = x.reshape((b, h, dilation, sub_len) + x.shape[5:])
        perm = (0, 1, 3, 2) + tuple(range(4, x.ndim))
        x = x.transpose(perm).reshape((b, h, sub_len * dilation) + x.shape[4:])
        return x[:, :, :s]

    return back(num), back(den), back(mx)

def _dilated_mixture(q, k, v):
    parts = [_dilated_partial(q, k, v, w, r) for (w, r) in DIL_PATTERNS]
    m_all = parts[0][2]
    for _, _, m in parts[1:]:
        m_all = jnp.maximum(m_all, m)
    num = 0.0
    den = 0.0
    for n_i, d_i, m_i in parts:
        scale = jnp.exp(m_i - m_all)
        num = num + n_i * scale[..., None]
        den = den + d_i * scale
    return num / den[..., None]

def _hgrn2_chunkwise(q, k, v, log_f):
    b, h, s, dk = q.shape
    dv = v.shape[-1]
    n = s // HGRN_CHUNK

    def chunks(x):
        return x.astype(jnp.float32).reshape(b, h, n, HGRN_CHUNK, x.shape[-1]).transpose(2, 0, 1, 3, 4)

    qc, kc, vc = chunks(q), chunks(k), chunks(v)
    g_cum = jnp.cumsum(chunks(log_f), axis=3)
    causal = jnp.tril(jnp.ones((HGRN_CHUNK, HGRN_CHUNK), dtype=bool))[:, :, None]

    def step(state, xs):
        qb, kb, vb, gb = xs
        diff = gb[:, :, :, None, :] - gb[:, :, None, :, :]
        decay = jnp.where(causal, jnp.exp(jnp.where(causal, diff, 0.0)), 0.0)
        scores = jnp.einsum('bhtd,bhsd,bhtsd->bhts', qb, kb, decay)
        o = jnp.einsum('bhts,bhsv->bhtv', scores, vb) + jnp.einsum('bhtd,bhdv->bhtv', qb * jnp.exp(gb), state)
        g_last = gb[:, :, -1, :]
        new_state = jnp.exp(g_last)[..., None] * state + jnp.einsum('bhsd,bhsv->bhdv', kb * jnp.exp(g_last[:, :, None, :] - gb), vb)
        return new_state, o

    state0 = jnp.zeros((b, h, dk, dv), jnp.float32)
    _, o = lax.scan(step, state0, (qc, kc, vc, g_cum))
    return o.transpose(1, 2, 0, 3, 4).reshape(b, h, s, dv)

def _hybrid_mixer(h, w_in, w_out, q_norm_g, k_norm_g, hgrn_norm_g, lower_bound):
    dt = h.dtype
    proj = h @ w_in
    offsets = []
    acc = 0
    for wdt in IN_SPLITS[:-1]:
        acc += wdt
        offsets.append(acc)
    qa, ka, va, qd, kd, vd, qh, fh, ih, gh = jnp.split(proj, offsets, axis=-1)

    o_a = _stick_breaking(_split_heads(qa, SB_HEADS), _split_heads(ka, SB_HEADS), _split_heads(va, SB_HEADS))

    qd = _rope(_rmsnorm(_split_heads(qd, DIL_HEADS)) * q_norm_g) * (HEAD_DIM ** -0.5)
    kd = _rope(_rmsnorm(_split_heads(kd, DIL_HEADS)) * k_norm_g)
    o_d = _dilated_mixture(qd, kd, _split_heads(vd, DIL_HEADS))

    lb = lower_bound.reshape(HGRN_HEADS, 1, HGRN_DK).astype(jnp.float32)
    z = _split_heads(fh, HGRN_HEADS).astype(jnp.float32)
    log_f = jnp.logaddexp(jnp.log(jnp.maximum(lb, LB_FLOOR)), jnp.log1p(-lb) + jax.nn.log_sigmoid(z))
    k_h = -jnp.expm1(log_f)
    q_h = jax.nn.silu(_split_heads(qh, HGRN_HEADS))
    o_h = _hgrn2_chunkwise(q_h, k_h, _split_heads(ih, HGRN_HEADS), log_f)
    o_h = _rmsnorm(o_h) * hgrn_norm_g * jax.nn.silu(_split_heads(gh, HGRN_HEADS).astype(jnp.float32))

    y = jnp.concatenate([_merge_heads(o_a).astype(dt), _merge_heads(o_d).astype(dt), _merge_heads(o_h).astype(dt)], axis=-1)
    return y @ w_out

def second_inputs(seed: int = 0) -> dict:
    key = jax.random.key(seed)
    ks = jax.random.split(key, 16)

    def nrm(k, shape, scale):
        return jax.random.normal(k, shape, jnp.float32) * scale

    return {
        "x": nrm(ks[0], (BATCH, SEQ, D_MODEL), 1.0),
        "c": nrm(ks[1], (BATCH, D_MODEL), 1.0),
        "w_mod": nrm(ks[2], (DEPTH, D_MODEL, N_MOD * D_MODEL), D_MODEL ** -0.5),
        "b_mod": nrm(ks[3], (DEPTH, N_MOD * D_MODEL), 0.02),
        "ffn1_w_gate": nrm(ks[4], (DEPTH, D_MODEL, D_FF), D_MODEL ** -0.5),
        "ffn1_w_up": nrm(ks[5], (DEPTH, D_MODEL, D_FF), D_MODEL ** -0.5),
        "ffn1_w_down": nrm(ks[6], (DEPTH, D_FF, D_MODEL), D_FF ** -0.5),
        "w_in": nrm(ks[7], (DEPTH, D_MODEL, IN_WIDTH), D_MODEL ** -0.5),
        "w_out": nrm(ks[8], (DEPTH, MIX_WIDTH, D_MODEL), MIX_WIDTH ** -0.5),
        "q_norm_g": 1.0 + nrm(ks[9], (DEPTH, HEAD_DIM), 0.02),
        "k_norm_g": 1.0 + nrm(ks[10], (DEPTH, HEAD_DIM), 0.02),
        "hgrn_norm_g": 1.0 + nrm(ks[11], (DEPTH, HGRN_DV), 0.02),
        "hgrn_lb_logits": nrm(ks[12], (DEPTH, HGRN_KDIM), 0.5),
        "ffn2_w_gate": nrm(ks[13], (DEPTH, D_MODEL, D_FF), D_MODEL ** -0.5),
        "ffn2_w_up": nrm(ks[14], (DEPTH, D_MODEL, D_FF), D_MODEL ** -0.5),
        "ffn2_w_down": nrm(ks[15], (DEPTH, D_FF, D_MODEL), D_FF ** -0.5),
    }

def second_block(x, c, w_mod, b_mod, ffn1_w_gate, ffn1_w_up, ffn1_w_down, w_in, w_out, q_norm_g, k_norm_g, hgrn_norm_g, hgrn_lb_logits, ffn2_w_gate, ffn2_w_up, ffn2_w_down):
    lb_sm = jax.nn.softmax(hgrn_lb_logits.astype(jnp.float32), axis=0)
    lower_bounds = jnp.clip(jnp.cumsum(lb_sm, axis=0) - lb_sm[0:1], 0.0, 1.0 - EPS)
    for l in range(DEPTH):
        mod = jax.nn.silu(c) @ w_mod[l] + b_mod[l]
        sh1, sc1, g1, sh2, sc2, g2, sh3, sc3, g3 = jnp.split(mod[:, None, :], N_MOD, axis=-1)
        h = _rmsnorm(x) * (1.0 + sc1) + sh1
        x = x + HALF_STEP * g1 * _swiglu(h, ffn1_w_gate[l], ffn1_w_up[l], ffn1_w_down[l])
        h = _rmsnorm(x) * (1.0 + sc2) + sh2
        x = x + g2 * _hybrid_mixer(h, w_in[l], w_out[l], q_norm_g[l], k_norm_g[l], hgrn_norm_g[l], lower_bounds[l])
        h = _rmsnorm(x) * (1.0 + sc3) + sh3
        x = x + HALF_STEP * g3 * _swiglu(h, ffn2_w_gate[l], ffn2_w_up[l], ffn2_w_down[l])
    return x


def setup_inputs(seed=0):
    out = dict(first_inputs(seed))
    for name, value in second_inputs(seed + 1).items():
        if name != "x":
            out[name + "_2"] = value
    return out


def reference(
    x, mem, positions, ln_mix_g, ln_mix_b, w_in, b_gate, b_forget, a_rel_bias, b_q_norm,
    b_kv_norm, b_w_uq, b_w_ukv, w_branch, w_mix_out, ln_xa_g, ln_xa_b, xa_w_q, xa_w_kv, xa_w_o,
    ln_ffn_g, ln_ffn_b, ffn_w_gu, ffn_w_down, c_2, w_mod_2, b_mod_2, ffn1_w_gate_2, ffn1_w_up_2,
    ffn1_w_down_2, w_in_2, w_out_2, q_norm_g_2, k_norm_g_2, hgrn_norm_g_2, hgrn_lb_logits_2,
    ffn2_w_gate_2, ffn2_w_up_2, ffn2_w_down_2,
):
    x = first_block(
        x, mem, positions, ln_mix_g, ln_mix_b, w_in, b_gate, b_forget, a_rel_bias, b_q_norm,
        b_kv_norm, b_w_uq, b_w_ukv, w_branch, w_mix_out, ln_xa_g, ln_xa_b, xa_w_q, xa_w_kv,
        xa_w_o, ln_ffn_g, ln_ffn_b, ffn_w_gu, ffn_w_down,
    )
    return second_block(
        x, c_2, w_mod_2, b_mod_2, ffn1_w_gate_2, ffn1_w_up_2, ffn1_w_down_2, w_in_2, w_out_2,
        q_norm_g_2, k_norm_g_2, hgrn_norm_g_2, hgrn_lb_logits_2, ffn2_w_gate_2, ffn2_w_up_2,
        ffn2_w_down_2,
    )


_drawn_inputs = setup_inputs


def setup_inputs(seed=0):
    import zlib

    import numpy as np

    out = dict(_drawn_inputs(seed))
    spreads = {}
    factors = {'b_gate': 8.0,
     'b_q_norm': 8.0,
     'b_kv_norm': 8.0,
     'q_norm_g_2': 22.615,
     'k_norm_g_2': 8.0,
     'hgrn_norm_g_2': 6.507,
     'hgrn_lb_logits_2': 7.207}
    for name, (base, spread) in spreads.items():
        noise = np.random.default_rng([zlib.crc32(name.encode()), seed]).standard_normal(out[name].shape)
        drawn = base * np.exp(spread * noise) if base else spread * noise
        out[name] = __import__('jax').numpy.asarray(drawn.astype(out[name].dtype))
    for name, factor in factors.items():
        out[name] = (out[name] * factor).astype(out[name].dtype)
    return out
```

```python
from contextlib import ExitStack

import numpy as np

import concourse.bass as bass
from concourse import mybir

F32 = mybir.dt.float32
F32R = mybir.dt.float32r
I32 = mybir.dt.int32
ALU = mybir.AluOpType
ACT = mybir.ActivationFunctionType
AX = mybir.AxisListType

P = 128
T = 256
L = 2
D = 1024
DC = D // P
FF = 2816
FC = FF // P
W = 1024
RING = 4
NEG = -1.0e30
ALPHA = (2 * L) ** 0.25

B_COLS, B_UQ, B_UKV, A_QKV, C_QKV = 0, 6, 10, 14, 26
GATE, BRANCH, OUT1, X_Q, X_KV, X_O = 38, 62, 74, 82, 86, 94
GU1, DOWN1, PANELS1 = 98, 142, 164
GU2A, DOWN2A, IN2, OUT2, GU2B, DOWN2B, PANELS2 = 0, 44, 66, 94, 102, 146, 168
GROUPS1, GROUPS2 = PANELS1 // RING, PANELS2 // RING
Q_B, Q_UQ, Q_UKV, Q_A, Q_C, Q_G, Q_BR, Q_OUT, Q_XQ, Q_XKV, Q_XO, Q_GU, PAIRS1 = \
    0, 3, 7, 11, 17, 23, 35, 47, 51, 53, 57, 61, 83
R_GUA, R_IN, R_OUT, R_GUB, PAIRS2 = 0, 22, 36, 40, 62
MOD_CHUNKS = 72
MOD_STEP = 18
HEADS1 = 28
P_MIXG, P_MIXB, P_XAG, P_XAB, P_FFG, P_FFB, P_GATE, P_QN, P_KVN, P_BF, NPAR = \
    0, 8, 16, 24, 32, 40, 48, 72, 75, 77, 78
P2_BMOD, P2_QG, P2_KG, P2_HG, NPAR2 = 0, 72, 73, 74, 75
CONSTS = {}
N_CONST = 0
for _name, _n in (("ident", P), ("ones", P), ("rot32", 32), ("tri", 2 * T), ("chunk_mask", 2 * T),
                  ("causal_mask", 2 * T), ("invf", 1), ("is_f", 1), ("is_one", 1), ("head", 8)):
    CONSTS[_name] = (N_CONST, _n)
    N_CONST += _n
CONSTS2 = {}
N_CONST2 = 0
for _name, _n in (("block64", P), ("rot64", P), ("cos", T), ("sin", T), ("dilated", 2 * T),
                  ("spans", 9 * P), ("levels", 8 * P), ("before", 2 * T), ("suffix", P)):
    CONSTS2[_name] = (N_CONST2, _n)
    N_CONST2 += _n


def build(nc, io, stop_after=9):
    with ExitStack() as ctx:
        def sb(name, shape, dt=F32):
            return ctx.enter_context(nc.sbuf_tensor(name, shape, dt))

        def sem(name):
            return ctx.enter_context(nc.semaphore(name))

        raw = sb("raw", [P, RING, W])
        w_hi = sb("w_hi", [P, RING, W], F32R)
        w_lo = sb("w_lo", [P, RING, W], F32R)
        x = sb("x", [P, DC, T])
        x_hi = sb("x_hi", [P, DC, T], F32R)
        x_lo = sb("x_lo", [P, DC, T], F32R)
        R = sb("R", [P, 44 * T], F32R)
        F = sb("F", [P, 54 * T])
        side = sb("side", [P, 3 * W + MOD_STEP * P])
        mod_raw = side[:, 0:2 * W].rearrange("p (b w) -> p b w", b=2)
        mod_prod = side[:, 2 * W:3 * W].rearrange("p (k m) -> p k m", m=P)
        mod_acc = side[:, 3 * W:3 * W + MOD_STEP * P].rearrange("p (k m) -> p k m", m=P)
        modv = sb("modv", [P, L * MOD_CHUNKS])
        modl = sb("modl", [P, MOD_CHUNKS])
        par2 = sb("par2", [P, NPAR2])
        lbl = sb("lbl", [P, L, 4])
        lb = sb("lb", [P, L, 4])
        lb_t = sb("lb_t", [P, 3, 4])
        lbc = sb("lbc", [P, 2, 4])
        silu_c = sb("silu_c", [P, 8])
        const = sb("const", [P, N_CONST])
        par_all = sb("par_all", [P, L, NPAR])
        par = sb("par", [P, NPAR])
        par2_all = sb("par2_all", [P, L, NPAR2])
        rope_cos = sb("rope_cos", [P, T])
        rope_sin = sb("rope_sin", [P, T])
        mean = sb("mean", [P, T])
        rstd = sb("rstd", [P, 2, T])
        neg_max = sb("neg_max", [P, 2, 2])
        den = sb("den", [P, 2, 2])
        pos_i = mean[:].bitcast(I32)
        ps = ctx.enter_context(nc.psum_tensor("ps", [P, 8, 512], F32))

        def c_(name):
            at, n = CONSTS[name]
            return const[:, at:at + n]

        def c2(name):
            at, n = CONSTS2[name]
            return side[:, at:at + n]

        ident, ones = c_("ident"), c_("ones")

        def f(at, n, width=T):
            return F[:, at:at + n * width].rearrange("p (n w) -> p n w", w=width)

        def r(at, n):
            return R[:, at:at + n * T].rearrange("p (n w) -> p n w", w=T)

        bias = f(0, 2, 512)
        prob = f(1024, 2, 512)
        prob_t = f(2048, 2, 512)
        v_nat = F[:, 3072:4096]
        c_all = f(4096, 6)
        q_b, kv_b, k_b, rot_b = f(5632, 8), f(7680, 8), f(9728, 8), f(11776, 8)
        qk, v_t = f(4096, 8), f(6144, 4)
        fl, fr = f(7168, 8), F[0:16, 9216:9472]
        flog, fabs = F[:, 9472:9728], F[:, 9728:9984]
        fl0, f_nat = F[0:16, 9984:10240], F[:, 10240:10272].rearrange("p (t c) -> p t c", t=2)
        gates, gate_tmp, merged = f(4096, 24), F[:, 1024:1536], f(1536, 8)
        mem = f(10240, 8)
        sq = f(7168, 8)
        sq_b = f(5632, 5)
        ffn_s, ffn_h = f(1024, 2), f(1536, 2)
        br_hi, br_lo = r(0, 12), r(3072, 12)
        mg_hi, mg_lo = r(6144, 8), r(8192, 8)
        cn_hi, cn_lo = r(6144, 5), r(7424, 5)
        mem_hi, mem_lo = r(0, 8), r(2048, 8)
        xo_hi, xo_lo = r(6144, 4), r(7168, 4)
        hid_hi, hid_lo = r(0, FC), r(FC * T, FC)
        mix_hi, mix_lo = r(0, 8), r(2048, 8)
        sq2, normed = f(0, 8), f(11264, 8)
        h_all = f(4096, 28)
        rot_tmp, rs4 = f(11264, 4), f(12288, 4)
        logf, logf_b, o_h = f(4096, 4), f(5120, 4), f(6144, 4)
        v_h, logf_nat = F[:, 11264:12288], F[:, 12288:13312]

        def by_tile(ap):
            return ap.rearrange("p h (k t) -> p k h t", k=2)

        def tiles4(at):
            return F[:, at:at + 1024].rearrange("p (k h t) -> p k h t", k=2, h=4)
        q_h, k_h = by_tile(h_all[:, 12:16, :]), by_tile(h_all[:, 16:20, :])
        h_e, h_qe, h_ke = tiles4(0), tiles4(1024), tiles4(2048)
        scores, cross = tiles4(3072), F[:, 13312:13824]

        raw_in = [sem(f"raw_in{i}") for i in range(RING)]
        hi_done, lo_done = sem("hi_done"), sem("lo_done")
        panel_used = sem("panel_used")
        pair_out = sem("pair_out")
        dma_turn, consts_in, x_in, par_set = sem("dma_turn"), sem("consts_in"), sem("x_in"), sem("par_set")
        init_done = sem("init_done")
        x_split_hi, x_split = sem("x_split_hi"), sem("x_split")
        mod_in = [sem("mod_in0"), sem("mod_in1")]
        mod_mul, mod_sum, mod_taken, mod_out = sem("mod_mul"), sem("mod_sum"), sem("mod_taken"), sem("mod_out")
        pe_turn = sem("pe_turn")
        mod_end = sem("mod_end")
        mod_turn, silu_done = sem("mod_turn"), sem("silu_done")
        rope_dve, rope_act = sem("rope_dve"), sem("rope_act")
        b_dve, b_act, b_pe = sem("b_dve"), sem("b_act"), sem("b_pe")
        c_dve, c_act, c_pe = sem("c_dve"), sem("c_act"), sem("c_pe")
        vt_pe, vt_dve = sem("vt_pe"), sem("vt_dve")
        at_s, at_stt, at_max, at_exp = sem("at_s"), sem("at_stt"), sem("at_max"), sem("at_exp")
        at_rc, at_p, at_t, at_pt = sem("at_rc"), sem("at_p"), sem("at_t"), sem("at_pt")
        at_o, at_oh, at_ol = sem("at_o"), sem("at_oh"), sem("at_ol")
        bias_in = [sem("bias_in0"), sem("bias_in1")]
        mem_in, mem_h, mem_l = sem("mem_in"), sem("mem_h"), sem("mem_l")
        br_dve, mg_h, mg_l = sem("br_dve"), sem("mg_h"), sem("mg_l")
        n_pe, n_dve, n_act = sem("n_pe"), sem("n_dve"), sem("n_act")
        ffn_act, ffn_dve, down_out = sem("ffn_act"), sem("ffn_dve"), sem("down_out")
        out_in = sem("out_in")
        lbl_in, lb_dve, lb_act, consts2_in = sem("lbl_in"), sem("lb_dve"), sem("lb_act"), sem("consts2_in")
        mod_set = sem("mod_set")
        rn_pe, rn_dve, rn_act = sem("rn_pe"), sem("rn_dve"), sem("rn_act")
        res2 = sem("res2")
        sb_z, sb_a, sb_d, sb_t, sb_e = sem("sb_z"), sem("sb_a"), sem("sb_d"), sem("sb_t"), sem("sb_e")
        sb_l, sb_w, sb_lw = sem("sb_l"), sem("sb_w"), sem("sb_lw")
        sb_o, sb_oh, sb_ol = sem("sb_o"), sem("sb_oh"), sem("sb_ol")
        dl_pe, dl_act, dl_dve = sem("dl_pe"), sem("dl_act"), sem("dl_dve")
        hg_act, hg_dve, hg_pe = sem("hg_act"), sem("hg_dve"), sem("hg_pe")
        hg_d, hg_exp, hg_qe, hg_ke = sem("hg_d"), sem("hg_exp"), sem("hg_qe"), sem("hg_ke")
        hg_hi, hg_a, lb_c, rn_x = sem("hg_hi"), sem("hg_a"), sem("lb_c"), sem("rn_x")
        hg_s, hg_m = sem("hg_s"), sem("hg_m")

        ND, NA, NP = 4, 12, 2
        BD, BA, BP = 21, 5, 4
        CD, CA, CP = 8, 3, 2
        HG, HA = 21, 9

        block = ctx.enter_context(nc.Block())

        @block.sync
        def _(sp):
            sp.dma_start(x[:], io["xT"]).then_inc(x_in, 16)
            for s in range(RING):
                sp.dma_start(raw[:, s, :], io["w"][s]).then_inc(raw_in[s], 16)
            sp.dma_start(const[:], io["const"]).then_inc(consts_in, 16)
            sp.dma_start(par_all[:], io["par1"]).then_inc(consts_in, 16)
            sp.dma_start(par2_all[:], io["par2"]).then_inc(consts_in, 16)
            sp.dma_start(lbl[:], io["lbl"]).then_inc(lbl_in, 16)
            sp.dma_start(pos_i[64:96, :], io["pos"].partition_broadcast(32)).then_inc(consts_in, 16)
            groups = L * (GROUPS1 + (GROUPS2 if stop_after > 1 else 0))
            with sp.Fori(1, groups) as g:
                for s in range(RING):
                    sp.wait_ge(lo_done, 4 * g + (s - 3))
                    sp.sem_inc(dma_turn, 1)
                    sp.dma_start(raw[:, s, :], io["w"][4 * g + s]).then_inc(raw_in[s], 16)

        @block.gpsimd
        def _(pool):
            pool.wait_ge(silu_done, 1)
            for b in range(2):
                pool.dma_start(mod_raw[:, b, :], io["wmod"][b]).then_inc(mod_in[b], 16)
            c_row = silu_c[:].rearrange("p (k o) -> p k o", o=1).broadcast_to([P, 8, P])
            with pool.Fori(0, L * MOD_CHUNKS // MOD_STEP) as step:
                pool.wait_ge(mod_taken, step + 1)
                pool.sem_inc(mod_turn, 1)
                for j in range(MOD_STEP // 2):
                    for b in range(2):
                        n = step * MOD_STEP + (2 * j + b)
                        pool.wait_ge(mod_in[b], (step * (MOD_STEP // 2) + (j + 1)) * 16)
                        w = mod_raw[:, b, :].rearrange("p (k m) -> p k m", k=8)
                        nc.gpsimd.tensor_tensor(mod_prod[:], w, c_row, ALU.mult).then_inc(mod_mul, 1)
                        pool.wait_ge(mod_mul, 4 * n + 1)
                        nxt = n + 2
                        pool.dma_start(mod_raw[:, b, :], io["wmod"][nxt]).then_inc(mod_in[b], 16)
                        for half in (4, 2, 1):
                            dst = mod_prod[:, 0:half, :] if half > 1 else mod_acc[:, 2 * j + b:2 * j + b + 1, :]
                            ins = nc.gpsimd.tensor_tensor(dst, mod_prod[:, 0:half, :],
                                                          mod_prod[:, half:2 * half, :], ALU.add)
                            ins.then_inc(mod_mul, 1)
                            pool.wait_ge(mod_mul, 4 * n + {4: 2, 2: 3, 1: 4}[half])
                pool.sem_inc(mod_sum, 1)
            for b in range(2):
                pool.wait_ge(mod_in[b], 16 * (L * MOD_CHUNKS // 2 + 1))
            pool.sem_inc(mod_end, 1)
            if stop_after < 2:
                return
            with pool.Fori(0, L) as l:
                for level in range(8):
                    pool.wait_ge(hg_exp, 8 * l + level + 1)
                    pool.wait_ge(hg_s, 9 * l + level + 1)
                    pool.sem_inc(mod_turn, 1)
                    if level < 7:
                        nc.gpsimd.tensor_tensor(h_ke, k_h, h_e, ALU.mult).then_inc(hg_ke, 1)
                    else:
                        nc.gpsimd.tensor_tensor(h_ke[:, 0], k_h[:, 0], h_e[:, 0], ALU.mult).then_inc(hg_ke, 1)

        def feed_hi(act, group, s):
            act.wait_ge(raw_in[s], 16 * group + 16)
            act.wait_ge(panel_used, 4 * group + (s + 1))
            nc.scalar.activation(w_hi[:, s, :], raw[:, s, :], ACT.Copy).then_inc(hi_done, 1)

        def feed_lo(dve, group, s):
            dve.wait_ge(hi_done, 4 * group + (s + 1))
            nc.vector.tensor_tensor(w_lo[:, s, :], raw[:, s, :], w_hi[:, s, :].bitcast(F32),
                                    ALU.subtract).then_inc(lo_done, 1)

        def panels(eng, group0, p0, n, feed, drain, limit):
            def turn(at, i, parts):
                for s in parts:
                    for k in (2, 3):
                        if at + s + k < limit:
                            feed(eng, group0 + i + (at + s + k) // 4, (at + s + k) % 4)
                    drain(group0 + i + (at + s + 1) // 4, (at + s + 1) % 4, 2 * i + (at - p0 + s) // 2, s // 2)
            if n >= 8:
                with eng.Fori(0, n // 4) as i:
                    turn(p0, i, (0, 2))
                if n % 4:
                    turn(p0 + n - n % 4, 0, (0,))
            else:
                for s in range(0, n, 4):
                    turn(p0 + s, 0, (0, 2) if n - s >= 4 else (0,))

        def only_feed(eng, group0, p0, p1, feed):
            n = (p1 - p0) // 4
            with eng.Fori(0, n) as i:
                for s in range(4):
                    feed(eng, group0 + i + (p0 + s) // 4, (p0 + s) % 4)
            for p in range(p0 + 4 * n, p1):
                feed(eng, group0 + p // 4, p % 4)

        def multiply(pe, out, at, m, k, s, rhs_hi, rhs_lo, start, stop, skip=False):
            hi, lo = w_hi[:, s, at:at + m], w_lo[:, s, at:at + m]
            nc.tensor.matmul(out, hi, rhs_hi, start=start, stop=False, skip_group_check=skip)
            nc.tensor.matmul(out, hi, rhs_lo, start=False, stop=False, skip_group_check=skip)
            return nc.tensor.matmul(out, lo, rhs_hi, start=False, stop=stop, skip_group_check=skip)

        def project(pe, group0, p0, n, pair0, rhs_hi, rhs_lo, chunks, m=P, per_panel=1):
            pe.wait_ge(pair_out, pair0 + 2)
            pe.sem_inc(pe_turn, 1)

            def panel(at, i, s_at):
                s = at % 4
                pe.wait_ge(lo_done, 4 * (group0 + i + at // 4) + (s + 1))
                for o in range(per_panel):
                    use = (s_at * per_panel + o) // 2
                    half = (s_at * per_panel + o) % 2
                    if half == 0:
                        uses = 2 * per_panel * i + use
                        pe.wait_ge(pair_out, pair0 + uses + 1)
                    out = ps[0:m, use % 2, half * T:(half + 1) * T]
                    for k in range(chunks):
                        ins = multiply(pe, out, (k * per_panel + o) * m, m, k, s, rhs_hi[:, k, :], rhs_lo[:, k, :],
                                       k == 0, k == chunks - 1)
                ins.then_inc(panel_used, 1)
            if n >= 8:
                with pe.Fori(0, n // 4) as i:
                    for s in range(4):
                        panel(p0 + s, i, s)
                for s in range(n % 4):
                    panel(p0 + n - n % 4 + s, 0, s + 4 * (n // 4))
            else:
                for s in range(n):
                    panel(p0 + s, 0, s)

        def down(pe, group0, p0, run):
            pe.wait_ge(ffn_dve, (run + 1) * 2 * FC)
            pe.wait_ge(down_out, 4 * run + 1)

            def panel(at, i, k, start, stop):
                s = at % 4
                pe.wait_ge(lo_done, 4 * (group0 + i + at // 4) + (s + 1))
                for m in range(DC):
                    ins = multiply(pe, ps[:, 4 + m // 2, (m % 2) * T:(m % 2 + 1) * T], m * P, P, k, s,
                                   hid_hi[:, k, :], hid_lo[:, k, :], start and m % 2 == 0, stop, True)
                ins.then_inc(panel_used, 1)
                return ins
            panel(p0, 0, 0, True, False)
            with pe.Fori(0, (FC - 2) // 4) as i:
                for s in range(4):
                    panel(p0 + 1 + s, i, 4 * i + (s + 1), False, False)
            panel(p0 + FC - 1, 0, FC - 1, False, True)

        def pe_attention(pe, head0, n, q, k, extra, v, rows, ready):
            ready(pe)
            for t in range(n + 2):
                if t < n:
                    pe.wait_ge(at_stt, head0 + t + 1)
                    for tile in range(2):
                        out = ps[:, 2 + t % 2, tile * T:(tile + 1) * T]
                        ins = nc.tensor.matmul(out, q(t, tile), k(t), start=True, stop=extra is None)
                        if extra is not None:
                            ins = nc.tensor.matmul(out, extra[0](t, tile), extra[1], start=False, stop=True)
                    ins.then_inc(at_s, 1)
                if 1 <= t <= n:
                    h = t - 1
                    pe.wait_ge(at_p, head0 + h + 1)
                    pe.wait_ge(at_pt, head0 + h + 1)
                    for kt in range(2):
                        for tile in range(2):
                            ins = nc.tensor.transpose(
                                ps[:, 4 + h % 2, kt * T + tile * P:kt * T + (tile + 1) * P],
                                prob[:, h % 2, tile * T + kt * P:tile * T + (kt + 1) * P], ident)
                    ins.then_inc(at_t, 1)
                if t >= 2:
                    h = t - 2
                    pe.wait_ge(at_pt, head0 + h + 3)
                    pe.wait_ge(at_ol, head0 + h + 1)
                    for kt in range(2):
                        ins = nc.tensor.matmul(ps[rows(h), 6 + h % 2, 0:T], v(h, kt),
                                               prob_t[:, h % 2, kt * T:(kt + 1) * T], start=kt == 0, stop=kt == 1)
                    ins.then_inc(at_o, 1)

        def act_attention(act, head0, n, rows, out_hi, reverse=False, bias_dma=None):
            for t in range(n + 2):
                if t < n:
                    act.wait_ge(at_max, head0 + t + 1)
                    for tile in range(2):
                        s = prob[:, t % 2, tile * T:(tile + 1) * T]
                        ins = nc.scalar.activation(s, s, ACT.Exp, bias=neg_max[:, t % 2, tile:tile + 1],
                                                   accum_out=den[:, t % 2, tile:tile + 1])
                        ins.then_inc(at_exp, 1)
                    if bias_dma is not None and t + 2 < n:
                        bias_dma(act, t + 2)
                if 1 <= t <= n:
                    h = t - 1
                    act.wait_ge(at_t, head0 + h + 3)
                    act.wait_ge(at_o, head0 + h + 1)
                    src = ps[:, 4 + h % 2, :].rearrange("p (k q) -> p k q", k=2)
                    if reverse:
                        src = src[:, :, ::-1]
                    nc.scalar.activation(prob_t[:, h % 2, :].rearrange("p (k q) -> p k q", k=2), src,
                                         ACT.Copy).then_inc(at_pt, 1)
                if t >= 2:
                    h = t - 2
                    act.wait_ge(at_o, head0 + h + 3)
                    nc.scalar.activation(out_hi(h)[rows(h), :], ps[rows(h), 6 + h % 2, 0:T],
                                         ACT.Copy).then_inc(at_oh, 1)

        def dve_attention(dve, head0, n, rows, out_hi, out_lo, scale, bias_of, bias_wait=None):
            for t in range(n + 2):
                if t < n:
                    if bias_wait is not None:
                        bias_wait(dve, t)
                    dve.wait_ge(at_s, head0 + t + 1)
                    dve.wait_ge(at_t, head0 + t + 1)
                    if bias_of is None:
                        nc.vector.tensor_scalar(prob[:, t % 2, :], ps[:, 2 + t % 2, :], scale, None,
                                                ALU.mult).then_inc(at_stt, 1)
                    else:
                        nc.vector.scalar_tensor_tensor(out=prob[:, t % 2, :], in0=ps[:, 2 + t % 2, :], scalar=scale,
                                                       in1=bias_of(t), op0=ALU.mult, op1=ALU.add).then_inc(at_stt, 1)
                    dve.wait_ge(at_stt, head0 + t + 3)
                    nc.vector.tensor_reduce(neg_max[:, t % 2, :], prob[:, t % 2, :].rearrange("p (t k) -> p t k", t=2),
                                            AX.X, ALU.max, negate=True).then_inc(at_max, 1)
                if 1 <= t <= n:
                    h = t - 1
                    dve.wait_ge(at_exp, 2 * (head0 + h) + 2)
                    nc.vector.reciprocal(den[:, h % 2, :], den[:, h % 2, :]).then_inc(at_rc, 1)
                    dve.wait_ge(at_rc, head0 + h + 1)
                    view = prob[:, h % 2, :].rearrange("p (t k) -> p t k", t=2)
                    nc.vector.tensor_tensor(view, view, den[:, h % 2, :].rearrange("p (t o) -> p t o", o=1)
                                            .broadcast_to([P, 2, T]), ALU.mult).then_inc(at_p, 1)
                if t >= 2:
                    h = t - 2
                    dve.wait_ge(at_oh, head0 + h + 1)
                    nc.vector.tensor_tensor(out_lo(h)[rows(h), :], ps[rows(h), 6 + h % 2, 0:T],
                                            out_hi(h)[rows(h), :].bitcast(F32), ALU.subtract).then_inc(at_ol, 1)

        def pe_turn_v(pe, run, src, chunks=range(4)):
            for tile in range(2):
                for at, c in enumerate(chunks):
                    ins = nc.tensor.transpose(ps[:, 6 + tile, at * P:(at + 1) * P],
                                              src[:, c, tile * P:(tile + 1) * P], ident)
                ins.then_inc(vt_pe, 1)

        def dve_turn_v(dve, run, v_nat=v_nat):
            for tile in range(2):
                dve.wait_ge(vt_pe, 2 * run + (tile + 1))
                nc.vector.tensor_copy(v_nat[:, tile * 512:(tile + 1) * 512], ps[:, 6 + tile, :]).then_inc(vt_dve, 1)

        def even_odd(h):
            return slice(64 * (h % 2), 64 * (h % 2) + 64)

        def whole(h):
            return slice(0, P)

        def pe_norm(pe, run, ready, between=None):
            ready()
            for c in range(DC):
                ins = nc.tensor.matmul(ps[:, 2, 0:T], ones, x[:, c, :], start=c == 0, stop=c == DC - 1)
            ins.then_inc(n_pe, 1)
            if between is not None:
                between()
            pe.wait_ge(n_act, run * NA + 1)
            for c in range(DC):
                ins = nc.tensor.matmul(ps[:, 2, T:2 * T], ones, sq[:, c, :], start=c == 0, stop=c == DC - 1)
            ins.then_inc(n_pe, 1)

        def over(v, n):
            return v.rearrange("p (o t) -> p o t", o=1).broadcast_to([P, n, T])

        def dve_norm(dve, run):
            base = run * ND
            dve.wait_ge(n_pe, run * NP + 1)
            nc.vector.tensor_scalar(mean[:], ps[:, 2, 0:T], 1.0 / D, None, ALU.mult).then_inc(n_dve, 1)
            dve.wait_ge(n_dve, base + 1)
            nc.vector.tensor_tensor(x[:], x[:], over(mean[:], DC), ALU.subtract).then_inc(n_dve, 1)
            dve.wait_ge(n_pe, run * NP + 2)
            nc.vector.tensor_scalar(rstd[:, 0, :], ps[:, 2, T:2 * T], 1.0 / D, 1e-5, ALU.mult, ALU.add)\
                .then_inc(n_dve, 1)
            dve.wait_ge(n_act, run * NA + 3)
            nc.vector.tensor_tensor(x[:], x[:], over(rstd[:, 0, :], DC), ALU.mult).then_inc(n_dve, 1)
            dve.wait_ge(x_split_hi, run + 2)
            nc.vector.tensor_tensor(x_lo[:], x[:], x_hi[:].bitcast(F32), ALU.subtract).then_inc(x_split, 1)

        def act_norm(act, run, gain):
            base = run * NA
            act.wait_ge(n_dve, run * ND + 2)
            nc.scalar.activation(sq[:], x[:], ACT.Square).then_inc(n_act, 1)
            act.wait_ge(n_dve, run * ND + 3)
            nc.scalar.activation(rstd[:, 0, :], rstd[:, 0, :], ACT.Ln).then_inc(n_act, 1)
            act.wait_ge(n_act, base + 2)
            nc.scalar.activation(rstd[:, 0, :], rstd[:, 0, :], ACT.Exp, scale=-0.5).then_inc(n_act, 1)
            act.wait_ge(n_dve, run * ND + 4)
            for c in range(DC):
                nc.scalar.activation(x[:, c, :], x[:, c, :], ACT.Identity, scale=par[:, gain + c:gain + c + 1],
                                     bias=par[:, gain + DC + c:gain + DC + c + 1]).then_inc(n_act, 1)
            act.wait_ge(n_act, base + 3 + DC)
            nc.scalar.activation(x_hi[:], x[:], ACT.Copy).then_inc(x_split_hi, 1)
            act.sem_inc(n_act, 1)

        def act_ffn(act, group0, p0, run, limit):
            def drain(group, s, q, b):
                act.wait_ge(panel_used, 4 * group + (s + 5))
                nc.scalar.activation(ffn_s[:, b, :], ps[:, b, 0:T], ACT.Silu).then_inc(ffn_act, 1)
                act.wait_ge(ffn_dve, 2 * FC * run + 2 * q + 1)
                nc.scalar.activation(hid_hi[:, q, :], ffn_h[:, b, :], ACT.Copy).then_inc(ffn_act, 1)
            panels(act, group0, p0, 2 * FC, feed_hi, drain, limit)

        def dve_ffn(dve, group0, p0, run, pair0, limit):
            def drain(group, s, q, b):
                dve.wait_ge(ffn_act, 2 * FC * run + 2 * q + 1)
                nc.vector.tensor_tensor(ffn_h[:, b, :], ps[:, b, T:2 * T], ffn_s[:, b, :], ALU.mult)\
                    .then_inc(ffn_dve, 1)
                dve.wait_ge(ffn_act, 2 * FC * run + 2 * q + 2)
                nc.vector.tensor_tensor(hid_lo[:, q, :], ffn_h[:, b, :], hid_hi[:, q, :].bitcast(F32), ALU.subtract)\
                    .then_inc(ffn_dve, 1)
                dve.sem_inc(pair_out, 1)
            panels(dve, group0, p0, 2 * FC, feed_lo, drain, limit)

        def chunk_c(c):
            return slice(64 * (c % 2), 64 * (c % 2) + 64)

        def pe_mod(pe, visit):
            pe.wait_ge(mod_sum, visit + 1)
            for j in range(MOD_STEP):
                ins = nc.tensor.matmul(ps[:, 3, j:j + 1], mod_acc[:, j, :], ones[:, 0:1], start=True, stop=True)
            ins.then_inc(mod_taken, 1)

        def dve_mod(dve, visit):
            dve.wait_ge(mod_taken, visit + 2)
            nc.vector.tensor_copy(modv[:, bass.ds(visit * MOD_STEP, MOD_STEP)], ps[:, 3, 0:MOD_STEP])\
                .then_inc(mod_out, 1)

        def f_tile(t, tile):
            return fl[0:16, t, tile * P:(tile + 1) * P]

        @block.tensor
        def _(pe):
            pe.sem_inc(panel_used, RING)
            pe.sem_inc(pair_out, 2)
            pe.sem_inc(mod_taken, 1)
            pe.sem_inc(down_out, 1)
            for s_ in (at_stt, at_pt, at_t, at_o, at_ol):
                pe.sem_inc(s_, 2)
            pe.wait_ge(consts_in, 64)
            with pe.Fori(0, L) as l:
                g0, q0, h0 = l * GROUPS1, l * PAIRS1, l * HEADS1
                pe.wait_ge(x_split, 3 * l + 1)
                project(pe, g0, B_COLS, 6, q0 + Q_B, x_hi, x_lo, DC)
                pe.wait_ge(pair_out, q0 + Q_UQ + 2)
                pe.sem_inc(pe_turn, 1)
                nc.tensor.matmul(ps[64:96, 3, 0:T], c_("rot32")[64:96, :], c_all[64:96, 5, :],
                                 start=True, stop=True).then_inc(b_pe, 1)
                pe.wait_ge(b_act, l * BA + 1)
                for c in range(3):
                    nc.tensor.matmul(ps[:, 2, 0:T], ones, sq_b[:, c, :], start=c == 0, stop=c == 2)
                for c in range(2):
                    ins = nc.tensor.matmul(ps[:, 2, T:2 * T], ones, sq_b[:, 3 + c, :], start=c == 0, stop=c == 1)
                ins.then_inc(b_pe, 1)
                pe.wait_ge(b_dve, l * BD + 11)
                project(pe, g0, B_UQ, 4, q0 + Q_UQ, cn_hi, cn_lo, 3, m=96, per_panel=2)
                project(pe, g0, B_UKV, 4, q0 + Q_UKV, cn_hi[:, 3:5, :], cn_lo[:, 3:5, :], 2, per_panel=2)
                pe.wait_ge(pair_out, q0 + Q_A + 2)
                pe.wait_ge(b_dve, l * BD + 11)
                pe.sem_inc(pe_turn, 1)
                for h in range(0, 8, 2):
                    ins = nc.tensor.matmul(ps[64:96, 2 + h // 2, :], c_("rot32")[64:96, :],
                                           q_b[64:96, h:h + 2, :], start=True, stop=True)
                ins.then_inc(b_pe, 1)
                for tile in range(2):
                    for h in range(8):
                        ins = nc.tensor.transpose(ps[:, 6 + tile, 64 * h:64 * h + 64],
                                                  kv_b[64:128, h, tile * P:(tile + 1) * P], ident[64:128, 64:128])
                ins.then_inc(b_pe, 1)

                def b_ready(pe):
                    pe.wait_ge(b_dve, l * BD + BD)
                pe_attention(pe, h0, 8, lambda h, t: q_b[0:96, h, t * P:(t + 1) * P], lambda h: k_b[0:96, h, :], None,
                             lambda h, kt: v_nat[:, kt * 512 + 64 * h:kt * 512 + 64 * h + 64], even_odd, b_ready)
                project(pe, g0, A_QKV, 12, q0 + Q_A, x_hi, x_lo, DC)
                pe.wait_ge(pair_out, q0 + Q_C + 2)
                pe.wait_ge(at_ol, h0 + 8 + 2)
                pe_turn_v(pe, 3 * l, v_t)

                def a_ready(pe):
                    pe.wait_ge(vt_dve, 6 * l + 2)
                pe_attention(pe, h0 + 8, 8, lambda h, t: qk[chunk_c(h), h // 2, t * P:(t + 1) * P],
                             lambda h: qk[chunk_c(h), 4 + h // 2, :], None,
                             lambda h, kt: v_nat[:, kt * 512 + 64 * h:kt * 512 + 64 * h + 64], even_odd, a_ready)
                pe_mod(pe, 4 * l)
                project(pe, g0, C_QKV, 12, q0 + Q_C, x_hi, x_lo, DC)
                pe.wait_ge(c_act, l * CA + CA)
                pe.wait_ge(c_dve, l * CD + 3)
                pe.sem_inc(pe_turn, 1)
                for tile in range(2):
                    ins = nc.tensor.transpose(ps[:, 2, 8 * tile:8 * tile + 8], flog[0:8, tile * P:(tile + 1) * P],
                                              ident[0:8, 0:8])
                ins.then_inc(c_pe, 1)
                pe.wait_ge(c_dve, l * CD + 5)
                for tile in range(2):
                    ins = nc.tensor.matmul(ps[0:16, 2, T:2 * T], f_nat[:, tile, :],
                                           c_("tri")[:, tile * T:(tile + 1) * T], start=tile == 0, stop=tile == 1)
                ins.then_inc(c_pe, 1)
                pe.wait_ge(pair_out, q0 + Q_G + 2)
                pe.wait_ge(at_ol, h0 + 16 + 2)
                pe_turn_v(pe, 3 * l + 1, v_t)

                def c_ready(pe):
                    pe.wait_ge(vt_dve, 6 * l + 4)
                    pe.wait_ge(mod_out, 4 * l + 1)
                    pe.wait_ge(c_dve, l * CD + CD)
                pe_attention(pe, h0 + 16, 8, lambda h, t: qk[chunk_c(h), h // 2, t * P:(t + 1) * P],
                             lambda h: qk[chunk_c(h), 4 + h // 2, :], (f_tile, fr),
                             lambda h, kt: v_nat[:, kt * 512 + 64 * h:kt * 512 + 64 * h + 64], even_odd, c_ready)
                project(pe, g0, GATE, 24, q0 + Q_G, x_hi, x_lo, DC)
                pe_mod(pe, 4 * l + 1)
                pe.wait_ge(at_ol, h0 + 24 + 2)
                for n in range(3):
                    project(pe, g0, BRANCH + 4 * n, 4, q0 + Q_BR + 4 * n, br_hi[:, 4 * n:4 * n + 4, :],
                            br_lo[:, 4 * n:4 * n + 4, :], 4, per_panel=2)
                pe.wait_ge(mg_l, l + 1)
                project(pe, g0, OUT1, 8, q0 + Q_OUT, mg_hi, mg_lo, DC)
                pe_norm(pe, 3 * l, lambda: pe.wait_ge(pair_out, q0 + Q_XQ + 2))
                pe.wait_ge(x_split, 3 * l + 2)
                project(pe, g0, X_Q, 4, q0 + Q_XQ, x_hi, x_lo, DC)
                pe.wait_ge(mem_l, l + 1)
                project(pe, g0, X_KV, 8, q0 + Q_XKV, mem_hi, mem_lo, DC)
                pe.wait_ge(pair_out, q0 + Q_XO + 2)
                pe_turn_v(pe, 3 * l + 2, v_t)

                def x_ready(pe):
                    pe.wait_ge(vt_dve, 6 * l + 6)
                    pe.wait_ge(mod_out, 4 * l + 2)
                pe_attention(pe, h0 + 24, 4, lambda h, t: qk[:, h, t * P:(t + 1) * P], lambda h: qk[:, 4 + h, :], None,
                             lambda h, kt: v_nat[:, kt * 512 + P * h:kt * 512 + P * h + P], whole, x_ready)
                pe.wait_ge(at_ol, h0 + 28 + 2)
                project(pe, g0, X_O, 4, q0 + Q_XO, xo_hi, xo_lo, 4, per_panel=2)
                pe_norm(pe, 3 * l + 1, lambda: pe.wait_ge(pair_out, q0 + Q_GU + 2), lambda: pe_mod(pe, 4 * l + 2))
                pe.wait_ge(x_split, 3 * l + 3)
                project(pe, g0, GU1, 2 * FC, q0 + Q_GU, x_hi, x_lo, DC)
                down(pe, g0, DOWN1, l)
                pe_norm(pe, 3 * l + 2, lambda: pe.wait_ge(down_out, 4 * l + 5), lambda: pe_mod(pe, 4 * l + 3))

            if stop_after < 2:
                return
            pe.wait_ge(consts2_in, 16)
            pe.sem_inc(hg_s, 1)
            with pe.Fori(0, L) as l:
                g0, q0, h0 = L * GROUPS1 + l * GROUPS2, L * PAIRS1 + l * PAIRS2, L * HEADS1 + 4 * l

                def norm2(k):
                    pe.wait_ge(rn_act, 3 * (3 * l + k) + 1)
                    for c in range(DC):
                        ins = nc.tensor.matmul(ps[:, 2, 0:T], ones, sq2[:, c, :], start=c == 0, stop=c == DC - 1)
                    ins.then_inc(rn_pe, 1)
                    pe.wait_ge(x_split, 3 * L + 1 + 3 * l + k + 1)
                norm2(0)
                project(pe, g0, GU2A, 2 * FC, q0 + R_GUA, x_hi, x_lo, DC)
                down(pe, g0, DOWN2A, L + 2 * l)
                norm2(1)
                project(pe, g0, IN2, 28, q0 + R_IN, x_hi, x_lo, DC)
                pe.wait_ge(pair_out, q0 + R_OUT + 2)
                pe_turn_v(pe, 0, h_all, (4, 5, 10, 11))
                for t in range(6):
                    if t < 4:
                        for kt in range(2):
                            ins = nc.tensor.matmul(ps[:, 2 + t % 2, kt * T:(kt + 1) * T],
                                                   h_all[chunk_c(t), 2 + t // 2, kt * P:(kt + 1) * P],
                                                   h_all[chunk_c(t), t // 2, :], start=True, stop=True)
                        ins.then_inc(sb_z, 1)
                    if 1 <= t <= 4:
                        h = t - 1
                        bank, b = ps[:, 4 + h % 2, :], h % 2
                        pe.wait_ge(sb_l, 4 * l + h + 1)
                        nc.tensor.matmul(bank[:, 0:T], c2("suffix"), prob_t[:, b, 0:T], start=True, stop=False)
                        nc.tensor.matmul(bank[:, 0:T], ones, prob_t[:, b, T:2 * T], start=False, stop=True)
                        nc.tensor.matmul(bank[:, T:2 * T], c2("suffix"), prob_t[:, b, T:2 * T],
                                         start=True, stop=True).then_inc(sb_t, 1)
                    if t >= 2:
                        h = t - 2
                        pe.wait_ge(sb_w, 4 * l + h + 1)
                        if h == 0:
                            pe.wait_ge(vt_dve, 2 * (3 * L + 2 * l) + 2)
                        if h >= 2:
                            pe.wait_ge(sb_ol, 4 * l + h - 1)
                        for kt in range(2):
                            ins = nc.tensor.matmul(ps[even_odd(h), 6 + h % 2, 0:T],
                                                   v_nat[:, kt * 512 + 64 * h:kt * 512 + 64 * h + 64],
                                                   prob[:, h % 2, kt * T:(kt + 1) * T], start=kt == 0, stop=kt == 1)
                        ins.then_inc(sb_o, 1)
                pe.wait_ge(dl_act, 3 * l + 1)
                for n in range(2):
                    ins = nc.tensor.matmul(ps[:, 2 + n, :], c2("block64"), rot_tmp[:, 2 * n:2 * n + 2, :],
                                           start=True, stop=True)
                ins.then_inc(dl_pe, 1)
                pe.wait_ge(dl_dve, 9 * l + 4)
                for n in range(2):
                    ins = nc.tensor.matmul(ps[:, 2 + n, :], c2("rot64"), h_all[:, 6 + 2 * n:8 + 2 * n, :],
                                           start=True, stop=True)
                ins.then_inc(dl_pe, 1)

                def d_ready(pe):
                    pe.wait_ge(dl_dve, 9 * l + 9)
                    pe.wait_ge(sb_ol, 4 * l + 4)
                pe_attention(pe, h0, 4, lambda h, t: h_all[chunk_c(h), 6 + h // 2, t * P:(t + 1) * P],
                             lambda h: h_all[chunk_c(h), 8 + h // 2, :], None,
                             lambda h, kt: v_nat[:, kt * 512 + 256 + 64 * h:kt * 512 + 256 + 64 * h + 64],
                             even_odd, d_ready)
                pe.wait_ge(hg_dve, HG * l + 11)
                pe.wait_ge(at_ol, h0 + 4 + 2)
                for tile in range(2):
                    for h in range(4):
                        ins = nc.tensor.transpose(ps[:, 2 + tile, h * P:(h + 1) * P],
                                                  logf[:, h, tile * P:(tile + 1) * P], ident)
                ins.then_inc(hg_pe, 1)
                pe_turn_v(pe, 0, h_all, (20, 21, 22, 23))
                pe.wait_ge(hg_dve, HG * l + 13)
                pe.wait_ge(vt_dve, 2 * (3 * L + 2 * l) + 4)
                for level in range(9):
                    if level < 8:
                        if level:
                            pe.wait_ge(hg_exp, 8 * l + level)
                        for tile in range(2):
                            span = level if level < 7 else 7 + tile
                            for h in range(4):
                                ins = nc.tensor.matmul(ps[:, 2 + tile, h * P:(h + 1) * P],
                                                       logf_nat[:, tile * 512 + h * P:tile * 512 + (h + 1) * P],
                                                       c2("spans")[:, span * P:(span + 1) * P], start=True, stop=True)
                        ins.then_inc(hg_d, 1)
                        pe.wait_ge(hg_qe, 8 * l + level + 1)
                        pe.wait_ge(hg_ke, 8 * l + level + 1)
                    if level:
                        pe.wait_ge(hg_m, 9 * l + level)
                    if level == 7:
                        for h in range(4):
                            ins = nc.tensor.matmul(ps[:, 4, h * P:(h + 1) * P], h_ke[:, 0, h, :], h_qe[:, 1, h, :],
                                                   start=True, stop=True)
                    else:
                        a, b = (h_ke, h_qe) if level < 8 else (k_h, q_h)
                        for tile in range(2):
                            for h in range(4):
                                ins = nc.tensor.matmul(ps[:, 4 + tile, h * P:(h + 1) * P], a[:, tile, h, :],
                                                       b[:, tile, h, :], start=True, stop=True)
                    ins.then_inc(hg_s, 1)
                pe.wait_ge(hg_m, 9 * l + 9)
                pe.wait_ge(hg_dve, HG * l + 14)
                for h in range(4):
                    out = ps[:, 6 + h // 2, :]
                    at = (h % 2) * T
                    nc.tensor.matmul(out[:, at:at + P], v_h[:, h * P:(h + 1) * P], scores[:, 0, h, :],
                                     start=True, stop=True)
                    nc.tensor.matmul(out[:, at + P:at + T], v_h[:, h * P:(h + 1) * P], cross[:, h * P:(h + 1) * P],
                                     start=True, stop=False)
                    ins = nc.tensor.matmul(out[:, at + P:at + T], v_h[:, 512 + h * P:512 + (h + 1) * P],
                                           scores[:, 1, h, :], start=False, stop=True)
                ins.then_inc(hg_pe, 1)
                pe.wait_ge(hg_act, HA * l + 7)
                for n in range(2):
                    ins = nc.tensor.matmul(ps[:, 2 + n, :], ones, sq2[:, 2 * n:2 * n + 2, :], start=True, stop=True)
                ins.then_inc(hg_pe, 1)
                pe.wait_ge(hg_dve, HG * l + HG)
                project(pe, g0, OUT2, 8, q0 + R_OUT, mix_hi, mix_lo, DC)
                norm2(2)
                project(pe, g0, GU2B, 2 * FC, q0 + R_GUB, x_hi, x_lo, DC)
                down(pe, g0, DOWN2B, L + 2 * l + 1)

        @block.scalar
        def _(act):
            act.dma_start(silu_c[:], io["c"]).then_inc(x_in, 16)
            act.wait_ge(x_in, 32)
            act.wait_ge(consts_in, 64)
            nc.scalar.activation(silu_c[:], silu_c[:], ACT.Silu).then_inc(silu_done, 1)
            nc.scalar.activation(x_hi[:], x[:], ACT.Copy).then_inc(x_split_hi, 1)
            for n in range(2):
                dst = (rope_sin, rope_cos)[n]
                act.wait_ge(rope_dve, 10 * (n + 1))
                nc.scalar.activation(dst[64:96, :], dst[64:96, :], ACT.Sin).then_inc(rope_act, 1)

            with act.Fori(0, L) as l:
                g0, q0, h0 = l * GROUPS1, l * PAIRS1, l * HEADS1
                act.wait_ge(par_set, l + 1)
                for p in range(2):
                    feed_hi(act, g0, p)

                def copy_pair(dst):
                    def drain(group, s, q, b):
                        act.wait_ge(panel_used, 4 * group + (s + 5))
                        nc.scalar.activation(dst(q), ps[:, b, :].rearrange("p (n w) -> p n w", w=T),
                                             ACT.Copy).then_inc(pair_out, 1)
                    return drain

                panels(act, g0, B_COLS, 6, feed_hi, copy_pair(lambda q: c_all[:, 2 * q:2 * q + 2, :]), PANELS1)
                act.wait_ge(pair_out, q0 + Q_UQ + 2)
                nc.scalar.activation(sq_b[:], c_all[:, 0:5, :], ACT.Square).then_inc(b_act, 1)
                act.wait_ge(b_dve, l * BD + 2)
                nc.scalar.activation(rstd[:], rstd[:], ACT.Ln).then_inc(b_act, 1)
                act.wait_ge(b_act, l * BA + 2)
                nc.scalar.activation(rstd[:], rstd[:], ACT.Exp, scale=-0.5).then_inc(b_act, 1)
                act.wait_ge(b_dve, l * BD + 10)
                nc.scalar.activation(cn_hi[:], c_all[:, 0:5, :], ACT.Copy).then_inc(b_act, 1)
                for j in range(4):
                    for p in (2 * j + B_UQ + 2, 2 * j + B_UQ + 3):
                        if p < A_QKV:
                            feed_hi(act, g0 + p // 4, p % 4)
                    for p in (B_UQ + 2 * j, B_UQ + 2 * j + 1):
                        act.wait_ge(panel_used, 4 * g0 + p + 5)
                        b = (p - B_UQ) % 2
                        m, dst = (96, q_b) if p < B_UKV else (P, kv_b)
                        h = 2 * ((p - B_UQ) % 4)
                        nc.scalar.activation(dst[0:m, h:h + 2, :], ps[0:m, b, :].rearrange("p (n w) -> p n w", w=T),
                                             ACT.Copy).then_inc(pair_out, 1)
                act.sem_inc(b_act, 1)
                act_attention(act, h0, 8, even_odd, lambda h: br_hi[:, 4 + h // 2, :])
                for p in range(A_QKV, A_QKV + 2):
                    feed_hi(act, g0 + p // 4, p % 4)

                def bias_dma(act, h):
                    act.wait_ge(at_stt, h0 + 8 + h + 1)
                    for blk in range(4):
                        rows = slice(64 * (blk % 2), 64 * (blk % 2) + 64)
                        at = (blk // 2) * T
                        n = T - 64 * blk
                        base = io["rel"][l]
                        src = base[h, blk, :, 0:n]
                        act.dma_start(bias[rows, h % 2, at:at + n], src).then_inc(bias_in[h % 2], 16)
                act.wait_ge(init_done, 1)
                for q in range(6):
                    for p in (A_QKV + 2 * q + 2, A_QKV + 2 * q + 3):
                        if p < C_QKV:
                            feed_hi(act, g0 + p // 4, p % 4)
                    act.wait_ge(panel_used, 4 * g0 + A_QKV + 2 * q + 1 + 5)
                    src = ps[:, q % 2, :].rearrange("p (n w) -> p n w", w=T)
                    if q < 2:
                        src = src[:, :, ::-1]
                    dst = qk[:, 2 * q:2 * q + 2, :] if q < 4 else v_t[:, 2 * q - 8:2 * q - 6, :]
                    nc.scalar.activation(dst, src, ACT.Copy).then_inc(pair_out, 1)
                bias_dma(act, 0)
                bias_dma(act, 1)
                act_attention(act, h0 + 8, 8, even_odd, lambda h: br_hi[:, h // 2, :], True, bias_dma)
                for p in range(C_QKV, C_QKV + 2):
                    feed_hi(act, g0 + p // 4, p % 4)
                for q in range(6):
                    for p in (C_QKV + 2 * q + 2, C_QKV + 2 * q + 3):
                        if p < GATE:
                            feed_hi(act, g0 + p // 4, p % 4)
                    act.wait_ge(panel_used, 4 * g0 + C_QKV + 2 * q + 1 + 5)
                    dst = qk[:, 2 * q:2 * q + 2, :] if q < 4 else v_t[:, 2 * q - 8:2 * q - 6, :]
                    nc.scalar.activation(dst, ps[:, q % 2, :].rearrange("p (n w) -> p n w", w=T),
                                         ACT.Copy).then_inc(pair_out, 1)
                    if q == 0:
                        act.wait_ge(c_dve, l * CD + 1)
                        nc.scalar.activation(fabs[0:8, :], flog[0:8, :], ACT.Abs).then_inc(c_act, 1)
                        act.wait_ge(c_act, l * CA + 1)
                        nc.scalar.activation(fabs[0:8, :], fabs[0:8, :], ACT.Exp, scale=-1.0).then_inc(c_act, 1)
                        act.wait_ge(c_act, l * CA + 2)
                        nc.scalar.activation(fabs[0:8, :], fabs[0:8, :], ACT.Ln, bias=1.0).then_inc(c_act, 1)
                act_attention(act, h0 + 16, 8, even_odd, lambda h: br_hi[:, 8 + h // 2, :])
                act.dma_start(mem[:], io["memT"]).then_inc(mem_in, 16)
                for p in range(GATE, GATE + 2):
                    feed_hi(act, g0 + p // 4, p % 4)
                for q in range(12):
                    for p in (GATE + 2 * q + 2, GATE + 2 * q + 3):
                        feed_hi(act, g0 + p // 4, p % 4)
                    act.wait_ge(panel_used, 4 * g0 + GATE + 2 * q + 1 + 5)
                    for o in range(2):
                        c = 2 * q + o
                        ins = nc.scalar.activation(gates[:, c, :], ps[:, q % 2, o * T:(o + 1) * T], ACT.Sigmoid,
                                                   bias=par[:, P_GATE + c:P_GATE + c + 1])
                    ins.then_inc(pair_out, 1)
                only_feed(act, g0, BRANCH + 2, BRANCH + 12, feed_hi)
                act.wait_ge(br_dve, l * 20 + 20)
                nc.scalar.activation(mg_hi[:], merged[:], ACT.Copy).then_inc(mg_h, 1)
                act.wait_ge(mem_in, 16 * l + 16)
                nc.scalar.activation(mem_hi[:], mem[:], ACT.Copy).then_inc(mem_h, 1)
                only_feed(act, g0, OUT1, X_Q, feed_hi)
                act_norm(act, 3 * l, P_MIXG)
                for p in range(X_Q, X_Q + 2):
                    feed_hi(act, g0 + p // 4, p % 4)
                for q in range(6):
                    for p in (X_Q + 2 * q + 2, X_Q + 2 * q + 3):
                        if p < X_O:
                            feed_hi(act, g0 + p // 4, p % 4)
                    act.wait_ge(panel_used, 4 * g0 + X_Q + 2 * q + 1 + 5)
                    dst = qk[:, 2 * q:2 * q + 2, :] if q < 4 else v_t[:, 2 * q - 8:2 * q - 6, :]
                    nc.scalar.activation(dst, ps[:, q % 2, :].rearrange("p (n w) -> p n w", w=T),
                                         ACT.Copy).then_inc(pair_out, 1)
                act_attention(act, h0 + 24, 4, whole, lambda h: xo_hi[:, h, :])
                for p in range(X_O, X_O + 4):
                    feed_hi(act, g0 + p // 4, p % 4)
                act_norm(act, 3 * l + 1, P_XAG)
                for p in range(GU1, GU1 + 2):
                    feed_hi(act, g0 + p // 4, p % 4)
                act_ffn(act, g0, GU1, l, PANELS1)
                only_feed(act, g0, DOWN1 + 2, PANELS1, feed_hi)
                act_norm(act, 3 * l + 2, P_FFG)

            if stop_after == 1:
                act.wait_ge(x_split, 7)
                act.dma_start(io["out"], x[:]).then_inc(out_in, 16)
                act.wait_ge(out_in, 16)
                return
            act.wait_ge(mod_end, 1)
            act.wait_ge(mod_taken, 9)
            act.dma_start(side[:, 0:N_CONST2], io["const2"]).then_inc(consts2_in, 16)
            act.wait_ge(lb_dve, 1)
            nc.scalar.activation(lb_t[:, 0:2, :], lb_t[:, 0:2, :], ACT.Exp).then_inc(lb_act, 1)
            act.wait_ge(consts2_in, 16)
            with act.Fori(0, L) as l:
                g0, q0, h0 = L * GROUPS1 + l * GROUPS2, L * PAIRS1 + l * PAIRS2, L * HEADS1 + 4 * l

                def norm2(k):
                    run = 3 * l + k
                    act.wait_ge(res2, run + 1)
                    nc.scalar.activation(sq2[:], x[:], ACT.Square).then_inc(rn_act, 1)
                    act.wait_ge(rn_dve, 10 * run + 1)
                    nc.scalar.activation(rstd[:, 0, :], rstd[:, 0, :], ACT.Ln).then_inc(rn_act, 1)
                    act.wait_ge(rn_act, 3 * run + 2)
                    nc.scalar.activation(rstd[:, 0, :], rstd[:, 0, :], ACT.Exp, scale=-0.5).then_inc(rn_act, 1)
                    act.wait_ge(rn_dve, 10 * run + 10)
                    nc.scalar.activation(x_hi[:], normed[:], ACT.Copy).then_inc(x_split_hi, 1)

                def feeds(p0, p1):
                    for p in range(p0, p1):
                        feed_hi(act, g0 + p // 4, p % 4)
                feeds(0, 2)
                norm2(0)
                act_ffn(act, g0, GU2A, L + 2 * l, PANELS2)
                only_feed(act, g0, DOWN2A + 2, IN2 + 2, feed_hi)
                norm2(1)

                def keep(group, s, q, b):
                    act.wait_ge(panel_used, 4 * group + (s + 5))
                    nc.scalar.activation(h_all[:, bass.ds(2 * q, 2), :], ps[:, b, :].rearrange("p (n w) -> p n w", w=T),
                                         ACT.Copy).then_inc(pair_out, 1)
                panels(act, g0, IN2, 28, feed_hi, keep, PANELS2)
                for t in range(6):
                    if t < 4:
                        s_, buf = 3 * (4 * l + t), prob_t[:, t % 2, :]
                        act.wait_ge(sb_d, 2 * (4 * l + t) + 1)
                        nc.scalar.activation(buf, prob[:, t % 2, :], ACT.Abs).then_inc(sb_a, 1)
                        act.wait_ge(sb_a, s_ + 1)
                        nc.scalar.activation(buf, buf, ACT.Exp, scale=-1.0).then_inc(sb_a, 1)
                        act.wait_ge(sb_a, s_ + 2)
                        nc.scalar.activation(buf, buf, ACT.Ln, bias=1.0).then_inc(sb_a, 1)
                    if 1 <= t <= 4:
                        h = t - 1
                        act.wait_ge(sb_lw, 4 * l + h + 1)
                        nc.scalar.activation(prob[:, h % 2, :], prob[:, h % 2, :], ACT.Exp).then_inc(sb_e, 1)
                    if t >= 2:
                        h = t - 2
                        act.wait_ge(sb_o, 4 * l + h + 1)
                        nc.scalar.activation(mix_hi[even_odd(h), h // 2, :], ps[even_odd(h), 6 + h % 2, 0:T],
                                             ACT.Copy).then_inc(sb_oh, 1)
                nc.scalar.activation(rot_tmp[:], h_all[:, 6:10, :], ACT.Square).then_inc(dl_act, 1)
                act.wait_ge(dl_dve, 9 * l + 2)
                nc.scalar.activation(rs4[:], rs4[:], ACT.Ln).then_inc(dl_act, 1)
                act.wait_ge(dl_act, 3 * l + 2)
                nc.scalar.activation(rs4[:], rs4[:], ACT.Exp, scale=-0.5).then_inc(dl_act, 1)
                act_attention(act, h0, 4, even_odd, lambda h: mix_hi[:, 2 + h // 2, :])
                ha = HA * l
                nc.scalar.activation(logf[:], h_all[:, 16:20, :], ACT.Sigmoid).then_inc(hg_act, 1)
                act.wait_ge(hg_act, ha + 1)
                nc.scalar.activation(h_all[:, 16:20, :], h_all[:, 16:20, :], ACT.Sigmoid, scale=-1.0)\
                    .then_inc(hg_act, 1)
                nc.scalar.activation(h_all[:, 12:16, :], h_all[:, 12:16, :], ACT.Silu).then_inc(hg_act, 1)
                nc.scalar.activation(h_all[:, 24:28, :], h_all[:, 24:28, :], ACT.Silu).then_inc(hg_act, 1)
                act.wait_ge(hg_dve, HG * l + 10)
                nc.scalar.activation(logf[:], logf[:], ACT.Ln).then_inc(hg_act, 1)
                nc.scalar.activation(logf_b[:], logf_b[:], ACT.Ln).then_inc(hg_act, 1)
                for level in range(8):
                    act.wait_ge(hg_d, 8 * l + level + 1)
                    if level:
                        act.wait_ge(hg_qe, 8 * l + level)
                        act.wait_ge(hg_ke, 8 * l + level)
                    nc.scalar.activation(F[:, 0:1024].rearrange("p (b c) -> p b c", b=2), ps[:, 2:4, :],
                                         ACT.Exp).then_inc(hg_exp, 1)
                act.wait_ge(hg_pe, 3 * l + 2)
                act.wait_ge(hg_ke, 8 * l + 8)
                act.wait_ge(hg_qe, 8 * l + 8)
                nc.scalar.activation(F[:, 0:1024].rearrange("p (b c) -> p b c", b=2), ps[:, 6:8, :],
                                     ACT.Square).then_inc(hg_act, 1)
                act.wait_ge(hg_dve, HG * l + 18)
                nc.scalar.activation(h_qe, h_qe, ACT.Ln).then_inc(hg_act, 1)
                act.wait_ge(hg_act, ha + 8)
                nc.scalar.activation(h_qe, h_qe, ACT.Exp, scale=-0.5).then_inc(hg_act, 1)
                act.wait_ge(hg_dve, HG * l + 20)
                nc.scalar.activation(mix_hi[:, 4:8, :], o_h[:], ACT.Copy).then_inc(hg_hi, 1)
                feeds(OUT2 + 2, GU2B + 2)
                norm2(2)
                act_ffn(act, g0, GU2B, L + 2 * l + 1, PANELS2)
                only_feed(act, g0, DOWN2B + 2, PANELS2, feed_hi)
            act.wait_ge(res2, 3 * L + 1)
            act.dma_start(io["out"], x[:]).then_inc(out_in, 16)
            act.wait_ge(out_in, 16)

        @block.vector
        def _(dve):
            nc.vector.memset(bias[:], NEG).then_inc(init_done, 1)
            dve.wait_ge(x_split_hi, 1)
            nc.vector.tensor_tensor(x_lo[:], x[:], x_hi[:].bitcast(F32), ALU.subtract).then_inc(x_split, 1)
            two_pi = 2.0 * np.pi
            hi = float(np.float32(np.round(two_pi * 256) / 256))
            mid = float(np.float32(np.round((two_pi - hi) * 2 ** 20) / 2 ** 20))
            low = float(np.float32(two_pi - hi - mid))
            magic = 12582912.0
            edge = 3.1415925
            rows = slice(64, 96)
            ang, turns = F[rows, 4096:4352], F[rows, 4352:4608]
            step = 0

            def chain(ins):
                nonlocal step
                ins.then_inc(rope_dve, 1)
                step += 1
                dve.wait_ge(rope_dve, step)
            dve.wait_ge(consts_in, 64)
            for n in range(2):
                out = (rope_sin, rope_cos)[n][rows, :]
                nc.vector.tensor_copy(ang, pos_i[rows, :]).then_inc(rope_dve, 1)
                step += 1
                dve.wait_ge(rope_dve, step)
                chain(nc.vector.tensor_scalar(ang, ang, c_("invf")[rows, :], None, ALU.mult))
                chain(nc.vector.tensor_scalar(turns, ang, 1.0 / two_pi, 0.25 * n, ALU.mult, ALU.add))
                chain(nc.vector.tensor_scalar(turns, turns, magic, None, ALU.add))
                chain(nc.vector.tensor_scalar(turns, turns, -magic, None, ALU.add))
                chain(nc.vector.scalar_tensor_tensor(out=ang, in0=turns, scalar=-hi, in1=ang,
                                                     op0=ALU.mult, op1=ALU.add))
                chain(nc.vector.scalar_tensor_tensor(out=ang, in0=turns, scalar=-mid, in1=ang,
                                                     op0=ALU.mult, op1=ALU.add))
                chain(nc.vector.scalar_tensor_tensor(out=ang, in0=turns, scalar=-low, in1=ang,
                                                     op0=ALU.mult, op1=ALU.add))
                chain(nc.vector.tensor_scalar(out, ang, 0.5 * np.pi * n, edge, ALU.add, ALU.min))
                chain(nc.vector.tensor_scalar(out, out, -edge, None, ALU.max))

            with dve.Fori(0, L) as l:
                g0, q0, h0 = l * GROUPS1, l * PAIRS1, l * HEADS1
                nc.vector.tensor_copy(par[:], par_all[:, l, :]).then_inc(par_set, 1)
                bd = l * BD
                for p in range(2):
                    feed_lo(dve, g0, p)
                for p in range(2, 8):
                    feed_lo(dve, g0 + p // 4, p % 4)
                dve.wait_ge(b_pe, l * BP + 2)
                nc.vector.tensor_scalar(rstd[:, 0, :], ps[:, 2, 0:T], 1.0 / 384, 1e-6, ALU.mult, ALU.add)\
                    .then_inc(b_dve, 1)
                nc.vector.tensor_scalar(rstd[:, 1, :], ps[:, 2, T:2 * T], 1.0 / 256, 1e-6, ALU.mult, ALU.add)\
                    .then_inc(b_dve, 1)
                dve.wait_ge(rope_act, 2)
                dve.wait_ge(pair_out, q0 + Q_UQ + 2)
                turned = rot_b[rows, 0, :]
                nc.vector.tensor_tensor(turned, ps[rows, 3, 0:T], rope_sin[rows, :], ALU.mult).then_inc(b_dve, 1)
                nc.vector.tensor_tensor(c_all[rows, 5, :], c_all[rows, 5, :], rope_cos[rows, :], ALU.mult)\
                    .then_inc(b_dve, 1)
                dve.wait_ge(b_dve, bd + 4)
                nc.vector.tensor_tensor(c_all[rows, 5, :], c_all[rows, 5, :], turned, ALU.add).then_inc(b_dve, 1)
                dve.wait_ge(b_act, l * BA + 3)
                dve.wait_ge(par_set, l + 1)
                for c in range(5):
                    nc.vector.scalar_tensor_tensor(out=c_all[:, c, :], in0=c_all[:, c, :],
                                                   scalar=par[:, P_QN + c:P_QN + c + 1], in1=rstd[:, c // 3, :],
                                                   op0=ALU.mult, op1=ALU.mult).then_inc(b_dve, 1)
                dve.wait_ge(b_act, l * BA + 4)
                nc.vector.tensor_tensor(cn_lo[:], c_all[:, 0:5, :], cn_hi[:].bitcast(F32), ALU.subtract)\
                    .then_inc(b_dve, 1)
                for p in range(8, A_QKV):
                    feed_lo(dve, g0 + p // 4, p % 4)
                dve.wait_ge(b_act, l * BA + 5)
                dve.wait_ge(pair_out, q0 + Q_A + 2)
                dve.wait_ge(b_dve, bd + 5)
                for h in range(8):
                    ins = nc.vector.tensor_copy(k_b[64:96, h, :], c_all[rows, 5, :])
                ins.then_inc(b_dve, 1)
                nc.vector.tensor_copy(k_b[0:64, :, :], kv_b[0:64, :, :]).then_inc(b_dve, 1)
                dve.wait_ge(b_pe, l * BP + 3)
                for h in range(0, 8, 2):
                    ins = nc.vector.tensor_tensor(
                        rot_b[rows, h:h + 2, :], ps[rows, 2 + h // 2, :].rearrange("p (n w) -> p n w", w=T),
                        rope_sin[rows, :].rearrange("p (o t) -> p o t", o=1).broadcast_to([32, 2, T]), ALU.mult)
                    ins.then_inc(b_dve, 1)
                nc.vector.tensor_tensor(q_b[rows, :, :], q_b[rows, :, :],
                                        rope_cos[rows, :].rearrange("p (o t) -> p o t", o=1)
                                        .broadcast_to([32, 8, T]), ALU.mult).then_inc(b_dve, 1)
                dve.wait_ge(b_dve, bd + 18)
                nc.vector.tensor_tensor(q_b[rows, :, :], q_b[rows, :, :], rot_b[rows, :, :], ALU.add)\
                    .then_inc(b_dve, 1)
                dve.wait_ge(b_pe, l * BP + 4)
                for tile in range(2):
                    nc.vector.tensor_copy(v_nat[:, tile * 512:(tile + 1) * 512], ps[:, 6 + tile, :])\
                        .then_inc(b_dve, 1)
                dve_attention(dve, h0, 8, even_odd, lambda h: br_hi[:, 4 + h // 2, :],
                              lambda h: br_lo[:, 4 + h // 2, :], 96.0 ** -0.5, lambda t: c_("chunk_mask"))
                nc.vector.tensor_scalar(flog[0:8, :], c_all[0:8, 5, :], par[0:8, P_BF:P_BF + 1], None, ALU.add)\
                    .then_inc(c_dve, 1)
                for p in range(A_QKV, C_QKV):
                    feed_lo(dve, g0 + p // 4, p % 4)
                dve_turn_v(dve, 3 * l)

                def bias_wait(dve, h):
                    dve.wait_ge(bias_in[h % 2], 64 * (4 * l + h // 2 + 1))
                dve_attention(dve, h0 + 8, 8, even_odd, lambda h: br_hi[:, h // 2, :],
                              lambda h: br_lo[:, h // 2, :], 0.125, lambda h: bias[:, h % 2, :], bias_wait)
                dve_mod(dve, 4 * l)
                for p in range(C_QKV, C_QKV + 8):
                    feed_lo(dve, g0 + p // 4, p % 4)
                dve.wait_ge(c_act, l * CA + 3)
                dve.wait_ge(c_dve, l * CD + 1)
                nc.vector.tensor_scalar(flog[0:8, :], flog[0:8, :], 0.0, None, ALU.min).then_inc(c_dve, 1)
                dve.wait_ge(c_dve, l * CD + 2)
                nc.vector.tensor_tensor(flog[0:8, :], flog[0:8, :], fabs[0:8, :], ALU.subtract).then_inc(c_dve, 1)
                for p in range(C_QKV + 8, GATE):
                    feed_lo(dve, g0 + p // 4, p % 4)
                dve.wait_ge(c_pe, l * CP + 1)
                f_src = ps[:, 2, 0:16].rearrange("p (t c) -> p t c", t=2)
                nc.vector.tensor_scalar(f_nat[:, :, 0:8], f_src, 8.0, None, ALU.mult).then_inc(c_dve, 1)
                nc.vector.tensor_scalar(f_nat[:, :, 8:16], f_src, -8.0, None, ALU.mult).then_inc(c_dve, 1)
                dve.wait_ge(c_pe, l * CP + 2)
                nc.vector.tensor_scalar(fl0[:], ps[0:16, 2, T:2 * T], c_("is_f")[0:16, :], c_("is_one")[0:16, :],
                                        ALU.mult, ALU.add).then_inc(c_dve, 1)
                nc.vector.tensor_scalar(fr[:], ps[0:16, 2, T:2 * T], c_("is_one")[0:16, :], c_("is_f")[0:16, :],
                                        ALU.mult, ALU.add).then_inc(c_dve, 1)
                dve.wait_ge(c_dve, l * CD + 7)
                nc.vector.tensor_tensor(fl[0:16, :, :], fl0[:].rearrange("p (o t) -> p o t", o=1)
                                        .broadcast_to([16, 8, T]),
                                        c_("head")[0:16, :].rearrange("p (h o) -> p h o", o=1)
                                        .broadcast_to([16, 8, T]), ALU.mult).then_inc(c_dve, 1)
                dve_turn_v(dve, 3 * l + 1)
                dve_attention(dve, h0 + 16, 8, even_odd, lambda h: br_hi[:, 8 + h // 2, :],
                              lambda h: br_lo[:, 8 + h // 2, :], 0.125, lambda t: c_("causal_mask"))
                for p in range(GATE, BRANCH + 2):
                    feed_lo(dve, g0 + p // 4, p % 4)
                dve_mod(dve, 4 * l + 1)
                step = 0
                for j in range(12):
                    p = BRANCH + j + 2
                    if p < OUT1:
                        feed_lo(dve, g0 + p // 4, p % 4)
                    n, c = j // 4, 2 * (j % 4)
                    dve.wait_ge(panel_used, 4 * g0 + BRANCH + j + 5)
                    dve.wait_ge(pair_out, q0 + Q_BR + 2)
                    gate = gates[:, 8 * n + c:8 * n + c + 2, :]
                    src = ps[:, j % 2, :].rearrange("p (n w) -> p n w", w=T)
                    tmp = gate_tmp.rearrange("p (n w) -> p n w", w=T)
                    dst = merged[:, c:c + 2, :] if n == 0 else tmp
                    nc.vector.tensor_tensor(dst, src, gate, ALU.mult).then_inc(br_dve, 1)
                    step += 1
                    dve.wait_ge(br_dve, l * 20 + step)
                    dve.sem_inc(pair_out, 1)
                    if n:
                        nc.vector.tensor_tensor(merged[:, c:c + 2, :], merged[:, c:c + 2, :], tmp, ALU.add)\
                            .then_inc(br_dve, 1)
                        step += 1
                        dve.wait_ge(br_dve, l * 20 + step)
                dve.wait_ge(mg_h, l + 1)
                nc.vector.tensor_tensor(mg_lo[:], merged[:], mg_hi[:].bitcast(F32), ALU.subtract).then_inc(mg_l, 1)
                dve.wait_ge(mem_h, l + 1)
                nc.vector.tensor_tensor(mem_lo[:], mem[:], mem_hi[:].bitcast(F32), ALU.subtract).then_inc(mem_l, 1)

                def residual(p0, n_pairs, per_panel):
                    for q in range(n_pairs):
                        last = p0 + (2 * q + 1 if per_panel == 1 else q)
                        dve.wait_ge(panel_used, 4 * g0 + last + 5)
                        dst = x[:, 2 * q:2 * q + 2, :]
                        nc.vector.scalar_tensor_tensor(out=dst, in0=dst, scalar=ALPHA,
                                                       in1=ps[:, q % 2, :].rearrange("p (n w) -> p n w", w=T),
                                                       op0=ALU.mult, op1=ALU.add).then_inc(pair_out, 1)
                        for p in (last + 3, last + 4) if per_panel == 1 else ():
                            if p < p0 + 8:
                                feed_lo(dve, g0 + p // 4, p % 4)
                for p in range(OUT1, OUT1 + 4):
                    feed_lo(dve, g0 + p // 4, p % 4)
                residual(OUT1, 4, 1)
                dve_norm(dve, 3 * l)
                for p in range(X_Q, X_O):
                    feed_lo(dve, g0 + p // 4, p % 4)
                dve_turn_v(dve, 3 * l + 2)
                dve_attention(dve, h0 + 24, 4, whole, lambda h: xo_hi[:, h, :], lambda h: xo_lo[:, h, :],
                              128.0 ** -0.5, None)
                for p in range(X_O, X_O + 4):
                    feed_lo(dve, g0 + p // 4, p % 4)
                residual(X_O, 4, 2)
                dve_norm(dve, 3 * l + 1)
                dve_mod(dve, 4 * l + 2)
                for p in range(GU1, GU1 + 2):
                    feed_lo(dve, g0 + p // 4, p % 4)
                dve_ffn(dve, g0, GU1, l, q0 + Q_GU, PANELS1)
                only_feed(dve, g0, DOWN1 + 2, PANELS1, feed_lo)
                dve.wait_ge(panel_used, 4 * g0 + PANELS1 + 4)
                for q in range(4):
                    dst = x[:, 2 * q:2 * q + 2, :]
                    nc.vector.scalar_tensor_tensor(out=dst, in0=dst, scalar=ALPHA,
                                                   in1=ps[:, 4 + q, :].rearrange("p (n w) -> p n w", w=T),
                                                   op0=ALU.mult, op1=ALU.add).then_inc(down_out, 1)
                dve_norm(dve, 3 * l + 2)
                dve_mod(dve, 4 * l + 3)

            if stop_after < 2:
                return
            dve.wait_ge(lbl_in, 16)
            nc.vector.tensor_tensor(lb_t[:, 2, :], lbl[:, 0, :], lbl[:, 1, :], ALU.max).then_inc(lb_c, 1)
            dve.wait_ge(lb_c, 1)
            nc.vector.tensor_tensor(lb_t[:, 0:2, :], lbl[:], lb_t[:, 2:3, :].broadcast_to([P, 2, 4]),
                                    ALU.subtract).then_inc(lb_dve, 1)
            dve.wait_ge(lb_act, 1)
            nc.vector.tensor_tensor(lb_t[:, 2, :], lb_t[:, 0, :], lb_t[:, 1, :], ALU.add).then_inc(lb_c, 1)
            dve.wait_ge(lb_c, 2)
            nc.vector.reciprocal(lb_t[:, 2, :], lb_t[:, 2, :]).then_inc(lb_c, 1)
            dve.wait_ge(lb_c, 3)
            nc.vector.tensor_tensor(lb_t[:, 0:2, :], lb_t[:, 0:2, :], lb_t[:, 2:3, :].broadcast_to([P, 2, 4]),
                                    ALU.mult).then_inc(lb_c, 1)
            dve.wait_ge(lb_c, 4)
            nc.vector.tensor_tensor(lb[:, 0, :], lb_t[:, 0, :], lb_t[:, 0, :], ALU.subtract).then_inc(lb_c, 1)
            nc.vector.tensor_tensor(lb_t[:, 2, :], lb_t[:, 0, :], lb_t[:, 1, :], ALU.add).then_inc(lb_c, 1)
            dve.wait_ge(lb_c, 6)
            nc.vector.tensor_tensor(lb[:, 1, :], lb_t[:, 2, :], lb_t[:, 0, :], ALU.subtract).then_inc(lb_c, 1)
            dve.wait_ge(lb_c, 7)
            nc.vector.tensor_scalar(lb[:], lb[:], 0.0, 1.0 - 1e-6, ALU.max, ALU.min).then_inc(lb_c, 1)
            dve.wait_ge(lb_c, 8)
            dve.wait_ge(mod_out, 8)
            dve.wait_ge(consts2_in, 16)
            nc.vector.tensor_copy(lb_t[:], lb_t[:]).then_inc(res2, 1)
            with dve.Fori(0, L) as l:
                g0, q0, h0 = L * GROUPS1 + l * GROUPS2, L * PAIRS1 + l * PAIRS2, L * HEADS1 + 4 * l
                nc.vector.tensor_copy(par2[:], par2_all[:, l, :]).then_inc(mod_set, 1)
                nc.vector.tensor_tensor(modl[:], modv[:, bass.ds(l * MOD_CHUNKS, MOD_CHUNKS)],
                                        par2_all[:, l, 0:MOD_CHUNKS], ALU.add).then_inc(mod_set, 1)
                nc.vector.tensor_copy(lbc[:, 0, :], lb[:, l, :]).then_inc(mod_set, 1)
                dve.wait_ge(mod_set, 10 * l + 3)
                nc.vector.tensor_scalar(lbc[:, 1, :], lbc[:, 0, :], 1e-30, None, ALU.max).then_inc(mod_set, 1)
                dve.wait_ge(mod_set, 10 * l + 4)
                nc.vector.tensor_scalar(lbc[:, 0, :], lbc[:, 0, :], -1.0, 1.0, ALU.mult, ALU.add).then_inc(mod_set, 1)
                for at in (8, 32, 56):
                    nc.vector.tensor_scalar(modl[:, at:at + 8], modl[:, at:at + 8], 1.0, None, ALU.add)\
                        .then_inc(mod_set, 1)
                for at in (16, 64):
                    nc.vector.tensor_scalar(modl[:, at:at + 8], modl[:, at:at + 8], 0.5, None, ALU.mult)\
                        .then_inc(mod_set, 1)
                dve.wait_ge(mod_set, 10 * l + 10)

                def norm2(k):
                    run = 3 * l + k
                    dve.wait_ge(rn_pe, run + 1)
                    nc.vector.tensor_scalar(rstd[:, 0, :], ps[:, 2, 0:T], 1.0 / D, 1e-6, ALU.mult, ALU.add)\
                        .then_inc(rn_dve, 1)
                    dve.wait_ge(rn_act, 3 * run + 3)
                    nc.vector.tensor_tensor(normed[:], x[:], over(rstd[:, 0, :], DC), ALU.mult).then_inc(rn_dve, 1)
                    dve.wait_ge(rn_dve, 10 * run + 2)
                    for c in range(DC):
                        at = 24 * k + c
                        nc.vector.tensor_scalar(normed[:, c, :], normed[:, c, :], modl[:, at + 8:at + 9],
                                                modl[:, at:at + 1], ALU.mult, ALU.add).then_inc(rn_dve, 1)
                    dve.wait_ge(x_split_hi, 3 * L + 1 + run + 1)
                    nc.vector.tensor_tensor(x_lo[:], normed[:], x_hi[:].bitcast(F32), ALU.subtract)\
                        .then_inc(x_split, 1)

                def feeds(p0, p1):
                    for p in range(p0, p1):
                        feed_lo(dve, g0 + p // 4, p % 4)

                def add_down(end, k):
                    dve.wait_ge(panel_used, 4 * g0 + end + 4)
                    for c in range(DC):
                        at = 24 * k + 16 + c
                        ins = nc.vector.scalar_tensor_tensor(
                            out=x[:, c, :], in0=ps[:, 4 + c // 2, (c % 2) * T:(c % 2 + 1) * T],
                            scalar=modl[:, at:at + 1], in1=x[:, c, :], op0=ALU.mult, op1=ALU.add)
                        ins.then_inc(down_out if c % 2 else rn_x, 1)
                    dve.wait_ge(down_out, 4 * (L + 2 * l + k // 2) + 5)
                    dve.sem_inc(res2, 1)
                feeds(0, 2)
                norm2(0)
                dve_ffn(dve, g0, GU2A, L + 2 * l, q0 + R_GUA, PANELS2)
                only_feed(dve, g0, DOWN2A + 2, IN2 + 2, feed_lo)
                add_down(IN2, 0)
                norm2(1)
                feeds(IN2 + 2, IN2 + 30)
                dve_turn_v(dve, 3 * L + 2 * l)
                for t in range(6):
                    if t < 4:
                        h, b = 4 * l + t, t % 2
                        dve.wait_ge(sb_z, h + 1)
                        if t >= 2:
                            dve.wait_ge(sb_o, h - 1)
                        nc.vector.tensor_scalar(prob[:, b, :], ps[:, 2 + b, :], 0.125, None, ALU.mult)\
                            .then_inc(sb_d, 1)
                        dve.wait_ge(sb_a, 3 * h + 3)
                        dve.wait_ge(sb_d, 2 * h + 1)
                        nc.vector.scalar_tensor_tensor(out=prob_t[:, b, :], in0=prob[:, b, :], scalar=0.0,
                                                       in1=prob_t[:, b, :], op0=ALU.max, op1=ALU.add)\
                            .then_inc(sb_d, 1)
                        dve.wait_ge(sb_d, 2 * h + 2)
                        nc.vector.scalar_tensor_tensor(out=prob_t[:, b, :], in0=prob_t[:, b, :], scalar=-1.0,
                                                       in1=c2("before"), op0=ALU.mult, op1=ALU.mult)\
                            .then_inc(sb_l, 1)
                    if 1 <= t <= 4:
                        h, b = 4 * l + t - 1, (t - 1) % 2
                        dve.wait_ge(sb_t, h + 1)
                        nc.vector.tensor_tensor(prob[:, b, :], prob[:, b, :], ps[:, 4 + b, :], ALU.add)\
                            .then_inc(sb_lw, 1)
                        dve.wait_ge(sb_e, h + 1)
                        nc.vector.scalar_tensor_tensor(out=prob[:, b, :], in0=prob[:, b, :], scalar=1.0,
                                                       in1=c2("before"), op0=ALU.min, op1=ALU.mult)\
                            .then_inc(sb_w, 1)
                    if t >= 2:
                        h = t - 2
                        dve.wait_ge(sb_oh, 4 * l + h + 1)
                        nc.vector.tensor_tensor(mix_lo[even_odd(h), h // 2, :], ps[even_odd(h), 6 + h % 2, 0:T],
                                                mix_hi[even_odd(h), h // 2, :].bitcast(F32), ALU.subtract)\
                            .then_inc(sb_ol, 1)
                dd = 9 * l
                dve.wait_ge(dl_pe, 2 * l + 1)
                for n in range(2):
                    nc.vector.tensor_scalar(rs4[:, 2 * n:2 * n + 2, :], ps[:, 2 + n, :]
                                            .rearrange("p (n w) -> p n w", w=T), 1.0 / 64, 1e-6, ALU.mult, ALU.add)\
                        .then_inc(dl_dve, 1)
                dve.wait_ge(dl_act, 3 * l + 3)
                for n in range(2):
                    v = h_all[:, 6 + 2 * n:8 + 2 * n, :]
                    nc.vector.scalar_tensor_tensor(out=v, in0=v, scalar=par2[:, P2_QG + n:P2_QG + n + 1],
                                                   in1=rs4[:, 2 * n:2 * n + 2, :], op0=ALU.mult, op1=ALU.mult)\
                        .then_inc(dl_dve, 1)
                dve.wait_ge(dl_pe, 2 * l + 2)
                for n in range(2):
                    nc.vector.tensor_tensor(rot_tmp[:, 2 * n:2 * n + 2, :],
                                            ps[:, 2 + n, :].rearrange("p (n w) -> p n w", w=T),
                                            over(c2("sin"), 2), ALU.mult).then_inc(dl_dve, 1)
                v = h_all[:, 6:10, :]
                nc.vector.tensor_tensor(v, v, over(c2("cos"), 4), ALU.mult).then_inc(dl_dve, 1)
                dve.wait_ge(dl_dve, dd + 7)
                nc.vector.tensor_tensor(v, v, rot_tmp[:], ALU.add).then_inc(dl_dve, 1)
                dve.wait_ge(dl_dve, dd + 8)
                dve.sem_inc(dl_dve, 1)
                dve_attention(dve, h0, 4, even_odd, lambda h: mix_hi[:, 2 + h // 2, :],
                              lambda h: mix_lo[:, 2 + h // 2, :], 0.125, lambda t: c2("dilated"))
                hd = HG * l
                dve.wait_ge(hg_act, HA * l + 4)
                for c in range(4):
                    nc.vector.tensor_scalar(logf[:, c, :], logf[:, c, :], lbc[:, 0, c:c + 1], lbc[:, 1, c:c + 1],
                                            ALU.mult, ALU.add).then_inc(hg_dve, 1)
                    nc.vector.tensor_scalar(h_all[:, 16 + c, :], h_all[:, 16 + c, :], lbc[:, 0, c:c + 1], None,
                                            ALU.mult).then_inc(hg_dve, 1)
                dve.wait_ge(hg_dve, hd + 8)
                nc.vector.tensor_scalar(logf_b[:], logf[:], 2.0 ** 50, 1.0, ALU.mult, ALU.min).then_inc(hg_dve, 1)
                dve.wait_ge(hg_dve, hd + 9)
                nc.vector.tensor_scalar(logf[:], logf[:], 2.0 ** -50, None, ALU.max).then_inc(hg_dve, 1)
                dve.wait_ge(hg_act, HA * l + 6)
                nc.vector.tensor_tensor(logf[:], logf[:], logf_b[:], ALU.add).then_inc(hg_dve, 1)
                dve.wait_ge(hg_pe, 3 * l + 1)
                for tile in range(2):
                    nc.vector.tensor_copy(logf_nat[:, tile * 512:(tile + 1) * 512], ps[:, 2 + tile, :])\
                        .then_inc(hg_dve, 1)
                dve_turn_v(dve, 3 * L + 2 * l + 1, v_h)
                for level in range(9):
                    if level < 8:
                        dve.wait_ge(hg_exp, 8 * l + level + 1)
                        dst, a, b = (h_qe, q_h, h_e) if level < 7 else (h_qe[:, 1], q_h[:, 1], h_e[:, 1])
                        nc.vector.tensor_tensor(dst, a, b, ALU.mult).then_inc(hg_qe, 1)
                    dve.wait_ge(hg_s, 9 * l + level + 2)
                    if level == 7:
                        nc.vector.tensor_copy(cross, ps[:, 4, :]).then_inc(hg_m, 1)
                        continue
                    at = level if level < 7 else 7
                    mask = c2("levels")[:, at * P:(at + 1) * P].rearrange("p (o t) -> p o t", o=1)
                    src = ps[:, 4:6, :].rearrange("p k (h t) -> p (k h) t", h=4)
                    flat = (lambda v: v.rearrange("p k h t -> p (k h) t"))
                    dst = scores if level == 0 else h_qe
                    nc.vector.tensor_tensor(flat(dst), src, mask.broadcast_to([P, 8, P]), ALU.mult).then_inc(hg_m, 1)
                    dve.wait_ge(hg_m, 9 * l + level + 1)
                    if level:
                        ins = nc.vector.tensor_tensor(flat(scores), flat(scores), flat(h_qe), ALU.add)
                        ins.then_inc(hg_a if level < 8 else hg_dve, 1)
                        if level < 8:
                            dve.wait_ge(hg_a, 6 * l + level)
                dve.wait_ge(hg_act, HA * l + 7)
                for n in range(2):
                    nc.vector.tensor_copy(o_h[:, 2 * n:2 * n + 2, :],
                                          ps[:, 6 + n, :].rearrange("p (n w) -> p n w", w=T)).then_inc(hg_dve, 1)
                dve.wait_ge(hg_pe, 3 * l + 3)
                for n in range(2):
                    nc.vector.tensor_scalar(F[:, 1024 + 512 * n:1536 + 512 * n], ps[:, 2 + n, :], 1.0 / P, 1e-6,
                                            ALU.mult, ALU.add).then_inc(hg_dve, 1)
                dve.wait_ge(hg_act, HA * l + 9)
                nc.vector.scalar_tensor_tensor(out=o_h[:], in0=o_h[:], scalar=par2[:, P2_HG:P2_HG + 1],
                                               in1=f(1024, 4), op0=ALU.mult, op1=ALU.mult).then_inc(hg_dve, 1)
                dve.wait_ge(hg_dve, hd + 19)
                nc.vector.tensor_tensor(o_h[:], o_h[:], h_all[:, 24:28, :], ALU.mult).then_inc(hg_dve, 1)
                dve.wait_ge(hg_hi, l + 1)
                nc.vector.tensor_tensor(mix_lo[:, 4:8, :], o_h[:], mix_hi[:, 4:8, :].bitcast(F32), ALU.subtract)\
                    .then_inc(hg_dve, 1)
                feeds(OUT2 + 2, OUT2 + 4)
                for q in range(4):
                    dve.wait_ge(panel_used, 4 * g0 + OUT2 + 2 * q + 1 + 5)
                    for c in (2 * q, 2 * q + 1):
                        ins = nc.vector.scalar_tensor_tensor(
                            out=x[:, c, :], in0=ps[:, q % 2, (c % 2) * T:(c % 2 + 1) * T],
                            scalar=modl[:, 40 + c:41 + c], in1=x[:, c, :], op0=ALU.mult, op1=ALU.add)
                        ins.then_inc(pair_out if c % 2 else rn_x, 1)
                    feeds(OUT2 + 2 * q + 4, min(OUT2 + 2 * q + 6, GU2B + 2))
                dve.wait_ge(pair_out, q0 + R_GUB + 2)
                dve.sem_inc(res2, 1)
                norm2(2)
                dve_ffn(dve, g0, GU2B, L + 2 * l + 1, q0 + R_GUB, PANELS2)
                only_feed(dve, g0, DOWN2B + 2, PANELS2, feed_lo)
                add_down(PANELS2, 2)


def constants():
    c = {}
    i = np.arange(P)
    t = np.arange(T)
    c["ident"] = np.eye(P)
    c["ones"] = np.ones((P, P))
    rot32 = np.zeros((P, 32))
    for m in range(16):
        rot32[64 + m + 16, m] = -1.0
        rot32[64 + m, m + 16] = 1.0
    c["rot32"] = rot32

    def tiles(a):
        return a.reshape(2, P, -1).transpose(1, 0, 2).reshape(P, -1)
    c["tri"] = tiles((t[:, None] <= t[None, :]).astype(np.float32))
    c["chunk_mask"] = tiles(np.where(t[None, :] // 64 <= t[:, None] // 64, 0.0, NEG))
    c["causal_mask"] = tiles(np.where(t[None, :] <= t[:, None], 0.0, NEG))
    invf = np.zeros((P, 1), np.float32)
    invf[64:96, 0] = np.tile(np.float32(10000.0) ** (-np.arange(16, dtype=np.float32) / np.float32(16)), 2)
    c["invf"] = invf
    c["is_f"] = (i < 8)[:, None] * 1.0
    c["is_one"] = ((i >= 8) & (i < 16))[:, None] * 1.0
    c["head"] = (i[:, None] % 8 == np.arange(8)[None, :]) * 1.0
    c["block64"] = (i[:, None] // 64 == i[None, :] // 64) * 1.0
    rot64 = np.zeros((P, P))
    for b in (0, 64):
        for m in range(32):
            rot64[b + m + 32, b + m] = -1.0
            rot64[b + m, b + m + 32] = 1.0
    c["rot64"] = rot64
    f64 = np.float32(10000.0) ** (-np.arange(32, dtype=np.float32) * np.float32(2.0) / np.float32(64))
    ang = t.astype(np.float32)[None, :] * np.tile(f64, 4)[:, None]
    c["cos"], c["sin"] = np.cos(ang), np.sin(ang)
    dist = t[:, None] - t[None, :]
    count = sum(((dist >= 0) & (dist % s == 0) & (dist // s <= P)).astype(int) for s in (1, 4, 16))
    c["dilated"] = tiles(np.where(count > 0, np.log(np.maximum(count, 1)), NEG))
    spans, levels = [], []
    for h in (1, 2, 4, 8, 16, 32, 64):
        base = i // (2 * h) * (2 * h)
        u, b, s = i[:, None], base[None, :], i[None, :]
        right = (s - b) >= h
        spans.append(np.where(right, (u >= b + h) & (u <= s), (u > s) & (u < b + h)) * 1.0)
        same = base[:, None] == base[None, :]
        levels.append((same & ((i - base)[:, None] < h) & ((i - base)[None, :] >= h)) * 1.0)
    spans.append((i[:, None] > i[None, :]) * 1.0)
    spans.append((i[:, None] <= i[None, :]) * 1.0)
    levels.append(np.eye(P))
    c["spans"], c["levels"] = np.concatenate(spans, 1), np.concatenate(levels, 1)
    c["before"] = tiles((t[:, None] < t[None, :]) * 1.0)
    c["suffix"] = (i[:, None] >= i[None, :]) * 1.0
    return [np.concatenate([np.asarray(c[n], np.float32).reshape(P, w) for n, (_, w) in which.items()], 1)
            for which in (CONSTS, CONSTS2)]


def k_panels(w, cols):
    k, n = w.shape
    a = w.reshape(k // P, P, n // cols, cols).transpose(2, 1, 0, 3).reshape(n // cols, P, -1)
    if a.shape[2] < W:
        a = np.pad(a, ((0, 0), (0, 0), (0, W - a.shape[2])))
    return a


def columns(v):
    return v.reshape(-1, P).T


def kernel(**inputs):
    import concourse.bacc as _bacc
    from concourse.bass_utils import run_bass_kernel_spmd as _run

    a = {n: np.asarray(v) for n, v in inputs.items()}
    stream = []
    for l in range(L):
        w_in = a["w_in"][l]
        b = w_in[:, 1536:2208]
        c_at, f_at, g_at = 2208, 3744, 3752
        z = np.zeros((D, 56), np.float32)
        odd = np.concatenate([w_in[:, f_at:f_at + 8], z, b[:, 640:672], z[:, :32]], 1)
        stream += [k_panels(np.concatenate([b[:, :640], odd], 1), P),
                   k_panels(a["b_w_uq"][l], 192), k_panels(a["b_w_ukv"][l], 256),
                   k_panels(w_in[:, :1536], P), k_panels(w_in[:, c_at:c_at + 1536], P),
                   k_panels(w_in[:, g_at:], P)]
        stream += [k_panels(a["w_branch"][l, n], 256) for n in range(3)]
        stream += [k_panels(a["w_mix_out"][l], P), k_panels(a["xa_w_q"][l], P), k_panels(a["xa_w_kv"][l], P),
                   k_panels(a["xa_w_o"][l], 256)]
        gu = k_panels(a["ffn_w_gu"][l], P)
        stream += [np.stack([gu[:FC], gu[FC:]], 1).reshape(2 * FC, P, W), a["ffn_w_down"][l].reshape(FC, P, W)]
    for l in range(L if STOP > 1 else 0):
        def ffn(n):
            g, u = (k_panels(a[f"ffn{n}_w_{k}_2"][l], P) for k in ("gate", "up"))
            return [np.stack([g, u], 1).reshape(2 * FC, P, W), a[f"ffn{n}_w_down_2"][l].reshape(FC, P, W)]
        stream += ffn(1) + [k_panels(a["w_in_2"][l], P), k_panels(a["w_out_2"][l], P)] + ffn(2)
    stream = np.concatenate(stream, 0)

    par1 = np.stack([np.concatenate(
        [columns(a[n][l]) for n in ("ln_mix_g", "ln_mix_b", "ln_xa_g", "ln_xa_b", "ln_ffn_g", "ln_ffn_b")]
        + [columns(a["b_gate"][l].reshape(-1)), columns(a["b_q_norm"][l]), columns(a["b_kv_norm"][l]),
           np.pad(a["b_forget"][l], (0, P - 8))[:, None]], 1) for l in range(L)], 1)
    par2 = np.stack([np.concatenate(
        [columns(a["b_mod_2"][l]), np.tile(a["q_norm_g_2"][l], 2)[:, None], np.tile(a["k_norm_g_2"][l], 2)[:, None],
         a["hgrn_norm_g_2"][l][:, None]], 1) for l in range(L)], 1)
    wmod = np.concatenate([k_panels(a["w_mod_2"][l], P) for l in range(L)], 0)
    wmod = np.concatenate([wmod, wmod[:2]], 0)
    rev = a["a_rel_bias"][:, :, ::-1]
    win = np.lib.stride_tricks.sliding_window_view(np.pad(rev, ((0, 0), (0, 0), (0, 256))), 256, axis=2)
    rel = np.stack([win[:, :, 1 + 64 * b:65 + 64 * b, :] for b in range(4)], 2)

    arrays = {
        "xT": a["x"][0].T.reshape(DC, P, T).transpose(1, 0, 2),
        "memT": a["mem"][0].T.reshape(DC, P, T).transpose(1, 0, 2),
        "pos": a["positions"].reshape(T),
        "c": columns(a["c_2"][0]),
        "lbl": a["hgrn_lb_logits_2"].reshape(L, 4, P).transpose(2, 0, 1),
        "w": stream, "wmod": wmod, "rel": rel, "par1": par1, "par2": par2, "const": constants()[0], "const2": constants()[1],
    }
    arrays = {n: np.ascontiguousarray(v) for n, v in arrays.items()}
    nc = _bacc.Bacc("TRN2", target_bir_lowering=False, num_devices=1)
    io = {n: nc.dram_tensor(f"in_{n}", v.shape, mybir.dt.from_np(v.dtype), kind="ExternalInput").ap()
          for n, v in arrays.items()}
    io["out"] = nc.dram_tensor("out", (P, DC, T), F32, kind="ExternalOutput").ap()
    build(nc, io, STOP)
    got = _run(nc, [{f"in_{n}": v for n, v in arrays.items()}], core_ids=[0])
    return got.results[0]["out"].transpose(2, 1, 0).reshape(1, T, D)


STOP = 2
```

```python
from contextlib import ExitStack

import numpy as np

import concourse.bass as bass
from concourse import mybir

F32 = mybir.dt.float32
F32R = mybir.dt.float32r
I32 = mybir.dt.int32
ALU = mybir.AluOpType
ACT = mybir.ActivationFunctionType
AX = mybir.AxisListType

P = 128
T = 256
L = 2
D = 1024
DC = D // P
FF = 2816
FC = FF // P
W = 1024
RING = 4
NEG = -1.0e30
ALPHA = (2 * L) ** 0.25

B_COLS, B_UQ, B_UKV, A_QKV, C_QKV = 0, 6, 10, 14, 26
GATE, BRANCH, OUT1, X_KV, X_Q, X_O = 38, 62, 74, 82, 90, 94
GU1, DOWN1, PANELS1 = 98, 142, 164
GU2A, DOWN2A, IN2, OUT2, GU2B, DOWN2B, PANELS2 = 0, 44, 66, 94, 102, 146, 168
GROUPS1, GROUPS2 = PANELS1 // RING, PANELS2 // RING
Q_B, Q_UQ, Q_UKV, Q_A, Q_C, Q_G, Q_BR, Q_OUT, Q_XKV, Q_XQ, Q_XO, Q_GU, PAIRS1 = \
    0, 3, 7, 11, 17, 23, 35, 47, 51, 55, 57, 61, 83
R_GUA, R_IN, R_OUT, R_GUB, PAIRS2 = 0, 22, 36, 40, 62
MOD_CHUNKS = 72
MOD_STEP = 18
HEADS1 = 28
P_MIXG, P_MIXB, P_XAG, P_XAB, P_FFG, P_FFB, P_GATE, P_QN, P_KVN, P_BF, NPAR = \
    0, 8, 16, 24, 32, 40, 48, 72, 75, 77, 78
P2_BMOD, P2_QG, P2_KG, P2_HG, NPAR2 = 0, 72, 73, 74, 75
CONSTS = {}
N_CONST = 0
for _name, _n in (("ident", P), ("ones", P), ("rot32", 32), ("tri", 2 * T), ("chunk_mask", 2 * T),
                  ("causal_mask", 2 * T), ("invf", 1), ("is_f", 1), ("is_one", 1), ("head", 8)):
    CONSTS[_name] = (N_CONST, _n)
    N_CONST += _n
CONSTS2 = {}
N_CONST2 = 0
for _name, _n in (("block64", P), ("rot64", P), ("cos", T), ("sin", T), ("dilated", 2 * T),
                  ("spans", 9 * P), ("levels", 8 * P), ("before", 2 * T), ("suffix", P)):
    CONSTS2[_name] = (N_CONST2, _n)
    N_CONST2 += _n


def build(nc, io, stop_after=9):
    with ExitStack() as ctx:
        def sb(name, shape, dt=F32):
            return ctx.enter_context(nc.sbuf_tensor(name, shape, dt))

        def sem(name):
            return ctx.enter_context(nc.semaphore(name))

        raw = sb("raw", [P, RING, W])
        w_hi = sb("w_hi", [P, RING, W], F32R)
        w_lo = sb("w_lo", [P, RING, W], F32R)
        x = sb("x", [P, DC, T])
        x_hi = sb("x_hi", [P, DC, T], F32R)
        x_lo = sb("x_lo", [P, DC, T], F32R)
        R = sb("R", [P, 44 * T], F32R)
        F = sb("F", [P, 54 * T])
        side = sb("side", [P, 3 * W + MOD_STEP * P])
        mod_raw = side[:, 0:2 * W].rearrange("p (b w) -> p b w", b=2)
        mod_prod = side[:, 2 * W:3 * W].rearrange("p (k m) -> p k m", m=P)
        mod_acc = side[:, 3 * W:3 * W + MOD_STEP * P].rearrange("p (k m) -> p k m", m=P)
        modv = sb("modv", [P, L * MOD_CHUNKS])
        modl = sb("modl", [P, MOD_CHUNKS])
        par2 = sb("par2", [P, NPAR2])
        lbl = sb("lbl", [P, L, 4])
        lb = sb("lb", [P, L, 4])
        lb_t = sb("lb_t", [P, 3, 4])
        lbc = sb("lbc", [P, 2, 4])
        silu_c = sb("silu_c", [P, 8])
        const = sb("const", [P, N_CONST])
        par_all = sb("par_all", [P, L, NPAR])
        par = sb("par", [P, NPAR])
        par2_all = sb("par2_all", [P, L, NPAR2])
        rope_cos = sb("rope_cos", [P, T])
        rope_sin = sb("rope_sin", [P, T])
        mean = sb("mean", [P, T])
        rstd = sb("rstd", [P, 2, T])
        neg_max = sb("neg_max", [P, 2, 2])
        den = sb("den", [P, 2, 2])
        pos_i = mean[:].bitcast(I32)
        ps = ctx.enter_context(nc.psum_tensor("ps", [P, 8, 512], F32))

        def c_(name):
            at, n = CONSTS[name]
            return const[:, at:at + n]

        def c2(name):
            at, n = CONSTS2[name]
            return side[:, at:at + n]

        ident, ones = c_("ident"), c_("ones")

        def f(at, n, width=T):
            return F[:, at:at + n * width].rearrange("p (n w) -> p n w", w=width)

        def r(at, n):
            return R[:, at:at + n * T].rearrange("p (n w) -> p n w", w=T)

        bias = f(0, 2, 512)
        prob = f(1024, 2, 512)
        prob_t = f(2048, 2, 512)
        v_nat = F[:, 3072:4096]
        c_all = f(4096, 6)
        q_b, kv_b, k_b, rot_b = f(5632, 8), f(7680, 8), f(9728, 8), f(11776, 8)
        qk_a, v_a = f(7680, 8), f(11776, 4)
        qk, v_t = f(4096, 8), f(6144, 4)
        fl, fr = f(9728, 8), F[0:16, 13056:13312]
        flog, fabs = F[:, 12800:13056], F[:, 13056:13312]
        fl0, f_nat = F[0:16, 13312:13568], F[:, 13568:13600].rearrange("p (t c) -> p t c", t=2)
        gates, gate_tmp, merged = f(6144, 24), F[:, 1024:1536], f(1536, 8)
        mem = f(4096, 8)
        sq = f(7168, 8)
        sq_b = f(5632, 5)
        ffn_s, ffn_h = f(1024, 2), f(1536, 2)
        br_hi, br_lo = r(0, 12), r(3072, 12)
        mg_hi, mg_lo = r(6144, 8), r(8192, 8)
        cn_hi, cn_lo = r(6144, 5), r(7424, 5)
        mem_hi, mem_lo = r(0, 8), r(3072, 8)
        xo_hi, xo_lo = r(6144, 4), r(7168, 4)
        hid_hi, hid_lo = r(0, FC), r(FC * T, FC)
        mix_hi, mix_lo = r(0, 8), r(2048, 8)
        sq2, normed = f(0, 8), f(11264, 8)
        h_all = f(4096, 28)
        rot_tmp, rs4 = f(11264, 4), f(12288, 4)
        logf, logf_b, o_h = f(4096, 4), f(5120, 4), f(6144, 4)
        v_h, logf_nat = F[:, 11264:12288], F[:, 12288:13312]

        def by_tile(ap):
            return ap.rearrange("p h (k t) -> p k h t", k=2)

        def tiles4(at):
            return F[:, at:at + 1024].rearrange("p (k h t) -> p k h t", k=2, h=4)
        q_h, k_h = by_tile(h_all[:, 12:16, :]), by_tile(h_all[:, 16:20, :])
        h_e, h_qe, h_ke = tiles4(0), tiles4(1024), tiles4(2048)
        scores, cross = tiles4(3072), F[:, 13312:13824]

        raw_in = [sem(f"raw_in{i}") for i in range(RING)]
        hi_done, lo_done = sem("hi_done"), sem("lo_done")
        panel_used = sem("panel_used")
        pair_out = sem("pair_out")
        dma_turn, consts_in, x_in, par_set = sem("dma_turn"), sem("consts_in"), sem("x_in"), sem("par_set")
        init_done = sem("init_done")
        x_split_hi, x_split = sem("x_split_hi"), sem("x_split")
        mod_in = [sem("mod_in0"), sem("mod_in1")]
        mod_mul, mod_sum, mod_taken, mod_out = sem("mod_mul"), sem("mod_sum"), sem("mod_taken"), sem("mod_out")
        pe_turn = sem("pe_turn")
        mod_end = sem("mod_end")
        mod_turn, silu_done = sem("mod_turn"), sem("silu_done")
        rope_dve, rope_act = sem("rope_dve"), sem("rope_act")
        b_dve, b_act, b_pe = sem("b_dve"), sem("b_act"), sem("b_pe")
        c_dve, c_act, c_pe = sem("c_dve"), sem("c_act"), sem("c_pe")
        vt_pe, vt_dve = sem("vt_pe"), sem("vt_dve")
        at_s, at_stt, at_max, at_exp = sem("at_s"), sem("at_stt"), sem("at_max"), sem("at_exp")
        at_rc, at_p, at_t, at_pt = sem("at_rc"), sem("at_p"), sem("at_t"), sem("at_pt")
        at_o, at_oh, at_ol = sem("at_o"), sem("at_oh"), sem("at_ol")
        bias_in = [sem("bias_in0"), sem("bias_in1")]
        mem_in, mem_h, mem_l = sem("mem_in"), sem("mem_h"), sem("mem_l")
        br_dve, mg_h, mg_l = sem("br_dve"), sem("mg_h"), sem("mg_l")
        n_pe, n_dve, n_act = sem("n_pe"), sem("n_dve"), sem("n_act")
        ffn_act, ffn_dve, down_out = sem("ffn_act"), sem("ffn_dve"), sem("down_out")
        out_in = sem("out_in")
        lbl_in, lb_dve, lb_act, consts2_in = sem("lbl_in"), sem("lb_dve"), sem("lb_act"), sem("consts2_in")
        mod_set, gate_done = sem("mod_set"), sem("gate_done")
        rn_pe, rn_dve, rn_act = sem("rn_pe"), sem("rn_dve"), sem("rn_act")
        res2 = sem("res2")
        sb_z, sb_a, sb_d, sb_t, sb_e = sem("sb_z"), sem("sb_a"), sem("sb_d"), sem("sb_t"), sem("sb_e")
        sb_l, sb_w, sb_lw = sem("sb_l"), sem("sb_w"), sem("sb_lw")
        sb_o, sb_oh, sb_ol = sem("sb_o"), sem("sb_oh"), sem("sb_ol")
        dl_pe, dl_act, dl_dve = sem("dl_pe"), sem("dl_act"), sem("dl_dve")
        hg_act, hg_dve, hg_pe = sem("hg_act"), sem("hg_dve"), sem("hg_pe")
        hg_d, hg_exp, hg_qe, hg_ke = sem("hg_d"), sem("hg_exp"), sem("hg_qe"), sem("hg_ke")
        hg_hi, hg_a, lb_c, rn_x = sem("hg_hi"), sem("hg_a"), sem("lb_c"), sem("rn_x")
        hg_s, hg_m = sem("hg_s"), sem("hg_m")

        ND, NA = 17, 6
        BD, BA, BP = 21, 5, 4
        CD, CA, CP = 8, 3, 2
        HG, HA = 21, 9

        block = ctx.enter_context(nc.Block())

        @block.sync
        def _(sp):
            sp.dma_start(x[:], io["xT"]).then_inc(x_in, 16)
            for s in range(RING):
                sp.dma_start(raw[:, s, :], io["w"][s]).then_inc(raw_in[s], 16)
            sp.dma_start(const[:], io["const"]).then_inc(consts_in, 16)
            sp.dma_start(par_all[:], io["par1"]).then_inc(consts_in, 16)
            sp.dma_start(par2_all[:], io["par2"]).then_inc(consts_in, 16)
            sp.dma_start(lbl[:], io["lbl"]).then_inc(lbl_in, 16)
            sp.dma_start(pos_i[64:96, :], io["pos"].partition_broadcast(32)).then_inc(consts_in, 16)
            groups = L * (GROUPS1 + (GROUPS2 if stop_after > 1 else 0))
            with sp.Fori(1, groups) as g:
                for s in range(RING):
                    sp.wait_ge(lo_done, 4 * g + (s - 3))
                    sp.sem_inc(dma_turn, 1)
                    sp.dma_start(raw[:, s, :], io["w"][4 * g + s]).then_inc(raw_in[s], 16)

        @block.gpsimd
        def _(pool):
            pool.wait_ge(silu_done, 1)
            for b in range(2):
                pool.dma_start(mod_raw[:, b, :], io["wmod"][b]).then_inc(mod_in[b], 16)
            c_row = silu_c[:].rearrange("p (k o) -> p k o", o=1).broadcast_to([P, 8, P])
            with pool.Fori(0, L * MOD_CHUNKS // MOD_STEP) as step:
                pool.wait_ge(mod_taken, step + 1)
                pool.sem_inc(mod_turn, 1)
                for j in range(MOD_STEP // 2):
                    for b in range(2):
                        n = step * MOD_STEP + (2 * j + b)
                        pool.wait_ge(mod_in[b], (step * (MOD_STEP // 2) + (j + 1)) * 16)
                        w = mod_raw[:, b, :].rearrange("p (k m) -> p k m", k=8)
                        nc.gpsimd.tensor_tensor(mod_prod[:], w, c_row, ALU.mult).then_inc(mod_mul, 1)
                        pool.wait_ge(mod_mul, 4 * n + 1)
                        nxt = n + 2
                        pool.dma_start(mod_raw[:, b, :], io["wmod"][nxt]).then_inc(mod_in[b], 16)
                        for half in (4, 2, 1):
                            dst = mod_prod[:, 0:half, :] if half > 1 else mod_acc[:, 2 * j + b:2 * j + b + 1, :]
                            ins = nc.gpsimd.tensor_tensor(dst, mod_prod[:, 0:half, :],
                                                          mod_prod[:, half:2 * half, :], ALU.add)
                            ins.then_inc(mod_mul, 1)
                            pool.wait_ge(mod_mul, 4 * n + {4: 2, 2: 3, 1: 4}[half])
                pool.sem_inc(mod_sum, 1)
            for b in range(2):
                pool.wait_ge(mod_in[b], 16 * (L * MOD_CHUNKS // 2 + 1))
            pool.sem_inc(mod_end, 1)
            if stop_after < 2:
                return
            with pool.Fori(0, L) as l:
                for level in range(8):
                    pool.wait_ge(hg_exp, 8 * l + level + 1)
                    pool.wait_ge(hg_s, 9 * l + level + 1)
                    pool.sem_inc(mod_turn, 1)
                    if level < 7:
                        nc.gpsimd.tensor_tensor(h_ke, k_h, h_e, ALU.mult).then_inc(hg_ke, 1)
                    else:
                        nc.gpsimd.tensor_tensor(h_ke[:, 0], k_h[:, 0], h_e[:, 0], ALU.mult).then_inc(hg_ke, 1)

        def feed_hi(act, group, s):
            act.wait_ge(raw_in[s], 16 * group + 16)
            act.wait_ge(panel_used, 4 * group + (s + 1))
            nc.scalar.activation(w_hi[:, s, :], raw[:, s, :], ACT.Copy).then_inc(hi_done, 1)

        def feed_lo(dve, group, s):
            dve.wait_ge(hi_done, 4 * group + (s + 1))
            nc.vector.tensor_tensor(w_lo[:, s, :], raw[:, s, :], w_hi[:, s, :].bitcast(F32),
                                    ALU.subtract).then_inc(lo_done, 1)

        def panels(eng, group0, p0, n, feed, drain, limit):
            def turn(at, i, parts):
                for s in parts:
                    for k in (2, 3):
                        if at + s + k < limit:
                            feed(eng, group0 + i + (at + s + k) // 4, (at + s + k) % 4)
                    drain(group0 + i + (at + s + 1) // 4, (at + s + 1) % 4, 2 * i + (at - p0 + s) // 2, s // 2)
            if n >= 8:
                with eng.Fori(0, n // 4) as i:
                    turn(p0, i, (0, 2))
                if n % 4:
                    turn(p0 + n - n % 4, 0, (0,))
            else:
                for s in range(0, n, 4):
                    turn(p0 + s, 0, (0, 2) if n - s >= 4 else (0,))

        def only_feed(eng, group0, p0, p1, feed):
            n = (p1 - p0) // 4
            with eng.Fori(0, n) as i:
                for s in range(4):
                    feed(eng, group0 + i + (p0 + s) // 4, (p0 + s) % 4)
            for p in range(p0 + 4 * n, p1):
                feed(eng, group0 + p // 4, p % 4)

        def multiply(pe, out, at, m, k, s, rhs_hi, rhs_lo, start, stop, skip=False):
            hi, lo = w_hi[:, s, at:at + m], w_lo[:, s, at:at + m]
            nc.tensor.matmul(out, hi, rhs_hi, start=start, stop=False, skip_group_check=skip)
            nc.tensor.matmul(out, hi, rhs_lo, start=False, stop=False, skip_group_check=skip)
            return nc.tensor.matmul(out, lo, rhs_hi, start=False, stop=stop, skip_group_check=skip)

        def spread(n, slots):
            return [[j for j in range(n) if j * slots // n == t] for t in range(slots)]

        def beside(pe, group0, p0, n, pair0, rhs_hi, rhs_lo, slots):
            plan = spread(n, slots)

            def fill(t):
                for j in plan[t] if t < slots else ():
                    s = (p0 + j) % 4
                    if j == 0:
                        pe.wait_ge(pair_out, pair0 + 2)
                    elif j % 2 == 0:
                        pe.wait_ge(pair_out, pair0 + j // 2 + 1)
                    pe.wait_ge(lo_done, 4 * (group0 + (p0 + j) // 4) + (s + 1))
                    for k in range(DC):
                        ins = multiply(pe, ps[:, j // 2 % 2, j % 2 * T:(j % 2 + 1) * T], k * P, P, k, s,
                                       rhs_hi[:, k, :], rhs_lo[:, k, :], k == 0, k == DC - 1)
                    ins.then_inc(panel_used, 1)
            return fill

        def feed_beside(eng, group0, p0, n, feed, slots, limit):
            plan = spread(n, slots)

            def fill(t):
                for j in plan[t] if t < slots else ():
                    if p0 + j + 2 < limit:
                        feed(eng, group0 + (p0 + j + 2) // 4, (p0 + j + 2) % 4)
            return fill

        def drain_beside(act, group0, p0, n, slots, drain):
            plan = spread(n, slots)

            def fill(t):
                for j in plan[t] if t < slots else ():
                    if j % 2:
                        act.wait_ge(panel_used, 4 * (group0 + (p0 + j) // 4) + ((p0 + j) % 4 + 5))
                        drain(j // 2, ps[:, j // 2 % 2, :].rearrange("p (n w) -> p n w", w=T))
            return fill

        def nothing(t):
            pass

        def project(pe, group0, p0, n, pair0, rhs_hi, rhs_lo, chunks, m=P, per_panel=1):
            pe.wait_ge(pair_out, pair0 + 2)
            pe.sem_inc(pe_turn, 1)

            def panel(at, i, s_at):
                s = at % 4
                pe.wait_ge(lo_done, 4 * (group0 + i + at // 4) + (s + 1))
                for o in range(per_panel):
                    use = (s_at * per_panel + o) // 2
                    half = (s_at * per_panel + o) % 2
                    if half == 0:
                        uses = 2 * per_panel * i + use
                        pe.wait_ge(pair_out, pair0 + uses + 1)
                    out = ps[0:m, use % 2, half * T:(half + 1) * T]
                    for k in range(chunks):
                        ins = multiply(pe, out, (k * per_panel + o) * m, m, k, s, rhs_hi[:, k, :], rhs_lo[:, k, :],
                                       k == 0, k == chunks - 1)
                ins.then_inc(panel_used, 1)
            if n >= 8:
                with pe.Fori(0, n // 4) as i:
                    for s in range(4):
                        panel(p0 + s, i, s)
                for s in range(n % 4):
                    panel(p0 + n - n % 4 + s, 0, s + 4 * (n // 4))
            else:
                for s in range(n):
                    panel(p0 + s, 0, s)

        def down(pe, group0, p0, run):
            pe.wait_ge(ffn_dve, (run + 1) * 2 * FC)
            pe.wait_ge(down_out, 4 * run + 1)

            def panel(at, i, k, start, stop):
                s = at % 4
                pe.wait_ge(lo_done, 4 * (group0 + i + at // 4) + (s + 1))
                for m in range(DC):
                    ins = multiply(pe, ps[:, 4 + m // 2, (m % 2) * T:(m % 2 + 1) * T], m * P, P, k, s,
                                   hid_hi[:, k, :], hid_lo[:, k, :], start and m % 2 == 0, stop, True)
                ins.then_inc(panel_used, 1)
                return ins
            panel(p0, 0, 0, True, False)
            with pe.Fori(0, (FC - 2) // 4) as i:
                for s in range(4):
                    panel(p0 + 1 + s, i, 4 * i + (s + 1), False, False)
            panel(p0 + FC - 1, 0, FC - 1, False, True)

        def pe_attention(pe, head0, n, q, k, extra, v, rows, ready, fill=nothing):
            ready(pe)
            for t in range(n + 2):
                if t < n:
                    pe.wait_ge(at_stt, head0 + t + 1)
                    for tile in range(2):
                        out = ps[:, 2 + t % 2, tile * T:(tile + 1) * T]
                        ins = nc.tensor.matmul(out, q(t, tile), k(t), start=True, stop=extra is None)
                        if extra is not None:
                            ins = nc.tensor.matmul(out, extra[0](t, tile), extra[1], start=False, stop=True)
                    ins.then_inc(at_s, 1)
                fill(t)
                if 1 <= t <= n:
                    h = t - 1
                    pe.wait_ge(at_p, head0 + h + 1)
                    pe.wait_ge(at_pt, head0 + h + 1)
                    for kt in range(2):
                        for tile in range(2):
                            ins = nc.tensor.transpose(
                                ps[:, 4 + h % 2, kt * T + tile * P:kt * T + (tile + 1) * P],
                                prob[:, h % 2, tile * T + kt * P:tile * T + (kt + 1) * P], ident)
                    ins.then_inc(at_t, 1)
                if t >= 2:
                    h = t - 2
                    pe.wait_ge(at_pt, head0 + h + 3)
                    pe.wait_ge(at_ol, head0 + h + 1)
                    for kt in range(2):
                        ins = nc.tensor.matmul(ps[rows(h), 6 + h % 2, 0:T], v(h, kt),
                                               prob_t[:, h % 2, kt * T:(kt + 1) * T], start=kt == 0, stop=kt == 1)
                    ins.then_inc(at_o, 1)

        def act_attention(act, head0, n, rows, out_hi, reverse=False, bias_dma=None, fill=nothing, drain=nothing):
            for t in range(n + 2):
                if t < n:
                    act.wait_ge(at_max, head0 + t + 1)
                    for tile in range(2):
                        s = prob[:, t % 2, tile * T:(tile + 1) * T]
                        ins = nc.scalar.activation(s, s, ACT.Exp, bias=neg_max[:, t % 2, tile:tile + 1],
                                                   accum_out=den[:, t % 2, tile:tile + 1])
                        ins.then_inc(at_exp, 1)
                    if bias_dma is not None and t + 2 < n:
                        bias_dma(act, t + 2)
                fill(t)
                drain(t)
                if 1 <= t <= n:
                    h = t - 1
                    act.wait_ge(at_t, head0 + h + 3)
                    act.wait_ge(at_o, head0 + h + 1)
                    src = ps[:, 4 + h % 2, :].rearrange("p (k q) -> p k q", k=2)
                    if reverse:
                        src = src[:, :, ::-1]
                    nc.scalar.activation(prob_t[:, h % 2, :].rearrange("p (k q) -> p k q", k=2), src,
                                         ACT.Copy).then_inc(at_pt, 1)
                if t >= 2:
                    h = t - 2
                    act.wait_ge(at_o, head0 + h + 3)
                    nc.scalar.activation(out_hi(h)[rows(h), :], ps[rows(h), 6 + h % 2, 0:T],
                                         ACT.Copy).then_inc(at_oh, 1)

        def dve_attention(dve, head0, n, rows, out_hi, out_lo, scale, bias_of, bias_wait=None, fill=nothing):
            for t in range(n + 2):
                if t < n:
                    if bias_wait is not None:
                        bias_wait(dve, t)
                    dve.wait_ge(at_s, head0 + t + 1)
                    dve.wait_ge(at_t, head0 + t + 1)
                    if bias_of is None:
                        nc.vector.tensor_scalar(prob[:, t % 2, :], ps[:, 2 + t % 2, :], scale, None,
                                                ALU.mult).then_inc(at_stt, 1)
                    else:
                        nc.vector.scalar_tensor_tensor(out=prob[:, t % 2, :], in0=ps[:, 2 + t % 2, :], scalar=scale,
                                                       in1=bias_of(t), op0=ALU.mult, op1=ALU.add).then_inc(at_stt, 1)
                    dve.wait_ge(at_stt, head0 + t + 3)
                    nc.vector.tensor_reduce(neg_max[:, t % 2, :], prob[:, t % 2, :].rearrange("p (t k) -> p t k", t=2),
                                            AX.X, ALU.max, negate=True).then_inc(at_max, 1)
                if 1 <= t <= n:
                    h = t - 1
                    dve.wait_ge(at_exp, 2 * (head0 + h) + 2)
                    nc.vector.reciprocal(den[:, h % 2, :], den[:, h % 2, :]).then_inc(at_rc, 1)
                    dve.wait_ge(at_rc, head0 + h + 1)
                    view = prob[:, h % 2, :].rearrange("p (t k) -> p t k", t=2)
                    nc.vector.tensor_tensor(view, view, den[:, h % 2, :].rearrange("p (t o) -> p t o", o=1)
                                            .broadcast_to([P, 2, T]), ALU.mult).then_inc(at_p, 1)
                fill(t)
                if t >= 2:
                    h = t - 2
                    dve.wait_ge(at_oh, head0 + h + 1)
                    nc.vector.tensor_tensor(out_lo(h)[rows(h), :], ps[rows(h), 6 + h % 2, 0:T],
                                            out_hi(h)[rows(h), :].bitcast(F32), ALU.subtract).then_inc(at_ol, 1)

        def pe_turn_v(pe, run, src, chunks=range(4)):
            for tile in range(2):
                for at, c in enumerate(chunks):
                    ins = nc.tensor.transpose(ps[:, 6 + tile, at * P:(at + 1) * P],
                                              src[:, c, tile * P:(tile + 1) * P], ident)
                ins.then_inc(vt_pe, 1)

        def dve_turn_v(dve, run, v_nat=v_nat):
            for tile in range(2):
                dve.wait_ge(vt_pe, 2 * run + (tile + 1))
                nc.vector.tensor_copy(v_nat[:, tile * 512:(tile + 1) * 512], ps[:, 6 + tile, :]).then_inc(vt_dve, 1)

        def even_odd(h):
            return slice(64 * (h % 2), 64 * (h % 2) + 64)

        def whole(h):
            return slice(0, P)

        def pe_sums(pe, of_x, base, sem_in, both=True):
            for q in range(4):
                pe.wait_ge(sem_in, base + q + 1)
                for c in (2 * q, 2 * q + 1):
                    if both:
                        nc.tensor.matmul(ps[:, 2, 0:T], ones, x[:, c, :], start=c == 0, stop=c == DC - 1,
                                         skip_group_check=True)
                    ins = nc.tensor.matmul(ps[:, 2, T:2 * T], ones, of_x[:, c, :], start=not both and c == 0,
                                           stop=c == DC - 1, skip_group_check=True)
            return ins

        def pe_norm(pe, run, between=None):
            pe_sums(pe, sq, run * NA, n_act).then_inc(n_pe, 1)
            if between is not None:
                between()

        def over(v, n):
            return v.rearrange("p (o t) -> p o t", o=1).broadcast_to([P, n, T])

        def dve_norm(dve, run, gain, between=nothing):
            base = run * ND
            dve.wait_ge(n_pe, run + 1)
            nc.vector.tensor_scalar(mean[:], ps[:, 2, 0:T], 1.0 / D, None, ALU.mult).then_inc(n_dve, 1)
            dve.wait_ge(n_dve, base + 1)
            nc.vector.tensor_tensor(rstd[:, 1, :], mean[:], mean[:], ALU.mult).then_inc(n_dve, 1)
            dve.wait_ge(n_dve, base + 2)
            nc.vector.scalar_tensor_tensor(out=rstd[:, 0, :], in0=ps[:, 2, T:2 * T], scalar=1.0 / D,
                                           in1=rstd[:, 1, :], op0=ALU.mult, op1=ALU.subtract).then_inc(n_dve, 1)
            dve.wait_ge(n_dve, base + 3)
            nc.vector.tensor_scalar(rstd[:, 0, :], rstd[:, 0, :], 0.0, 1e-5, ALU.max, ALU.add).then_inc(n_dve, 1)
            nc.vector.tensor_tensor(x[:], x[:], over(mean[:], DC), ALU.subtract).then_inc(n_dve, 1)
            between(0)
            dve.wait_ge(n_act, run * NA + 6)
            dve.wait_ge(n_dve, base + 5)
            for q in range(5):
                if q < 4:
                    pair = x[:, 2 * q:2 * q + 2, :]
                    nc.vector.tensor_tensor(pair, pair, over(rstd[:, 0, :], 2), ALU.mult).then_inc(n_dve, 1)
                    dve.wait_ge(n_dve, base + 3 * q + 6)
                    for c in (2 * q, 2 * q + 1):
                        nc.vector.tensor_scalar(x[:, c, :], x[:, c, :], par[:, gain + c:gain + c + 1],
                                                par[:, gain + DC + c:gain + DC + c + 1], ALU.mult, ALU.add)\
                            .then_inc(n_dve, 1)
                if q:
                    pair = slice(2 * q - 2, 2 * q)
                    dve.wait_ge(x_split_hi, 4 * run + q + 1)
                    nc.vector.tensor_tensor(x_lo[:, pair, :], x[:, pair, :], x_hi[:, pair, :].bitcast(F32),
                                            ALU.subtract).then_inc(x_split, 1)
                between(1 + q)

        def pin(act, name="natural_log_exp_and_others"):
            nc.scalar.preload_act_table_set(name)

        def act_norm(act, run, whole_pair, between=nothing):
            base = run * NA
            pin(act)
            for q in range(4):
                whole_pair(q)
                nc.scalar.activation(sq[:, 2 * q:2 * q + 2, :], x[:, 2 * q:2 * q + 2, :], ACT.Square)\
                    .then_inc(n_act, 1)
            between(0)
            act.wait_ge(n_dve, run * ND + 4)
            nc.scalar.activation(rstd[:, 0, :], rstd[:, 0, :], ACT.Ln).then_inc(n_act, 1)
            act.wait_ge(n_act, base + 5)
            nc.scalar.activation(rstd[:, 0, :], rstd[:, 0, :], ACT.Exp, scale=-0.5).then_inc(n_act, 1)
            between(1)
            for q in range(4):
                pair = slice(2 * q, 2 * q + 2)
                act.wait_ge(n_dve, run * ND + 3 * q + 8)
                nc.scalar.activation(x_hi[:, pair, :], x[:, pair, :], ACT.Copy).then_inc(x_split_hi, 1)
                between(2 + q)

        def act_ffn(act, group0, p0, run, limit):
            def drain(group, s, q, b):
                act.wait_ge(panel_used, 4 * group + (s + 5))
                nc.scalar.activation(ffn_s[:, b, :], ps[:, b, 0:T], ACT.Silu).then_inc(ffn_act, 1)
                act.wait_ge(ffn_dve, 2 * FC * run + 2 * q + 1)
                nc.scalar.activation(hid_hi[:, q, :], ffn_h[:, b, :], ACT.Copy).then_inc(ffn_act, 1)
            nc.scalar.preload_act_table(ACT.Silu)
            panels(act, group0, p0, 2 * FC, feed_hi, drain, limit)

        def dve_ffn(dve, group0, p0, run, pair0, limit):
            def drain(group, s, q, b):
                dve.wait_ge(ffn_act, 2 * FC * run + 2 * q + 1)
                nc.vector.tensor_tensor(ffn_h[:, b, :], ps[:, b, T:2 * T], ffn_s[:, b, :], ALU.mult)\
                    .then_inc(ffn_dve, 1)
                dve.wait_ge(ffn_act, 2 * FC * run + 2 * q + 2)
                nc.vector.tensor_tensor(hid_lo[:, q, :], ffn_h[:, b, :], hid_hi[:, q, :].bitcast(F32), ALU.subtract)\
                    .then_inc(ffn_dve, 1)
                dve.sem_inc(pair_out, 1)
            panels(dve, group0, p0, 2 * FC, feed_lo, drain, limit)

        def chunk_c(c):
            return slice(64 * (c % 2), 64 * (c % 2) + 64)

        def pe_mod(pe, visit):
            pe.wait_ge(mod_sum, visit + 1)
            for j in range(MOD_STEP):
                ins = nc.tensor.matmul(ps[:, 3, j:j + 1], mod_acc[:, j, :], ones[:, 0:1], start=True, stop=True)
            ins.then_inc(mod_taken, 1)

        def dve_mod(dve, visit):
            dve.wait_ge(mod_taken, visit + 2)
            nc.vector.tensor_copy(modv[:, bass.ds(visit * MOD_STEP, MOD_STEP)], ps[:, 3, 0:MOD_STEP])\
                .then_inc(mod_out, 1)

        def f_tile(t, tile):
            return fl[0:16, t, tile * P:(tile + 1) * P]

        @block.tensor
        def _(pe):
            pe.sem_inc(panel_used, RING)
            pe.sem_inc(pair_out, 2)
            pe.sem_inc(mod_taken, 1)
            pe.sem_inc(down_out, 1)
            for s_ in (at_stt, at_pt, at_t, at_o, at_ol):
                pe.sem_inc(s_, 2)
            pe.wait_ge(consts_in, 64)
            with pe.Fori(0, L) as l:
                g0, q0, h0 = l * GROUPS1, l * PAIRS1, l * HEADS1
                pe.wait_ge(x_split, 12 * l + 1)
                project(pe, g0, B_COLS, 6, q0 + Q_B, x_hi, x_lo, DC)
                pe.wait_ge(pair_out, q0 + Q_UQ + 2)
                pe.sem_inc(pe_turn, 1)
                nc.tensor.matmul(ps[64:96, 3, 0:T], c_("rot32")[64:96, :], c_all[64:96, 5, :],
                                 start=True, stop=True).then_inc(b_pe, 1)
                pe.wait_ge(b_act, l * BA + 1)
                for c in range(3):
                    nc.tensor.matmul(ps[:, 2, 0:T], ones, sq_b[:, c, :], start=c == 0, stop=c == 2)
                for c in range(2):
                    ins = nc.tensor.matmul(ps[:, 2, T:2 * T], ones, sq_b[:, 3 + c, :], start=c == 0, stop=c == 1)
                ins.then_inc(b_pe, 1)
                pe.wait_ge(b_dve, l * BD + 11)
                project(pe, g0, B_UQ, 4, q0 + Q_UQ, cn_hi, cn_lo, 3, m=96, per_panel=2)
                project(pe, g0, B_UKV, 4, q0 + Q_UKV, cn_hi[:, 3:5, :], cn_lo[:, 3:5, :], 2, per_panel=2)
                pe.wait_ge(pair_out, q0 + Q_A + 2)
                pe.wait_ge(b_dve, l * BD + 11)
                pe.sem_inc(pe_turn, 1)
                for h in range(0, 8, 2):
                    ins = nc.tensor.matmul(ps[64:96, 2 + h // 2, :], c_("rot32")[64:96, :],
                                           q_b[64:96, h:h + 2, :], start=True, stop=True)
                ins.then_inc(b_pe, 1)
                for tile in range(2):
                    for h in range(8):
                        ins = nc.tensor.transpose(ps[:, 6 + tile, 64 * h:64 * h + 64],
                                                  kv_b[64:128, h, tile * P:(tile + 1) * P], ident[64:128, 64:128])
                ins.then_inc(b_pe, 1)

                def b_ready(pe):
                    pe.wait_ge(b_dve, l * BD + BD)
                pe_attention(pe, h0, 8, lambda h, t: q_b[0:96, h, t * P:(t + 1) * P], lambda h: k_b[0:96, h, :], None,
                             lambda h, kt: v_nat[:, kt * 512 + 64 * h:kt * 512 + 64 * h + 64], even_odd, b_ready,
                             beside(pe, g0, A_QKV, 12, q0 + Q_A, x_hi, x_lo, 10))
                pe.wait_ge(c_dve, l * CD + 3)
                pe.wait_ge(at_stt, h0 + 8 + 2)
                pe.sem_inc(pe_turn, 1)
                for tile in range(2):
                    ins = nc.tensor.transpose(ps[:, 2, 8 * tile:8 * tile + 8], flog[0:8, tile * P:(tile + 1) * P],
                                              ident[0:8, 0:8])
                ins.then_inc(c_pe, 1)
                pe.wait_ge(pair_out, q0 + Q_C + 2)
                pe.wait_ge(at_ol, h0 + 8 + 2)
                pe_turn_v(pe, 3 * l, v_a)
                pe.wait_ge(c_dve, l * CD + 5)
                for tile in range(2):
                    ins = nc.tensor.matmul(ps[0:16, 2, T:2 * T], f_nat[:, tile, :],
                                           c_("tri")[:, tile * T:(tile + 1) * T], start=tile == 0, stop=tile == 1)
                ins.then_inc(c_pe, 1)

                def a_ready(pe):
                    pe.wait_ge(vt_dve, 6 * l + 2)
                    pe.wait_ge(c_dve, l * CD + 7)
                pe_attention(pe, h0 + 8, 8, lambda h, t: qk_a[chunk_c(h), h // 2, t * P:(t + 1) * P],
                             lambda h: qk_a[chunk_c(h), 4 + h // 2, :], None,
                             lambda h, kt: v_nat[:, kt * 512 + 64 * h:kt * 512 + 64 * h + 64], even_odd, a_ready,
                             beside(pe, g0, C_QKV, 12, q0 + Q_C, x_hi, x_lo, 10))
                pe_mod(pe, 4 * l)
                pe.wait_ge(pair_out, q0 + Q_G + 2)
                pe.wait_ge(at_ol, h0 + 16 + 2)
                pe_turn_v(pe, 3 * l + 1, v_t)

                def c_ready(pe):
                    pe.wait_ge(vt_dve, 6 * l + 4)
                    pe.wait_ge(mod_out, 4 * l + 1)
                    pe.wait_ge(c_dve, l * CD + CD)
                pe_attention(pe, h0 + 16, 8, lambda h, t: qk[chunk_c(h), h // 2, t * P:(t + 1) * P],
                             lambda h: qk[chunk_c(h), 4 + h // 2, :], (f_tile, fr),
                             lambda h, kt: v_nat[:, kt * 512 + 64 * h:kt * 512 + 64 * h + 64], even_odd, c_ready,
                             beside(pe, g0, GATE, 12, q0 + Q_G, x_hi, x_lo, 10))
                pe.wait_ge(at_ol, h0 + 24 + 2)
                project(pe, g0, GATE + 12, 12, q0 + Q_G + 6, x_hi, x_lo, DC)
                pe_mod(pe, 4 * l + 1)
                for n in range(3):
                    project(pe, g0, BRANCH + 4 * n, 4, q0 + Q_BR + 4 * n, br_hi[:, 4 * n:4 * n + 4, :],
                            br_lo[:, 4 * n:4 * n + 4, :], 4, per_panel=2)
                pe.wait_ge(mg_l, l + 1)
                project(pe, g0, OUT1, 8, q0 + Q_OUT, mg_hi, mg_lo, DC)
                pe.wait_ge(mem_l, l + 1)
                memory_part = beside(pe, g0, X_KV, 8, q0 + Q_XKV, mem_hi, mem_lo, 8)
                pe_norm(pe, 3 * l, lambda: [memory_part(t) for t in range(8)])
                pe.wait_ge(x_split, 12 * l + 5)
                project(pe, g0, X_Q, 4, q0 + Q_XQ, x_hi, x_lo, DC)
                pe.wait_ge(pair_out, q0 + Q_XO + 2)
                pe_turn_v(pe, 3 * l + 2, v_t)

                def x_ready(pe):
                    pe.wait_ge(vt_dve, 6 * l + 6)
                    pe.wait_ge(mod_out, 4 * l + 2)
                pe_attention(pe, h0 + 24, 4, lambda h, t: qk[:, h, t * P:(t + 1) * P], lambda h: qk[:, 4 + h, :], None,
                             lambda h, kt: v_nat[:, kt * 512 + P * h:kt * 512 + P * h + P], whole, x_ready)
                pe.wait_ge(at_ol, h0 + 28 + 2)
                project(pe, g0, X_O, 4, q0 + Q_XO, xo_hi, xo_lo, 4, per_panel=2)
                pe_norm(pe, 3 * l + 1, lambda: pe_mod(pe, 4 * l + 2))
                pe.wait_ge(x_split, 12 * l + 9)
                project(pe, g0, GU1, 2 * FC, q0 + Q_GU, x_hi, x_lo, DC)
                down(pe, g0, DOWN1, l)
                pe_norm(pe, 3 * l + 2, lambda: pe_mod(pe, 4 * l + 3))

            if stop_after < 2:
                return
            pe.wait_ge(consts2_in, 16)
            pe.sem_inc(hg_s, 1)
            with pe.Fori(0, L) as l:
                g0, q0, h0 = L * GROUPS1 + l * GROUPS2, L * PAIRS1 + l * PAIRS2, L * HEADS1 + 4 * l

                def norm2(k):
                    pe.wait_ge(rn_act, 3 * (3 * l + k) + 1)
                    for c in range(DC):
                        ins = nc.tensor.matmul(ps[:, 2, 0:T], ones, sq2[:, c, :], start=c == 0, stop=c == DC - 1)
                    ins.then_inc(rn_pe, 1)
                    pe.wait_ge(x_split, 12 * L + 1 + 3 * l + k + 1)
                norm2(0)
                project(pe, g0, GU2A, 2 * FC, q0 + R_GUA, x_hi, x_lo, DC)
                down(pe, g0, DOWN2A, L + 2 * l)
                norm2(1)
                project(pe, g0, IN2, 28, q0 + R_IN, x_hi, x_lo, DC)
                pe.wait_ge(pair_out, q0 + R_OUT + 2)
                pe_turn_v(pe, 0, h_all, (4, 5, 10, 11))
                for t in range(6):
                    if t < 4:
                        for kt in range(2):
                            ins = nc.tensor.matmul(ps[:, 2 + t % 2, kt * T:(kt + 1) * T],
                                                   h_all[chunk_c(t), 2 + t // 2, kt * P:(kt + 1) * P],
                                                   h_all[chunk_c(t), t // 2, :], start=True, stop=True)
                        ins.then_inc(sb_z, 1)
                    if 1 <= t <= 4:
                        h = t - 1
                        bank, b = ps[:, 4 + h % 2, :], h % 2
                        pe.wait_ge(sb_l, 4 * l + h + 1)
                        nc.tensor.matmul(bank[:, 0:T], c2("suffix"), prob_t[:, b, 0:T], start=True, stop=False)
                        nc.tensor.matmul(bank[:, 0:T], ones, prob_t[:, b, T:2 * T], start=False, stop=True)
                        nc.tensor.matmul(bank[:, T:2 * T], c2("suffix"), prob_t[:, b, T:2 * T],
                                         start=True, stop=True).then_inc(sb_t, 1)
                    if t >= 2:
                        h = t - 2
                        pe.wait_ge(sb_w, 4 * l + h + 1)
                        if h == 0:
                            pe.wait_ge(vt_dve, 2 * (3 * L + 2 * l) + 2)
                        if h >= 2:
                            pe.wait_ge(sb_ol, 4 * l + h - 1)
                        for kt in range(2):
                            ins = nc.tensor.matmul(ps[even_odd(h), 6 + h % 2, 0:T],
                                                   v_nat[:, kt * 512 + 64 * h:kt * 512 + 64 * h + 64],
                                                   prob[:, h % 2, kt * T:(kt + 1) * T], start=kt == 0, stop=kt == 1)
                        ins.then_inc(sb_o, 1)
                pe.wait_ge(dl_act, 3 * l + 1)
                for n in range(2):
                    ins = nc.tensor.matmul(ps[:, 2 + n, :], c2("block64"), rot_tmp[:, 2 * n:2 * n + 2, :],
                                           start=True, stop=True)
                ins.then_inc(dl_pe, 1)
                pe.wait_ge(dl_dve, 9 * l + 4)
                for n in range(2):
                    ins = nc.tensor.matmul(ps[:, 2 + n, :], c2("rot64"), h_all[:, 6 + 2 * n:8 + 2 * n, :],
                                           start=True, stop=True)
                ins.then_inc(dl_pe, 1)

                def d_ready(pe):
                    pe.wait_ge(dl_dve, 9 * l + 9)
                    pe.wait_ge(sb_ol, 4 * l + 4)
                pe_attention(pe, h0, 4, lambda h, t: h_all[chunk_c(h), 6 + h // 2, t * P:(t + 1) * P],
                             lambda h: h_all[chunk_c(h), 8 + h // 2, :], None,
                             lambda h, kt: v_nat[:, kt * 512 + 256 + 64 * h:kt * 512 + 256 + 64 * h + 64],
                             even_odd, d_ready)
                pe.wait_ge(hg_dve, HG * l + 11)
                pe.wait_ge(at_ol, h0 + 4 + 2)
                for tile in range(2):
                    for h in range(4):
                        ins = nc.tensor.transpose(ps[:, 2 + tile, h * P:(h + 1) * P],
                                                  logf[:, h, tile * P:(tile + 1) * P], ident)
                ins.then_inc(hg_pe, 1)
                pe_turn_v(pe, 0, h_all, (20, 21, 22, 23))
                pe.wait_ge(hg_dve, HG * l + 13)
                pe.wait_ge(vt_dve, 2 * (3 * L + 2 * l) + 4)
                for level in range(9):
                    if level < 8:
                        if level:
                            pe.wait_ge(hg_exp, 8 * l + level)
                        for tile in range(2):
                            span = level if level < 7 else 7 + tile
                            for h in range(4):
                                ins = nc.tensor.matmul(ps[:, 2 + tile, h * P:(h + 1) * P],
                                                       logf_nat[:, tile * 512 + h * P:tile * 512 + (h + 1) * P],
                                                       c2("spans")[:, span * P:(span + 1) * P], start=True, stop=True)
                        ins.then_inc(hg_d, 1)
                        pe.wait_ge(hg_qe, 8 * l + level + 1)
                        pe.wait_ge(hg_ke, 8 * l + level + 1)
                    if level:
                        pe.wait_ge(hg_m, 9 * l + level)
                    if level == 7:
                        for h in range(4):
                            ins = nc.tensor.matmul(ps[:, 4, h * P:(h + 1) * P], h_ke[:, 0, h, :], h_qe[:, 1, h, :],
                                                   start=True, stop=True)
                    else:
                        a, b = (h_ke, h_qe) if level < 8 else (k_h, q_h)
                        for tile in range(2):
                            for h in range(4):
                                ins = nc.tensor.matmul(ps[:, 4 + tile, h * P:(h + 1) * P], a[:, tile, h, :],
                                                       b[:, tile, h, :], start=True, stop=True)
                    ins.then_inc(hg_s, 1)
                pe.wait_ge(hg_m, 9 * l + 9)
                pe.wait_ge(hg_dve, HG * l + 14)
                for h in range(4):
                    out = ps[:, 6 + h // 2, :]
                    at = (h % 2) * T
                    nc.tensor.matmul(out[:, at:at + P], v_h[:, h * P:(h + 1) * P], scores[:, 0, h, :],
                                     start=True, stop=True)
                    nc.tensor.matmul(out[:, at + P:at + T], v_h[:, h * P:(h + 1) * P], cross[:, h * P:(h + 1) * P],
                                     start=True, stop=False)
                    ins = nc.tensor.matmul(out[:, at + P:at + T], v_h[:, 512 + h * P:512 + (h + 1) * P],
                                           scores[:, 1, h, :], start=False, stop=True)
                ins.then_inc(hg_pe, 1)
                pe.wait_ge(hg_act, HA * l + 7)
                for n in range(2):
                    ins = nc.tensor.matmul(ps[:, 2 + n, :], ones, sq2[:, 2 * n:2 * n + 2, :], start=True, stop=True)
                ins.then_inc(hg_pe, 1)
                pe.wait_ge(hg_dve, HG * l + HG)
                project(pe, g0, OUT2, 8, q0 + R_OUT, mix_hi, mix_lo, DC)
                norm2(2)
                project(pe, g0, GU2B, 2 * FC, q0 + R_GUB, x_hi, x_lo, DC)
                down(pe, g0, DOWN2B, L + 2 * l + 1)

        @block.scalar
        def _(act):
            act.dma_start(silu_c[:], io["c"]).then_inc(x_in, 16)
            act.wait_ge(x_in, 32)
            act.wait_ge(consts_in, 64)
            nc.scalar.activation(silu_c[:], silu_c[:], ACT.Silu).then_inc(silu_done, 1)
            nc.scalar.activation(x_hi[:], x[:], ACT.Copy).then_inc(x_split_hi, 1)
            for n in range(2):
                dst = (rope_sin, rope_cos)[n]
                act.wait_ge(rope_dve, 10 * (n + 1))
                nc.scalar.activation(dst[64:96, :], dst[64:96, :], ACT.Sin).then_inc(rope_act, 1)

            with act.Fori(0, L) as l:
                g0, q0, h0 = l * GROUPS1, l * PAIRS1, l * HEADS1
                act.wait_ge(par_set, l + 1)
                for p in range(2):
                    feed_hi(act, g0, p)

                def copy_pair(dst):
                    def drain(group, s, q, b):
                        act.wait_ge(panel_used, 4 * group + (s + 5))
                        nc.scalar.activation(dst(q), ps[:, b, :].rearrange("p (n w) -> p n w", w=T),
                                             ACT.Copy).then_inc(pair_out, 1)
                    return drain

                panels(act, g0, B_COLS, 6, feed_hi, copy_pair(lambda q: c_all[:, 2 * q:2 * q + 2, :]), PANELS1)
                act.wait_ge(pair_out, q0 + Q_UQ + 2)
                nc.scalar.activation(sq_b[:], c_all[:, 0:5, :], ACT.Square).then_inc(b_act, 1)
                act.wait_ge(b_dve, l * BD + 2)
                nc.scalar.activation(rstd[:], rstd[:], ACT.Ln).then_inc(b_act, 1)
                act.wait_ge(b_act, l * BA + 2)
                nc.scalar.activation(rstd[:], rstd[:], ACT.Exp, scale=-0.5).then_inc(b_act, 1)
                act.wait_ge(b_dve, l * BD + 10)
                nc.scalar.activation(cn_hi[:], c_all[:, 0:5, :], ACT.Copy).then_inc(b_act, 1)
                for j in range(4):
                    for p in (2 * j + B_UQ + 2, 2 * j + B_UQ + 3):
                        if p < A_QKV:
                            feed_hi(act, g0 + p // 4, p % 4)
                    for p in (B_UQ + 2 * j, B_UQ + 2 * j + 1):
                        act.wait_ge(panel_used, 4 * g0 + p + 5)
                        b = (p - B_UQ) % 2
                        m, dst = (96, q_b) if p < B_UKV else (P, kv_b)
                        h = 2 * ((p - B_UQ) % 4)
                        nc.scalar.activation(dst[0:m, h:h + 2, :], ps[0:m, b, :].rearrange("p (n w) -> p n w", w=T),
                                             ACT.Copy).then_inc(pair_out, 1)
                act.sem_inc(b_act, 1)
                def keep_a(q, src):
                    dst = qk_a[:, 2 * q:2 * q + 2, :] if q < 4 else v_a[:, 2 * q - 8:2 * q - 6, :]
                    nc.scalar.activation(dst, src[:, :, ::-1] if q < 2 else src, ACT.Copy).then_inc(pair_out, 1)

                def keep_c(q, src):
                    dst = qk[:, 2 * q:2 * q + 2, :] if q < 4 else v_t[:, 2 * q - 8:2 * q - 6, :]
                    nc.scalar.activation(dst, src, ACT.Copy).then_inc(pair_out, 1)

                def keep_gate(q, src):
                    for o in range(2):
                        c = 2 * q + o
                        ins = nc.scalar.activation(gates[:, c, :], src[:, o, :], ACT.Identity,
                                                   bias=par[:, P_GATE + c:P_GATE + c + 1])
                    ins.then_inc(pair_out, 1)

                def feeds(p0, p1):
                    for p in range(p0, p1):
                        feed_hi(act, g0 + p // 4, p % 4)
                pin(act)
                feeds(A_QKV, A_QKV + 2)
                act_attention(act, h0, 8, even_odd, lambda h: br_hi[:, 4 + h // 2, :], False, None,
                              feed_beside(act, g0, A_QKV, 12, feed_hi, 10, PANELS1),
                              drain_beside(act, g0, A_QKV, 12, 10, keep_a))

                def bias_dma(act, h):
                    act.wait_ge(at_stt, h0 + 8 + h + 1)
                    for blk in range(4):
                        rows = slice(64 * (blk % 2), 64 * (blk % 2) + 64)
                        at = (blk // 2) * T
                        n = T - 64 * blk
                        src = io["rel"][l][h, blk, :, 0:n]
                        act.dma_start(bias[rows, h % 2, at:at + n], src).then_inc(bias_in[h % 2], 16)
                act.wait_ge(init_done, 1)
                bias_dma(act, 0)
                bias_dma(act, 1)
                act.wait_ge(c_dve, l * CD + 1)
                nc.scalar.activation(fabs[0:8, :], flog[0:8, :], ACT.Abs).then_inc(c_act, 1)
                act.wait_ge(c_act, l * CA + 1)
                nc.scalar.activation(fabs[0:8, :], fabs[0:8, :], ACT.Exp, scale=-1.0).then_inc(c_act, 1)
                act.wait_ge(c_act, l * CA + 2)
                nc.scalar.activation(fabs[0:8, :], fabs[0:8, :], ACT.Ln, bias=1.0).then_inc(c_act, 1)
                act_attention(act, h0 + 8, 8, even_odd, lambda h: br_hi[:, h // 2, :], True, bias_dma,
                              feed_beside(act, g0, C_QKV, 12, feed_hi, 10, PANELS1),
                              drain_beside(act, g0, C_QKV, 12, 10, keep_c))
                act_attention(act, h0 + 16, 8, even_odd, lambda h: br_hi[:, 8 + h // 2, :], False, None,
                              feed_beside(act, g0, GATE, 12, feed_hi, 10, PANELS1),
                              drain_beside(act, g0, GATE, 12, 10, keep_gate))
                act.dma_start(mem[:], io["memT"]).then_inc(mem_in, 16)
                for q in range(6):
                    feeds(GATE + 12 + 2 * q + 2, GATE + 12 + 2 * q + 4)
                    act.wait_ge(panel_used, 4 * g0 + GATE + 12 + 2 * q + 1 + 5)
                    keep_gate(6 + q, ps[:, q % 2, :].rearrange("p (n w) -> p n w", w=T))
                act.wait_ge(pair_out, q0 + Q_BR + 2)
                nc.scalar.activation(gates[:], gates[:], ACT.Sigmoid).then_inc(gate_done, 1)
                only_feed(act, g0, BRANCH + 2, BRANCH + 12, feed_hi)
                act.wait_ge(mem_in, 16 * l + 16)
                nc.scalar.activation(mem_hi[:], mem[:], ACT.Copy).then_inc(mem_h, 1)
                feeds(OUT1, OUT1 + 2)
                act.wait_ge(br_dve, l * 20 + 20)
                nc.scalar.activation(mg_hi[:], merged[:], ACT.Copy).then_inc(mg_h, 1)
                feeds(OUT1 + 2, X_KV + 2)

                def keep_mem(q, src):
                    dst = qk[:, 4 + 2 * q:6 + 2 * q, :] if q < 2 else v_t[:, 2 * q - 4:2 * q - 2, :]
                    nc.scalar.activation(dst, src, ACT.Copy).then_inc(pair_out, 1)
                mem_feed = feed_beside(act, g0, X_KV, 8, feed_hi, 8, PANELS1)
                mem_drain = drain_beside(act, g0, X_KV, 8, 8, keep_mem)

                def mem_steps(at):
                    for t in ((0, 1), (2, 3), (4,), (5,), (6,), (7,))[at]:
                        mem_feed(t)
                        mem_drain(t)
                act_norm(act, 3 * l, lambda q: act.wait_ge(pair_out, q0 + Q_OUT + q + 3), mem_steps)
                for q in range(2):
                    feeds(X_Q + 2 * q + 2, min(X_Q + 2 * q + 4, X_O))
                    act.wait_ge(panel_used, 4 * g0 + X_Q + 2 * q + 1 + 5)
                    nc.scalar.activation(qk[:, 2 * q:2 * q + 2, :], ps[:, q % 2, :].rearrange("p (n w) -> p n w", w=T),
                                         ACT.Copy).then_inc(pair_out, 1)
                act_attention(act, h0 + 24, 4, whole, lambda h: xo_hi[:, h, :], False, None,
                              feed_beside(act, g0, X_O - 2, 4, feed_hi, 4, PANELS1))
                act_norm(act, 3 * l + 1, lambda q: act.wait_ge(pair_out, q0 + Q_XO + q + 3),
                         lambda at: feeds(GU1 + at, GU1 + at + 1) if at < 2 else None)
                act_ffn(act, g0, GU1, l, PANELS1)
                only_feed(act, g0, DOWN1 + 2, PANELS1, feed_hi)
                act_norm(act, 3 * l + 2, lambda q: act.wait_ge(down_out, 4 * l + q + 2))

            if stop_after == 1:
                act.wait_ge(x_split, 12 * L + 1)
                act.dma_start(io["out"], x[:]).then_inc(out_in, 16)
                act.wait_ge(out_in, 16)
                return
            act.wait_ge(mod_end, 1)
            act.wait_ge(mod_taken, 9)
            act.dma_start(side[:, 0:N_CONST2], io["const2"]).then_inc(consts2_in, 16)
            act.wait_ge(lb_dve, 1)
            nc.scalar.activation(lb_t[:, 0:2, :], lb_t[:, 0:2, :], ACT.Exp).then_inc(lb_act, 1)
            act.wait_ge(consts2_in, 16)
            with act.Fori(0, L) as l:
                g0, q0, h0 = L * GROUPS1 + l * GROUPS2, L * PAIRS1 + l * PAIRS2, L * HEADS1 + 4 * l

                def norm2(k):
                    run = 3 * l + k
                    act.wait_ge(res2, run + 1)
                    nc.scalar.activation(sq2[:], x[:], ACT.Square).then_inc(rn_act, 1)
                    act.wait_ge(rn_dve, 10 * run + 1)
                    nc.scalar.activation(rstd[:, 0, :], rstd[:, 0, :], ACT.Ln).then_inc(rn_act, 1)
                    act.wait_ge(rn_act, 3 * run + 2)
                    nc.scalar.activation(rstd[:, 0, :], rstd[:, 0, :], ACT.Exp, scale=-0.5).then_inc(rn_act, 1)
                    act.wait_ge(rn_dve, 10 * run + 10)
                    nc.scalar.activation(x_hi[:], normed[:], ACT.Copy).then_inc(x_split_hi, 1)

                def feeds(p0, p1):
                    for p in range(p0, p1):
                        feed_hi(act, g0 + p // 4, p % 4)
                feeds(0, 2)
                norm2(0)
                act_ffn(act, g0, GU2A, L + 2 * l, PANELS2)
                only_feed(act, g0, DOWN2A + 2, IN2 + 2, feed_hi)
                norm2(1)

                def keep(group, s, q, b):
                    act.wait_ge(panel_used, 4 * group + (s + 5))
                    nc.scalar.activation(h_all[:, bass.ds(2 * q, 2), :], ps[:, b, :].rearrange("p (n w) -> p n w", w=T),
                                         ACT.Copy).then_inc(pair_out, 1)
                panels(act, g0, IN2, 28, feed_hi, keep, PANELS2)
                for t in range(6):
                    if t < 4:
                        s_, buf = 3 * (4 * l + t), prob_t[:, t % 2, :]
                        act.wait_ge(sb_d, 2 * (4 * l + t) + 1)
                        nc.scalar.activation(buf, prob[:, t % 2, :], ACT.Abs).then_inc(sb_a, 1)
                        act.wait_ge(sb_a, s_ + 1)
                        nc.scalar.activation(buf, buf, ACT.Exp, scale=-1.0).then_inc(sb_a, 1)
                        act.wait_ge(sb_a, s_ + 2)
                        nc.scalar.activation(buf, buf, ACT.Ln, bias=1.0).then_inc(sb_a, 1)
                    if 1 <= t <= 4:
                        h = t - 1
                        act.wait_ge(sb_lw, 4 * l + h + 1)
                        nc.scalar.activation(prob[:, h % 2, :], prob[:, h % 2, :], ACT.Exp).then_inc(sb_e, 1)
                    if t >= 2:
                        h = t - 2
                        act.wait_ge(sb_o, 4 * l + h + 1)
                        nc.scalar.activation(mix_hi[even_odd(h), h // 2, :], ps[even_odd(h), 6 + h % 2, 0:T],
                                             ACT.Copy).then_inc(sb_oh, 1)
                nc.scalar.activation(rot_tmp[:], h_all[:, 6:10, :], ACT.Square).then_inc(dl_act, 1)
                act.wait_ge(dl_dve, 9 * l + 2)
                nc.scalar.activation(rs4[:], rs4[:], ACT.Ln).then_inc(dl_act, 1)
                act.wait_ge(dl_act, 3 * l + 2)
                nc.scalar.activation(rs4[:], rs4[:], ACT.Exp, scale=-0.5).then_inc(dl_act, 1)
                act_attention(act, h0, 4, even_odd, lambda h: mix_hi[:, 2 + h // 2, :])
                ha = HA * l
                nc.scalar.activation(logf[:], h_all[:, 16:20, :], ACT.Sigmoid).then_inc(hg_act, 1)
                act.wait_ge(hg_act, ha + 1)
                nc.scalar.activation(h_all[:, 16:20, :], h_all[:, 16:20, :], ACT.Sigmoid, scale=-1.0)\
                    .then_inc(hg_act, 1)
                nc.scalar.activation(h_all[:, 12:16, :], h_all[:, 12:16, :], ACT.Silu).then_inc(hg_act, 1)
                nc.scalar.activation(h_all[:, 24:28, :], h_all[:, 24:28, :], ACT.Silu).then_inc(hg_act, 1)
                act.wait_ge(hg_dve, HG * l + 10)
                nc.scalar.activation(logf[:], logf[:], ACT.Ln).then_inc(hg_act, 1)
                nc.scalar.activation(logf_b[:], logf_b[:], ACT.Ln).then_inc(hg_act, 1)
                for level in range(8):
                    act.wait_ge(hg_d, 8 * l + level + 1)
                    if level:
                        act.wait_ge(hg_qe, 8 * l + level)
                        act.wait_ge(hg_ke, 8 * l + level)
                    nc.scalar.activation(F[:, 0:1024].rearrange("p (b c) -> p b c", b=2), ps[:, 2:4, :],
                                         ACT.Exp).then_inc(hg_exp, 1)
                act.wait_ge(hg_pe, 3 * l + 2)
                act.wait_ge(hg_ke, 8 * l + 8)
                act.wait_ge(hg_qe, 8 * l + 8)
                nc.scalar.activation(F[:, 0:1024].rearrange("p (b c) -> p b c", b=2), ps[:, 6:8, :],
                                     ACT.Square).then_inc(hg_act, 1)
                act.wait_ge(hg_dve, HG * l + 18)
                nc.scalar.activation(h_qe, h_qe, ACT.Ln).then_inc(hg_act, 1)
                act.wait_ge(hg_act, ha + 8)
                nc.scalar.activation(h_qe, h_qe, ACT.Exp, scale=-0.5).then_inc(hg_act, 1)
                act.wait_ge(hg_dve, HG * l + 20)
                nc.scalar.activation(mix_hi[:, 4:8, :], o_h[:], ACT.Copy).then_inc(hg_hi, 1)
                feeds(OUT2 + 2, GU2B + 2)
                norm2(2)
                act_ffn(act, g0, GU2B, L + 2 * l + 1, PANELS2)
                only_feed(act, g0, DOWN2B + 2, PANELS2, feed_hi)
            act.wait_ge(res2, 3 * L + 1)
            act.dma_start(io["out"], x[:]).then_inc(out_in, 16)
            act.wait_ge(out_in, 16)

        @block.vector
        def _(dve):
            nc.vector.memset(bias[:], NEG).then_inc(init_done, 1)
            dve.wait_ge(x_split_hi, 1)
            nc.vector.tensor_tensor(x_lo[:], x[:], x_hi[:].bitcast(F32), ALU.subtract).then_inc(x_split, 1)
            two_pi = 2.0 * np.pi
            hi = float(np.float32(np.round(two_pi * 256) / 256))
            mid = float(np.float32(np.round((two_pi - hi) * 2 ** 20) / 2 ** 20))
            low = float(np.float32(two_pi - hi - mid))
            magic = 12582912.0
            edge = 3.1415925
            rows = slice(64, 96)
            ang, turns = F[rows, 4096:4352], F[rows, 4352:4608]
            step = 0

            def chain(ins):
                nonlocal step
                ins.then_inc(rope_dve, 1)
                step += 1
                dve.wait_ge(rope_dve, step)
            dve.wait_ge(consts_in, 64)
            for n in range(2):
                out = (rope_sin, rope_cos)[n][rows, :]
                nc.vector.tensor_copy(ang, pos_i[rows, :]).then_inc(rope_dve, 1)
                step += 1
                dve.wait_ge(rope_dve, step)
                chain(nc.vector.tensor_scalar(ang, ang, c_("invf")[rows, :], None, ALU.mult))
                chain(nc.vector.tensor_scalar(turns, ang, 1.0 / two_pi, 0.25 * n, ALU.mult, ALU.add))
                chain(nc.vector.tensor_scalar(turns, turns, magic, None, ALU.add))
                chain(nc.vector.tensor_scalar(turns, turns, -magic, None, ALU.add))
                chain(nc.vector.scalar_tensor_tensor(out=ang, in0=turns, scalar=-hi, in1=ang,
                                                     op0=ALU.mult, op1=ALU.add))
                chain(nc.vector.scalar_tensor_tensor(out=ang, in0=turns, scalar=-mid, in1=ang,
                                                     op0=ALU.mult, op1=ALU.add))
                chain(nc.vector.scalar_tensor_tensor(out=ang, in0=turns, scalar=-low, in1=ang,
                                                     op0=ALU.mult, op1=ALU.add))
                chain(nc.vector.tensor_scalar(out, ang, 0.5 * np.pi * n, edge, ALU.add, ALU.min))
                chain(nc.vector.tensor_scalar(out, out, -edge, None, ALU.max))

            with dve.Fori(0, L) as l:
                g0, q0, h0 = l * GROUPS1, l * PAIRS1, l * HEADS1
                nc.vector.tensor_copy(par[:], par_all[:, l, :]).then_inc(par_set, 1)
                bd = l * BD
                for p in range(2):
                    feed_lo(dve, g0, p)
                for p in range(2, 8):
                    feed_lo(dve, g0 + p // 4, p % 4)
                dve.wait_ge(b_pe, l * BP + 2)
                nc.vector.tensor_scalar(rstd[:, 0, :], ps[:, 2, 0:T], 1.0 / 384, 1e-6, ALU.mult, ALU.add)\
                    .then_inc(b_dve, 1)
                nc.vector.tensor_scalar(rstd[:, 1, :], ps[:, 2, T:2 * T], 1.0 / 256, 1e-6, ALU.mult, ALU.add)\
                    .then_inc(b_dve, 1)
                dve.wait_ge(rope_act, 2)
                dve.wait_ge(pair_out, q0 + Q_UQ + 2)
                turned = rot_b[rows, 0, :]
                nc.vector.tensor_tensor(turned, ps[rows, 3, 0:T], rope_sin[rows, :], ALU.mult).then_inc(b_dve, 1)
                nc.vector.tensor_tensor(c_all[rows, 5, :], c_all[rows, 5, :], rope_cos[rows, :], ALU.mult)\
                    .then_inc(b_dve, 1)
                dve.wait_ge(b_dve, bd + 4)
                nc.vector.tensor_tensor(c_all[rows, 5, :], c_all[rows, 5, :], turned, ALU.add).then_inc(b_dve, 1)
                dve.wait_ge(b_act, l * BA + 3)
                dve.wait_ge(par_set, l + 1)
                for c in range(5):
                    nc.vector.scalar_tensor_tensor(out=c_all[:, c, :], in0=c_all[:, c, :],
                                                   scalar=par[:, P_QN + c:P_QN + c + 1], in1=rstd[:, c // 3, :],
                                                   op0=ALU.mult, op1=ALU.mult).then_inc(b_dve, 1)
                dve.wait_ge(b_act, l * BA + 4)
                nc.vector.tensor_tensor(cn_lo[:], c_all[:, 0:5, :], cn_hi[:].bitcast(F32), ALU.subtract)\
                    .then_inc(b_dve, 1)
                for p in range(8, A_QKV):
                    feed_lo(dve, g0 + p // 4, p % 4)
                dve.wait_ge(b_act, l * BA + 5)
                dve.wait_ge(pair_out, q0 + Q_A + 2)
                dve.wait_ge(b_dve, bd + 5)
                for h in range(8):
                    ins = nc.vector.tensor_copy(k_b[64:96, h, :], c_all[rows, 5, :])
                ins.then_inc(b_dve, 1)
                nc.vector.tensor_copy(k_b[0:64, :, :], kv_b[0:64, :, :]).then_inc(b_dve, 1)
                dve.wait_ge(b_pe, l * BP + 3)
                for h in range(0, 8, 2):
                    ins = nc.vector.tensor_tensor(
                        rot_b[rows, h:h + 2, :], ps[rows, 2 + h // 2, :].rearrange("p (n w) -> p n w", w=T),
                        rope_sin[rows, :].rearrange("p (o t) -> p o t", o=1).broadcast_to([32, 2, T]), ALU.mult)
                    ins.then_inc(b_dve, 1)
                nc.vector.tensor_tensor(q_b[rows, :, :], q_b[rows, :, :],
                                        rope_cos[rows, :].rearrange("p (o t) -> p o t", o=1)
                                        .broadcast_to([32, 8, T]), ALU.mult).then_inc(b_dve, 1)
                dve.wait_ge(b_dve, bd + 18)
                nc.vector.tensor_tensor(q_b[rows, :, :], q_b[rows, :, :], rot_b[rows, :, :], ALU.add)\
                    .then_inc(b_dve, 1)
                dve.wait_ge(b_pe, l * BP + 4)
                for tile in range(2):
                    nc.vector.tensor_copy(v_nat[:, tile * 512:(tile + 1) * 512], ps[:, 6 + tile, :])\
                        .then_inc(b_dve, 1)
                def feeds(p0, p1):
                    for p in range(p0, p1):
                        feed_lo(dve, g0 + p // 4, p % 4)
                feeds(A_QKV, A_QKV + 2)
                dve_attention(dve, h0, 8, even_odd, lambda h: br_hi[:, 4 + h // 2, :],
                              lambda h: br_lo[:, 4 + h // 2, :], 96.0 ** -0.5, lambda t: c_("chunk_mask"), None,
                              feed_beside(dve, g0, A_QKV, 12, feed_lo, 10, PANELS1))
                nc.vector.tensor_scalar(flog[0:8, :], c_all[0:8, 5, :], par[0:8, P_BF:P_BF + 1], None, ALU.add)\
                    .then_inc(c_dve, 1)
                dve.wait_ge(c_act, l * CA + 3)
                dve.wait_ge(c_dve, l * CD + 1)
                nc.vector.tensor_scalar(flog[0:8, :], flog[0:8, :], 0.0, None, ALU.min).then_inc(c_dve, 1)
                dve.wait_ge(c_dve, l * CD + 2)
                nc.vector.tensor_tensor(flog[0:8, :], flog[0:8, :], fabs[0:8, :], ALU.subtract).then_inc(c_dve, 1)
                dve.wait_ge(c_pe, l * CP + 1)
                f_src = ps[:, 2, 0:16].rearrange("p (t c) -> p t c", t=2)
                nc.vector.tensor_scalar(f_nat[:, :, 0:8], f_src, 8.0, None, ALU.mult).then_inc(c_dve, 1)
                nc.vector.tensor_scalar(f_nat[:, :, 8:16], f_src, -8.0, None, ALU.mult).then_inc(c_dve, 1)
                dve_turn_v(dve, 3 * l)
                dve.wait_ge(c_pe, l * CP + 2)
                nc.vector.tensor_scalar(fl0[:], ps[0:16, 2, T:2 * T], c_("is_f")[0:16, :], c_("is_one")[0:16, :],
                                        ALU.mult, ALU.add).then_inc(c_dve, 1)
                nc.vector.tensor_scalar(fr[:], ps[0:16, 2, T:2 * T], c_("is_one")[0:16, :], c_("is_f")[0:16, :],
                                        ALU.mult, ALU.add).then_inc(c_dve, 1)

                def bias_wait(dve, h):
                    dve.wait_ge(bias_in[h % 2], 64 * (4 * l + h // 2 + 1))
                dve_attention(dve, h0 + 8, 8, even_odd, lambda h: br_hi[:, h // 2, :],
                              lambda h: br_lo[:, h // 2, :], 0.125, lambda h: bias[:, h % 2, :], bias_wait,
                              feed_beside(dve, g0, C_QKV, 12, feed_lo, 10, PANELS1))
                dve_mod(dve, 4 * l)
                dve.wait_ge(c_dve, l * CD + 7)
                nc.vector.tensor_tensor(fl[0:16, :, :], fl0[:].rearrange("p (o t) -> p o t", o=1)
                                        .broadcast_to([16, 8, T]),
                                        c_("head")[0:16, :].rearrange("p (h o) -> p h o", o=1)
                                        .broadcast_to([16, 8, T]), ALU.mult).then_inc(c_dve, 1)
                dve_turn_v(dve, 3 * l + 1)
                dve_attention(dve, h0 + 16, 8, even_odd, lambda h: br_hi[:, 8 + h // 2, :],
                              lambda h: br_lo[:, 8 + h // 2, :], 0.125, lambda t: c_("causal_mask"), None,
                              feed_beside(dve, g0, GATE, 12, feed_lo, 10, PANELS1))
                feeds(GATE + 14, BRANCH + 2)
                dve_mod(dve, 4 * l + 1)
                step = 0
                for j in range(12):
                    p = BRANCH + j + 2
                    feeds(p, p + 1)
                    n, c = j // 4, 2 * (j % 4)
                    dve.wait_ge(panel_used, 4 * g0 + BRANCH + j + 5)
                    dve.wait_ge(gate_done, l + 1)
                    gate = gates[:, 8 * n + c:8 * n + c + 2, :]
                    src = ps[:, j % 2, :].rearrange("p (n w) -> p n w", w=T)
                    tmp = gate_tmp.rearrange("p (n w) -> p n w", w=T)
                    dst = merged[:, c:c + 2, :] if n == 0 else tmp
                    nc.vector.tensor_tensor(dst, src, gate, ALU.mult).then_inc(br_dve, 1)
                    step += 1
                    dve.wait_ge(br_dve, l * 20 + step)
                    dve.sem_inc(pair_out, 1)
                    if n:
                        nc.vector.tensor_tensor(merged[:, c:c + 2, :], merged[:, c:c + 2, :], tmp, ALU.add)\
                            .then_inc(br_dve, 1)
                        step += 1
                        dve.wait_ge(br_dve, l * 20 + step)
                    if j == 5:
                        dve.wait_ge(mem_h, l + 1)
                        nc.vector.tensor_tensor(mem_lo[:], mem[:], mem_hi[:].bitcast(F32), ALU.subtract)\
                            .then_inc(mem_l, 1)
                dve.wait_ge(mg_h, l + 1)
                nc.vector.tensor_tensor(mg_lo[:], merged[:], mg_hi[:].bitcast(F32), ALU.subtract).then_inc(mg_l, 1)

                def residual(p0, n_pairs, per_panel):
                    for q in range(n_pairs):
                        last = p0 + (2 * q + 1 if per_panel == 1 else q)
                        dve.wait_ge(panel_used, 4 * g0 + last + 5)
                        dst = x[:, 2 * q:2 * q + 2, :]
                        nc.vector.scalar_tensor_tensor(out=dst, in0=dst, scalar=ALPHA,
                                                       in1=ps[:, q % 2, :].rearrange("p (n w) -> p n w", w=T),
                                                       op0=ALU.mult, op1=ALU.add).then_inc(pair_out, 1)
                        if per_panel == 1:
                            feeds(last + 3, min(last + 5, p0 + 10))
                feeds(OUT1 + 2, OUT1 + 4)
                residual(OUT1, 4, 1)
                mem_feed = feed_beside(dve, g0, X_KV, 8, feed_lo, 8, PANELS1)
                dve_norm(dve, 3 * l, P_MIXG,
                         lambda at: [mem_feed(t) for t in ((0, 1), (2,), (3,), (4,), (5,), (6, 7))[at]])
                feeds(X_Q + 2, X_O)
                dve_turn_v(dve, 3 * l + 2)
                dve_attention(dve, h0 + 24, 4, whole, lambda h: xo_hi[:, h, :], lambda h: xo_lo[:, h, :],
                              128.0 ** -0.5, None, None, feed_beside(dve, g0, X_O - 2, 4, feed_lo, 4, PANELS1))
                residual(X_O, 4, 2)
                dve_norm(dve, 3 * l + 1, P_XAG, lambda at: feeds(GU1 + at, GU1 + at + 1) if at < 2 else None)
                dve_mod(dve, 4 * l + 2)
                dve_ffn(dve, g0, GU1, l, q0 + Q_GU, PANELS1)
                only_feed(dve, g0, DOWN1 + 2, PANELS1, feed_lo)
                dve.wait_ge(panel_used, 4 * g0 + PANELS1 + 4)
                for q in range(4):
                    dst = x[:, 2 * q:2 * q + 2, :]
                    nc.vector.scalar_tensor_tensor(out=dst, in0=dst, scalar=ALPHA,
                                                   in1=ps[:, 4 + q, :].rearrange("p (n w) -> p n w", w=T),
                                                   op0=ALU.mult, op1=ALU.add).then_inc(down_out, 1)
                dve_norm(dve, 3 * l + 2, P_FFG)
                dve_mod(dve, 4 * l + 3)

            if stop_after < 2:
                return
            dve.wait_ge(lbl_in, 16)
            nc.vector.tensor_tensor(lb_t[:, 2, :], lbl[:, 0, :], lbl[:, 1, :], ALU.max).then_inc(lb_c, 1)
            dve.wait_ge(lb_c, 1)
            nc.vector.tensor_tensor(lb_t[:, 0:2, :], lbl[:], lb_t[:, 2:3, :].broadcast_to([P, 2, 4]),
                                    ALU.subtract).then_inc(lb_dve, 1)
            dve.wait_ge(lb_act, 1)
            nc.vector.tensor_tensor(lb_t[:, 2, :], lb_t[:, 0, :], lb_t[:, 1, :], ALU.add).then_inc(lb_c, 1)
            dve.wait_ge(lb_c, 2)
            nc.vector.reciprocal(lb_t[:, 2, :], lb_t[:, 2, :]).then_inc(lb_c, 1)
            dve.wait_ge(lb_c, 3)
            nc.vector.tensor_tensor(lb_t[:, 0:2, :], lb_t[:, 0:2, :], lb_t[:, 2:3, :].broadcast_to([P, 2, 4]),
                                    ALU.mult).then_inc(lb_c, 1)
            dve.wait_ge(lb_c, 4)
            nc.vector.tensor_tensor(lb[:, 0, :], lb_t[:, 0, :], lb_t[:, 0, :], ALU.subtract).then_inc(lb_c, 1)
            nc.vector.tensor_tensor(lb_t[:, 2, :], lb_t[:, 0, :], lb_t[:, 1, :], ALU.add).then_inc(lb_c, 1)
            dve.wait_ge(lb_c, 6)
            nc.vector.tensor_tensor(lb[:, 1, :], lb_t[:, 2, :], lb_t[:, 0, :], ALU.subtract).then_inc(lb_c, 1)
            dve.wait_ge(lb_c, 7)
            nc.vector.tensor_scalar(lb[:], lb[:], 0.0, 1.0 - 1e-6, ALU.max, ALU.min).then_inc(lb_c, 1)
            dve.wait_ge(lb_c, 8)
            dve.wait_ge(mod_out, 8)
            dve.wait_ge(consts2_in, 16)
            nc.vector.tensor_copy(lb_t[:], lb_t[:]).then_inc(res2, 1)
            with dve.Fori(0, L) as l:
                g0, q0, h0 = L * GROUPS1 + l * GROUPS2, L * PAIRS1 + l * PAIRS2, L * HEADS1 + 4 * l
                nc.vector.tensor_copy(par2[:], par2_all[:, l, :]).then_inc(mod_set, 1)
                nc.vector.tensor_tensor(modl[:], modv[:, bass.ds(l * MOD_CHUNKS, MOD_CHUNKS)],
                                        par2_all[:, l, 0:MOD_CHUNKS], ALU.add).then_inc(mod_set, 1)
                nc.vector.tensor_copy(lbc[:, 0, :], lb[:, l, :]).then_inc(mod_set, 1)
                dve.wait_ge(mod_set, 10 * l + 3)
                nc.vector.tensor_scalar(lbc[:, 1, :], lbc[:, 0, :], 1e-30, None, ALU.max).then_inc(mod_set, 1)
                dve.wait_ge(mod_set, 10 * l + 4)
                nc.vector.tensor_scalar(lbc[:, 0, :], lbc[:, 0, :], -1.0, 1.0, ALU.mult, ALU.add).then_inc(mod_set, 1)
                for at in (8, 32, 56):
                    nc.vector.tensor_scalar(modl[:, at:at + 8], modl[:, at:at + 8], 1.0, None, ALU.add)\
                        .then_inc(mod_set, 1)
                for at in (16, 64):
                    nc.vector.tensor_scalar(modl[:, at:at + 8], modl[:, at:at + 8], 0.5, None, ALU.mult)\
                        .then_inc(mod_set, 1)
                dve.wait_ge(mod_set, 10 * l + 10)

                def norm2(k):
                    run = 3 * l + k
                    dve.wait_ge(rn_pe, run + 1)
                    nc.vector.tensor_scalar(rstd[:, 0, :], ps[:, 2, 0:T], 1.0 / D, 1e-6, ALU.mult, ALU.add)\
                        .then_inc(rn_dve, 1)
                    dve.wait_ge(rn_act, 3 * run + 3)
                    nc.vector.tensor_tensor(normed[:], x[:], over(rstd[:, 0, :], DC), ALU.mult).then_inc(rn_dve, 1)
                    dve.wait_ge(rn_dve, 10 * run + 2)
                    for c in range(DC):
                        at = 24 * k + c
                        nc.vector.tensor_scalar(normed[:, c, :], normed[:, c, :], modl[:, at + 8:at + 9],
                                                modl[:, at:at + 1], ALU.mult, ALU.add).then_inc(rn_dve, 1)
                    dve.wait_ge(x_split_hi, 12 * L + 1 + run + 1)
                    nc.vector.tensor_tensor(x_lo[:], normed[:], x_hi[:].bitcast(F32), ALU.subtract)\
                        .then_inc(x_split, 1)

                def feeds(p0, p1):
                    for p in range(p0, p1):
                        feed_lo(dve, g0 + p // 4, p % 4)

                def add_down(end, k):
                    dve.wait_ge(panel_used, 4 * g0 + end + 4)
                    for c in range(DC):
                        at = 24 * k + 16 + c
                        ins = nc.vector.scalar_tensor_tensor(
                            out=x[:, c, :], in0=ps[:, 4 + c // 2, (c % 2) * T:(c % 2 + 1) * T],
                            scalar=modl[:, at:at + 1], in1=x[:, c, :], op0=ALU.mult, op1=ALU.add)
                        ins.then_inc(down_out if c % 2 else rn_x, 1)
                    dve.wait_ge(down_out, 4 * (L + 2 * l + k // 2) + 5)
                    dve.sem_inc(res2, 1)
                feeds(0, 2)
                norm2(0)
                dve_ffn(dve, g0, GU2A, L + 2 * l, q0 + R_GUA, PANELS2)
                only_feed(dve, g0, DOWN2A + 2, IN2 + 2, feed_lo)
                add_down(IN2, 0)
                norm2(1)
                feeds(IN2 + 2, IN2 + 30)
                dve_turn_v(dve, 3 * L + 2 * l)
                for t in range(6):
                    if t < 4:
                        h, b = 4 * l + t, t % 2
                        dve.wait_ge(sb_z, h + 1)
                        if t >= 2:
                            dve.wait_ge(sb_o, h - 1)
                        nc.vector.tensor_scalar(prob[:, b, :], ps[:, 2 + b, :], 0.125, None, ALU.mult)\
                            .then_inc(sb_d, 1)
                        dve.wait_ge(sb_a, 3 * h + 3)
                        dve.wait_ge(sb_d, 2 * h + 1)
                        nc.vector.scalar_tensor_tensor(out=prob_t[:, b, :], in0=prob[:, b, :], scalar=0.0,
                                                       in1=prob_t[:, b, :], op0=ALU.max, op1=ALU.add)\
                            .then_inc(sb_d, 1)
                        dve.wait_ge(sb_d, 2 * h + 2)
                        nc.vector.scalar_tensor_tensor(out=prob_t[:, b, :], in0=prob_t[:, b, :], scalar=-1.0,
                                                       in1=c2("before"), op0=ALU.mult, op1=ALU.mult)\
                            .then_inc(sb_l, 1)
                    if 1 <= t <= 4:
                        h, b = 4 * l + t - 1, (t - 1) % 2
                        dve.wait_ge(sb_t, h + 1)
                        nc.vector.tensor_tensor(prob[:, b, :], prob[:, b, :], ps[:, 4 + b, :], ALU.add)\
                            .then_inc(sb_lw, 1)
                        dve.wait_ge(sb_e, h + 1)
                        nc.vector.scalar_tensor_tensor(out=prob[:, b, :], in0=prob[:, b, :], scalar=1.0,
                                                       in1=c2("before"), op0=ALU.min, op1=ALU.mult)\
                            .then_inc(sb_w, 1)
                    if t >= 2:
                        h = t - 2
                        dve.wait_ge(sb_oh, 4 * l + h + 1)
                        nc.vector.tensor_tensor(mix_lo[even_odd(h), h // 2, :], ps[even_odd(h), 6 + h % 2, 0:T],
                                                mix_hi[even_odd(h), h // 2, :].bitcast(F32), ALU.subtract)\
                            .then_inc(sb_ol, 1)
                dd = 9 * l
                dve.wait_ge(dl_pe, 2 * l + 1)
                for n in range(2):
                    nc.vector.tensor_scalar(rs4[:, 2 * n:2 * n + 2, :], ps[:, 2 + n, :]
                                            .rearrange("p (n w) -> p n w", w=T), 1.0 / 64, 1e-6, ALU.mult, ALU.add)\
                        .then_inc(dl_dve, 1)
                dve.wait_ge(dl_act, 3 * l + 3)
                for n in range(2):
                    v = h_all[:, 6 + 2 * n:8 + 2 * n, :]
                    nc.vector.scalar_tensor_tensor(out=v, in0=v, scalar=par2[:, P2_QG + n:P2_QG + n + 1],
                                                   in1=rs4[:, 2 * n:2 * n + 2, :], op0=ALU.mult, op1=ALU.mult)\
                        .then_inc(dl_dve, 1)
                dve.wait_ge(dl_pe, 2 * l + 2)
                for n in range(2):
                    nc.vector.tensor_tensor(rot_tmp[:, 2 * n:2 * n + 2, :],
                                            ps[:, 2 + n, :].rearrange("p (n w) -> p n w", w=T),
                                            over(c2("sin"), 2), ALU.mult).then_inc(dl_dve, 1)
                v = h_all[:, 6:10, :]
                nc.vector.tensor_tensor(v, v, over(c2("cos"), 4), ALU.mult).then_inc(dl_dve, 1)
                dve.wait_ge(dl_dve, dd + 7)
                nc.vector.tensor_tensor(v, v, rot_tmp[:], ALU.add).then_inc(dl_dve, 1)
                dve.wait_ge(dl_dve, dd + 8)
                dve.sem_inc(dl_dve, 1)
                dve_attention(dve, h0, 4, even_odd, lambda h: mix_hi[:, 2 + h // 2, :],
                              lambda h: mix_lo[:, 2 + h // 2, :], 0.125, lambda t: c2("dilated"))
                hd = HG * l
                dve.wait_ge(hg_act, HA * l + 4)
                for c in range(4):
                    nc.vector.tensor_scalar(logf[:, c, :], logf[:, c, :], lbc[:, 0, c:c + 1], lbc[:, 1, c:c + 1],
                                            ALU.mult, ALU.add).then_inc(hg_dve, 1)
                    nc.vector.tensor_scalar(h_all[:, 16 + c, :], h_all[:, 16 + c, :], lbc[:, 0, c:c + 1], None,
                                            ALU.mult).then_inc(hg_dve, 1)
                dve.wait_ge(hg_dve, hd + 8)
                nc.vector.tensor_scalar(logf_b[:], logf[:], 2.0 ** 50, 1.0, ALU.mult, ALU.min).then_inc(hg_dve, 1)
                dve.wait_ge(hg_dve, hd + 9)
                nc.vector.tensor_scalar(logf[:], logf[:], 2.0 ** -50, None, ALU.max).then_inc(hg_dve, 1)
                dve.wait_ge(hg_act, HA * l + 6)
                nc.vector.tensor_tensor(logf[:], logf[:], logf_b[:], ALU.add).then_inc(hg_dve, 1)
                dve.wait_ge(hg_pe, 3 * l + 1)
                for tile in range(2):
                    nc.vector.tensor_copy(logf_nat[:, tile * 512:(tile + 1) * 512], ps[:, 2 + tile, :])\
                        .then_inc(hg_dve, 1)
                dve_turn_v(dve, 3 * L + 2 * l + 1, v_h)
                for level in range(9):
                    if level < 8:
                        dve.wait_ge(hg_exp, 8 * l + level + 1)
                        dst, a, b = (h_qe, q_h, h_e) if level < 7 else (h_qe[:, 1], q_h[:, 1], h_e[:, 1])
                        nc.vector.tensor_tensor(dst, a, b, ALU.mult).then_inc(hg_qe, 1)
                    dve.wait_ge(hg_s, 9 * l + level + 2)
                    if level == 7:
                        nc.vector.tensor_copy(cross, ps[:, 4, :]).then_inc(hg_m, 1)
                        continue
                    at = level if level < 7 else 7
                    mask = c2("levels")[:, at * P:(at + 1) * P].rearrange("p (o t) -> p o t", o=1)
                    src = ps[:, 4:6, :].rearrange("p k (h t) -> p (k h) t", h=4)
                    flat = (lambda v: v.rearrange("p k h t -> p (k h) t"))
                    dst = scores if level == 0 else h_qe
                    nc.vector.tensor_tensor(flat(dst), src, mask.broadcast_to([P, 8, P]), ALU.mult).then_inc(hg_m, 1)
                    dve.wait_ge(hg_m, 9 * l + level + 1)
                    if level:
                        ins = nc.vector.tensor_tensor(flat(scores), flat(scores), flat(h_qe), ALU.add)
                        ins.then_inc(hg_a if level < 8 else hg_dve, 1)
                        if level < 8:
                            dve.wait_ge(hg_a, 6 * l + level)
                dve.wait_ge(hg_act, HA * l + 7)
                for n in range(2):
                    nc.vector.tensor_copy(o_h[:, 2 * n:2 * n + 2, :],
                                          ps[:, 6 + n, :].rearrange("p (n w) -> p n w", w=T)).then_inc(hg_dve, 1)
                dve.wait_ge(hg_pe, 3 * l + 3)
                for n in range(2):
                    nc.vector.tensor_scalar(F[:, 1024 + 512 * n:1536 + 512 * n], ps[:, 2 + n, :], 1.0 / P, 1e-6,
                                            ALU.mult, ALU.add).then_inc(hg_dve, 1)
                dve.wait_ge(hg_act, HA * l + 9)
                nc.vector.scalar_tensor_tensor(out=o_h[:], in0=o_h[:], scalar=par2[:, P2_HG:P2_HG + 1],
                                               in1=f(1024, 4), op0=ALU.mult, op1=ALU.mult).then_inc(hg_dve, 1)
                dve.wait_ge(hg_dve, hd + 19)
                nc.vector.tensor_tensor(o_h[:], o_h[:], h_all[:, 24:28, :], ALU.mult).then_inc(hg_dve, 1)
                dve.wait_ge(hg_hi, l + 1)
                nc.vector.tensor_tensor(mix_lo[:, 4:8, :], o_h[:], mix_hi[:, 4:8, :].bitcast(F32), ALU.subtract)\
                    .then_inc(hg_dve, 1)
                feeds(OUT2 + 2, OUT2 + 4)
                for q in range(4):
                    dve.wait_ge(panel_used, 4 * g0 + OUT2 + 2 * q + 1 + 5)
                    for c in (2 * q, 2 * q + 1):
                        ins = nc.vector.scalar_tensor_tensor(
                            out=x[:, c, :], in0=ps[:, q % 2, (c % 2) * T:(c % 2 + 1) * T],
                            scalar=modl[:, 40 + c:41 + c], in1=x[:, c, :], op0=ALU.mult, op1=ALU.add)
                        ins.then_inc(pair_out if c % 2 else rn_x, 1)
                    feeds(OUT2 + 2 * q + 4, min(OUT2 + 2 * q + 6, GU2B + 2))
                dve.wait_ge(pair_out, q0 + R_GUB + 2)
                dve.sem_inc(res2, 1)
                norm2(2)
                dve_ffn(dve, g0, GU2B, L + 2 * l + 1, q0 + R_GUB, PANELS2)
                only_feed(dve, g0, DOWN2B + 2, PANELS2, feed_lo)
                add_down(PANELS2, 2)


def constants():
    c = {}
    i = np.arange(P)
    t = np.arange(T)
    c["ident"] = np.eye(P)
    c["ones"] = np.ones((P, P))
    rot32 = np.zeros((P, 32))
    for m in range(16):
        rot32[64 + m + 16, m] = -1.0
        rot32[64 + m, m + 16] = 1.0
    c["rot32"] = rot32

    def tiles(a):
        return a.reshape(2, P, -1).transpose(1, 0, 2).reshape(P, -1)
    c["tri"] = tiles((t[:, None] <= t[None, :]).astype(np.float32))
    c["chunk_mask"] = tiles(np.where(t[None, :] // 64 <= t[:, None] // 64, 0.0, NEG))
    c["causal_mask"] = tiles(np.where(t[None, :] <= t[:, None], 0.0, NEG))
    invf = np.zeros((P, 1), np.float32)
    invf[64:96, 0] = np.tile(np.float32(10000.0) ** (-np.arange(16, dtype=np.float32) / np.float32(16)), 2)
    c["invf"] = invf
    c["is_f"] = (i < 8)[:, None] * 1.0
    c["is_one"] = ((i >= 8) & (i < 16))[:, None] * 1.0
    c["head"] = (i[:, None] % 8 == np.arange(8)[None, :]) * 1.0
    c["block64"] = (i[:, None] // 64 == i[None, :] // 64) * 1.0
    rot64 = np.zeros((P, P))
    for b in (0, 64):
        for m in range(32):
            rot64[b + m + 32, b + m] = -1.0
            rot64[b + m, b + m + 32] = 1.0
    c["rot64"] = rot64
    f64 = np.float32(10000.0) ** (-np.arange(32, dtype=np.float32) * np.float32(2.0) / np.float32(64))
    ang = t.astype(np.float32)[None, :] * np.tile(f64, 4)[:, None]
    c["cos"], c["sin"] = np.cos(ang), np.sin(ang)
    dist = t[:, None] - t[None, :]
    count = sum(((dist >= 0) & (dist % s == 0) & (dist // s <= P)).astype(int) for s in (1, 4, 16))
    c["dilated"] = tiles(np.where(count > 0, np.log(np.maximum(count, 1)), NEG))
    spans, levels = [], []
    for h in (1, 2, 4, 8, 16, 32, 64):
        base = i // (2 * h) * (2 * h)
        u, b, s = i[:, None], base[None, :], i[None, :]
        right = (s - b) >= h
        spans.append(np.where(right, (u >= b + h) & (u <= s), (u > s) & (u < b + h)) * 1.0)
        same = base[:, None] == base[None, :]
        levels.append((same & ((i - base)[:, None] < h) & ((i - base)[None, :] >= h)) * 1.0)
    spans.append((i[:, None] > i[None, :]) * 1.0)
    spans.append((i[:, None] <= i[None, :]) * 1.0)
    levels.append(np.eye(P))
    c["spans"], c["levels"] = np.concatenate(spans, 1), np.concatenate(levels, 1)
    c["before"] = tiles((t[:, None] < t[None, :]) * 1.0)
    c["suffix"] = (i[:, None] >= i[None, :]) * 1.0
    return [np.concatenate([np.asarray(c[n], np.float32).reshape(P, w) for n, (_, w) in which.items()], 1)
            for which in (CONSTS, CONSTS2)]


def k_panels(w, cols):
    k, n = w.shape
    a = w.reshape(k // P, P, n // cols, cols).transpose(2, 1, 0, 3).reshape(n // cols, P, -1)
    if a.shape[2] < W:
        a = np.pad(a, ((0, 0), (0, 0), (0, W - a.shape[2])))
    return a


def columns(v):
    return v.reshape(-1, P).T


def kernel(**inputs):
    import concourse.bacc as _bacc
    from concourse.bass_utils import run_bass_kernel_spmd as _run

    a = {n: np.asarray(v) for n, v in inputs.items()}
    stream = []
    for l in range(L):
        w_in = a["w_in"][l]
        b = w_in[:, 1536:2208]
        c_at, f_at, g_at = 2208, 3744, 3752
        z = np.zeros((D, 56), np.float32)
        odd = np.concatenate([w_in[:, f_at:f_at + 8], z, b[:, 640:672], z[:, :32]], 1)
        stream += [k_panels(np.concatenate([b[:, :640], odd], 1), P),
                   k_panels(a["b_w_uq"][l], 192), k_panels(a["b_w_ukv"][l], 256),
                   k_panels(w_in[:, :1536], P), k_panels(w_in[:, c_at:c_at + 1536], P),
                   k_panels(w_in[:, g_at:], P)]
        stream += [k_panels(a["w_branch"][l, n], 256) for n in range(3)]
        stream += [k_panels(a["w_mix_out"][l], P), k_panels(a["xa_w_kv"][l], P), k_panels(a["xa_w_q"][l], P),
                   k_panels(a["xa_w_o"][l], 256)]
        gu = k_panels(a["ffn_w_gu"][l], P)
        stream += [np.stack([gu[:FC], gu[FC:]], 1).reshape(2 * FC, P, W), a["ffn_w_down"][l].reshape(FC, P, W)]
    for l in range(L if STOP > 1 else 0):
        def ffn(n):
            g, u = (k_panels(a[f"ffn{n}_w_{k}_2"][l], P) for k in ("gate", "up"))
            return [np.stack([g, u], 1).reshape(2 * FC, P, W), a[f"ffn{n}_w_down_2"][l].reshape(FC, P, W)]
        stream += ffn(1) + [k_panels(a["w_in_2"][l], P), k_panels(a["w_out_2"][l], P)] + ffn(2)
    stream = np.concatenate(stream, 0)

    par1 = np.stack([np.concatenate(
        [columns(a[n][l]) for n in ("ln_mix_g", "ln_mix_b", "ln_xa_g", "ln_xa_b", "ln_ffn_g", "ln_ffn_b")]
        + [columns(a["b_gate"][l].reshape(-1)), columns(a["b_q_norm"][l]), columns(a["b_kv_norm"][l]),
           np.pad(a["b_forget"][l], (0, P - 8))[:, None]], 1) for l in range(L)], 1)
    par2 = np.stack([np.concatenate(
        [columns(a["b_mod_2"][l]), np.tile(a["q_norm_g_2"][l], 2)[:, None], np.tile(a["k_norm_g_2"][l], 2)[:, None],
         a["hgrn_norm_g_2"][l][:, None]], 1) for l in range(L)], 1)
    wmod = np.concatenate([k_panels(a["w_mod_2"][l], P) for l in range(L)], 0)
    wmod = np.concatenate([wmod, wmod[:2]], 0)
    rev = a["a_rel_bias"][:, :, ::-1]
    win = np.lib.stride_tricks.sliding_window_view(np.pad(rev, ((0, 0), (0, 0), (0, 256))), 256, axis=2)
    rel = np.stack([win[:, :, 1 + 64 * b:65 + 64 * b, :] for b in range(4)], 2)

    arrays = {
        "xT": a["x"][0].T.reshape(DC, P, T).transpose(1, 0, 2),
        "memT": a["mem"][0].T.reshape(DC, P, T).transpose(1, 0, 2),
        "pos": a["positions"].reshape(T),
        "c": columns(a["c_2"][0]),
        "lbl": a["hgrn_lb_logits_2"].reshape(L, 4, P).transpose(2, 0, 1),
        "w": stream, "wmod": wmod, "rel": rel, "par1": par1, "par2": par2, "const": constants()[0], "const2": constants()[1],
    }
    arrays = {n: np.ascontiguousarray(v) for n, v in arrays.items()}
    nc = _bacc.Bacc("TRN2", target_bir_lowering=False, num_devices=1)
    io = {n: nc.dram_tensor(f"in_{n}", v.shape, mybir.dt.from_np(v.dtype), kind="ExternalInput").ap()
          for n, v in arrays.items()}
    io["out"] = nc.dram_tensor("out", (P, DC, T), F32, kind="ExternalOutput").ap()
    build(nc, io, STOP)
    got = _run(nc, [{f"in_{n}": v for n, v in arrays.items()}], core_ids=[0])
    return got.results[0]["out"].transpose(2, 1, 0).reshape(1, T, D)


STOP = 2
```

```python
from contextlib import ExitStack

import numpy as np

import concourse.bass as bass
from concourse import mybir

F32 = mybir.dt.float32
F32R = mybir.dt.float32r
I32 = mybir.dt.int32
ALU = mybir.AluOpType
ACT = mybir.ActivationFunctionType
AX = mybir.AxisListType

P = 128
T = 256
L = 2
D = 1024
DC = D // P
FF = 2816
FC = FF // P
W = 1024
RING = 4
NEG = -1.0e30
ALPHA = (2 * L) ** 0.25

B_COLS, A_Q, B_UQ, B_UKV, A_KV, C_QKV = 0, 6, 10, 14, 18, 26
GATE, BRANCH, OUT1, X_KV, X_Q, X_O = 38, 62, 74, 82, 90, 94
GU1, DOWN1, PANELS1 = 98, 142, 164
GU2A, DOWN2A, IN2, OUT2, GU2B, DOWN2B, PANELS2 = 0, 44, 66, 94, 102, 146, 168
GROUPS1, GROUPS2 = PANELS1 // RING, PANELS2 // RING
Q_B, Q_AQ, Q_UQ, Q_UKV, Q_A, Q_C, Q_G, Q_BR, Q_OUT, Q_XKV, Q_XQ, Q_XO, Q_GU, PAIRS1 = \
    0, 3, 5, 9, 13, 17, 23, 35, 47, 51, 55, 57, 61, 83
R_GUA, R_IN, R_OUT, R_GUB, PAIRS2 = 0, 22, 36, 40, 62
IN2_PARTS = ((12, 6, 6), (18, 2, 2), (20, 4, 6), (24, 4, 4))
MOD_CHUNKS = 72
MOD_STEP = 18
HEADS1 = 28
P_MIXG, P_MIXB, P_XAG, P_XAB, P_FFG, P_FFB, P_GATE, P_QN, P_KVN, P_BF, NPAR = \
    0, 8, 16, 24, 32, 40, 48, 72, 75, 77, 78
P2_BMOD, P2_QG, P2_KG, P2_HG, NPAR2 = 0, 72, 73, 74, 75
CONSTS = {}
N_CONST = 0
for _name, _n in (("ident", P), ("ones", P), ("rot32", 32), ("tri", 2 * T), ("chunk_mask", 2 * T),
                  ("causal_mask", 2 * T), ("invf", 1), ("is_f", 1), ("is_one", 1), ("head", 8)):
    CONSTS[_name] = (N_CONST, _n)
    N_CONST += _n
CONSTS2 = {}
N_CONST2 = 0
for _name, _n in (("block64", P), ("rot64", P), ("cos", T), ("sin", T), ("dilated", 2 * T),
                  ("spans", 9 * P), ("levels", 8 * P), ("before", 2 * T), ("suffix", P)):
    CONSTS2[_name] = (N_CONST2, _n)
    N_CONST2 += _n


def build(nc, io):
    with ExitStack() as ctx:
        def sb(name, shape, dt=F32):
            return ctx.enter_context(nc.sbuf_tensor(name, shape, dt))

        def sem(name):
            return ctx.enter_context(nc.semaphore(name))

        raw = sb("raw", [P, RING, W])
        w_hi = sb("w_hi", [P, RING, W], F32R)
        w_lo = sb("w_lo", [P, RING, W], F32R)
        x = sb("x", [P, DC, T])
        x_hi = sb("x_hi", [P, DC, T], F32R)
        x_lo = sb("x_lo", [P, DC, T], F32R)
        R = sb("R", [P, 44 * T], F32R)
        F = sb("F", [P, 54 * T])
        side = sb("side", [P, 3 * W + MOD_STEP * P])
        mod_raw = side[:, 0:2 * W].rearrange("p (b w) -> p b w", b=2)
        mod_prod = side[:, 2 * W:3 * W].rearrange("p (k m) -> p k m", m=P)
        mod_acc = side[:, 3 * W:3 * W + MOD_STEP * P].rearrange("p (k m) -> p k m", m=P)
        modv = sb("modv", [P, L * MOD_CHUNKS])
        modl = sb("modl", [P, MOD_CHUNKS])
        par2 = sb("par2", [P, NPAR2])
        lbl = sb("lbl", [P, L, 4])
        lb = sb("lb", [P, L, 4])
        lb_t = sb("lb_t", [P, 3, 4])
        lbc = sb("lbc", [P, 2, 4])
        silu_c = sb("silu_c", [P, 8])
        const = sb("const", [P, N_CONST])
        par_all = sb("par_all", [P, L, NPAR])
        par = sb("par", [P, NPAR])
        par2_all = sb("par2_all", [P, L, NPAR2])
        rope_cos = sb("rope_cos", [P, T])
        rope_sin = sb("rope_sin", [P, T])
        mean = sb("mean", [P, T])
        rstd = sb("rstd", [P, 2, T])
        neg_max = sb("neg_max", [P, 2, 2])
        den = sb("den", [P, 2, 2])
        pos_i = mean[:].bitcast(I32)
        ps = ctx.enter_context(nc.psum_tensor("ps", [P, 8, 512], F32))

        def c_(name):
            at, n = CONSTS[name]
            return const[:, at:at + n]

        def c2(name):
            at, n = CONSTS2[name]
            return side[:, at:at + n]

        ident, ones = c_("ident"), c_("ones")

        def f(at, n, width=T):
            return F[:, at:at + n * width].rearrange("p (n w) -> p n w", w=width)

        def r(at, n):
            return R[:, at:at + n * T].rearrange("p (n w) -> p n w", w=T)

        bias = f(0, 2, 512)
        prob = f(1024, 2, 512)
        prob_t = f(2048, 2, 512)
        v_nat = F[:, 3072:4096]
        c_all = f(4096, 6)
        q_b, kv_b, rot_b = f(5632, 8), f(9728, 8), f(11776, 8)
        qk_a, v_a = f(7680, 8), f(11776, 4)
        qk, v_t = f(4096, 8), f(6144, 4)
        fl, fr = f(9728, 8), F[0:16, 13056:13312]
        flog, fabs = F[:, 12800:13056], F[:, 13056:13312]
        fl0, f_nat = F[0:16, 13312:13568], F[:, 13568:13600].rearrange("p (t c) -> p t c", t=2)
        gates, gate_tmp, merged = f(6144, 24), F[:, 1024:1536], f(1536, 8)
        mem = f(4096, 8)
        sq = f(7168, 8)
        sq_b = f(5632, 5)
        ffn_s, ffn_h = f(1024, 2), f(1536, 2)
        br_hi, br_lo = r(0, 12), r(3072, 12)
        mg_hi, mg_lo = r(6144, 8), r(8192, 8)
        cn_hi, cn_lo = r(6144, 5), r(7424, 5)
        mem_hi, mem_lo = r(0, 8), r(3072, 8)
        xo_hi, xo_lo = r(6144, 4), r(7168, 4)
        hid_hi, hid_lo = r(0, FC), r(FC * T, FC)
        mix_hi, mix_lo = r(0, 8), r(2048, 8)
        sq2, normed = f(0, 8), f(11264, 8)
        h_all = f(4096, 28)
        rot_tmp, rs4 = f(11264, 4), f(12288, 4)
        logf, logf_b, o_h = f(4096, 4), f(5120, 4), f(6144, 4)
        v_h, logf_nat = F[:, 11264:12288], F[:, 12288:13312]

        def by_tile(ap):
            return ap.rearrange("p h (k t) -> p k h t", k=2)

        def tiles4(at):
            return F[:, at:at + 1024].rearrange("p (k h t) -> p k h t", k=2, h=4)
        q_h, k_h = by_tile(h_all[:, 12:16, :]), by_tile(h_all[:, 16:20, :])
        h_e, h_qe, h_ke = ([tiles4(at), tiles4(4096 + at)] for at in (0, 1024, 2048))
        scores, cross = tiles4(3072), F[:, 13312:13824]

        raw_in = [sem(f"raw_in{i}") for i in range(RING)]
        hi_done, lo_done = sem("hi_done"), sem("lo_done")
        panel_used = sem("panel_used")
        pair_out = sem("pair_out")
        dma_turn, consts_in, c_in, par_set = sem("dma_turn"), sem("consts_in"), sem("c_in"), sem("par_set")
        x_in = [sem(f"x_in{q}") for q in range(4)]
        init_done = sem("init_done")
        x_split_hi, x_split = sem("x_split_hi"), sem("x_split")
        mod_in = [sem("mod_in0"), sem("mod_in1")]
        mod_mul, mod_sum, mod_taken, mod_out = sem("mod_mul"), sem("mod_sum"), sem("mod_taken"), sem("mod_out")
        pe_turn = sem("pe_turn")
        mod_end = sem("mod_end")
        mod_turn, silu_done = sem("mod_turn"), sem("silu_done")
        rope_dve, rope_act = sem("rope_dve"), sem("rope_act")
        b_dve, b_act, b_pe, b_v, b_key = sem("b_dve"), sem("b_act"), sem("b_pe"), sem("b_v"), sem("b_key")
        c_dve, c_act, c_pe = sem("c_dve"), sem("c_act"), sem("c_pe")
        vt_pe, vt_dve = sem("vt_pe"), sem("vt_dve")
        at_s, at_stt, at_max, at_exp = sem("at_s"), sem("at_stt"), sem("at_max"), sem("at_exp")
        at_rc, at_p, at_t, at_pt = sem("at_rc"), sem("at_p"), sem("at_t"), sem("at_pt")
        at_o, at_oh, at_ol = sem("at_o"), sem("at_oh"), sem("at_ol")
        bias_in = [sem("bias_in0"), sem("bias_in1")]
        mem_in, mem_h, mem_l = sem("mem_in"), sem("mem_h"), sem("mem_l")
        br_dve, mg_h, mg_l = sem("br_dve"), sem("mg_h"), sem("mg_l")
        n_pe, n_dve, n_act = sem("n_pe"), sem("n_dve"), sem("n_act")
        ffn_act, ffn_dve, down_out = sem("ffn_act"), sem("ffn_dve"), sem("down_out")
        out_in = sem("out_in")
        lbl_in, lb_dve, lb_act, consts2_in = sem("lbl_in"), sem("lb_dve"), sem("lb_act"), sem("consts2_in")
        mod_set, gate_done = sem("mod_set"), sem("gate_done")
        rn_pe, rn_dve, rn_act = sem("rn_pe"), sem("rn_dve"), sem("rn_act")
        res2 = sem("res2")
        sb_z, sb_a, sb_d, sb_t, sb_e = sem("sb_z"), sem("sb_a"), sem("sb_d"), sem("sb_t"), sem("sb_e")
        sb_l, sb_w, sb_lw = sem("sb_l"), sem("sb_w"), sem("sb_lw")
        sb_o, sb_oh, sb_ol = sem("sb_o"), sem("sb_oh"), sem("sb_ol")
        dl_pe, dl_act, dl_dve = sem("dl_pe"), sem("dl_act"), sem("dl_dve")
        hg_act, hg_dve, hg_pe = sem("hg_act"), sem("hg_dve"), sem("hg_pe")
        hg_d, hg_exp, hg_qe, hg_ke = sem("hg_d"), sem("hg_exp"), sem("hg_qe"), sem("hg_ke")
        hg_hi, hg_a, lb_c, rn_x = sem("hg_hi"), sem("hg_a"), sem("lb_c"), sem("rn_x")
        hg_s, hg_m = sem("hg_s"), sem("hg_m")

        ND, NA = 17, 6
        BD, BA, BP = 23, 5, 4
        CD, CA, CP = 8, 3, 2
        HG, HA = 21, 9

        block = ctx.enter_context(nc.Block())

        @block.sync
        def _(sp):
            for q in range(4):
                sp.dma_start(x[:, 2 * q:2 * q + 2, :], io["xT"][:, 2 * q:2 * q + 2, :]).then_inc(x_in[q], 16)
                sp.dma_start(raw[:, q, :], io["w"][q]).then_inc(raw_in[q], 16)
            sp.dma_start(const[:], io["const"]).then_inc(consts_in, 16)
            sp.dma_start(par_all[:], io["par1"]).then_inc(consts_in, 16)
            sp.dma_start(par2_all[:], io["par2"]).then_inc(consts_in, 16)
            sp.dma_start(lbl[:], io["lbl"]).then_inc(lbl_in, 16)
            sp.dma_start(pos_i[64:96, :], io["pos"].partition_broadcast(32)).then_inc(consts_in, 16)
            groups = L * (GROUPS1 + GROUPS2) + 1
            with sp.Fori(1, groups) as g:
                for s in range(RING):
                    sp.wait_ge(lo_done, 4 * g + (s - 3))
                    sp.sem_inc(dma_turn, 1)
                    sp.dma_start(raw[:, s, :], io["w"][4 * g + s]).then_inc(raw_in[s], 16)
            for s in range(RING):
                sp.wait_ge(raw_in[s], 16 * groups)

        @block.gpsimd
        def _(pool):
            pool.wait_ge(silu_done, 1)
            for b in range(2):
                pool.dma_start(mod_raw[:, b, :], io["wmod"][b]).then_inc(mod_in[b], 16)
            c_row = silu_c[:].rearrange("p (k o) -> p k o", o=1).broadcast_to([P, 8, P])
            with pool.Fori(0, L * MOD_CHUNKS // MOD_STEP) as step:
                pool.wait_ge(mod_taken, step + 1)
                pool.sem_inc(mod_turn, 1)
                for j in range(MOD_STEP // 2):
                    for b in range(2):
                        n = step * MOD_STEP + (2 * j + b)
                        pool.wait_ge(mod_in[b], (step * (MOD_STEP // 2) + (j + 1)) * 16)
                        w = mod_raw[:, b, :].rearrange("p (k m) -> p k m", k=8)
                        nc.gpsimd.tensor_tensor(mod_prod[:], w, c_row, ALU.mult).then_inc(mod_mul, 1)
                        pool.wait_ge(mod_mul, 4 * n + 1)
                        nxt = n + 2
                        pool.dma_start(mod_raw[:, b, :], io["wmod"][nxt]).then_inc(mod_in[b], 16)
                        for half in (4, 2, 1):
                            dst = mod_prod[:, 0:half, :] if half > 1 else mod_acc[:, 2 * j + b:2 * j + b + 1, :]
                            ins = nc.gpsimd.tensor_tensor(dst, mod_prod[:, 0:half, :],
                                                          mod_prod[:, half:2 * half, :], ALU.add)
                            ins.then_inc(mod_mul, 1)
                            pool.wait_ge(mod_mul, 4 * n + {4: 2, 2: 3, 1: 4}[half])
                pool.sem_inc(mod_sum, 1)
            for b in range(2):
                pool.wait_ge(mod_in[b], 16 * (L * MOD_CHUNKS // 2 + 1))
            pool.sem_inc(mod_end, 1)
            with pool.Fori(0, L) as l:
                for level in range(8):
                    pool.wait_ge(hg_exp, 8 * l + level + 1)
                    pool.wait_ge(hg_s, 9 * l + max(level, 1))
                    pool.sem_inc(mod_turn, 1)
                    b, at = level % 2, slice(0, 2) if level < 7 else slice(0, 1)
                    nc.gpsimd.tensor_tensor(h_ke[b][:, at], k_h[:, at], h_e[b][:, at], ALU.mult).then_inc(hg_ke, 1)

        def feed_hi(act, group, s):
            act.wait_ge(raw_in[s], 16 * group + 16)
            act.wait_ge(panel_used, 4 * group + (s + 1))
            nc.scalar.activation(w_hi[:, s, :], raw[:, s, :], ACT.Copy).then_inc(hi_done, 1)

        def feed_lo(dve, group, s):
            dve.wait_ge(hi_done, 4 * group + (s + 1))
            nc.vector.tensor_tensor(w_lo[:, s, :], raw[:, s, :], w_hi[:, s, :].bitcast(F32),
                                    ALU.subtract).then_inc(lo_done, 1)

        def panels(eng, group0, p0, n, feed, drain, limit):
            def turn(at, i, parts):
                for s in parts:
                    for k in (2, 3):
                        if at + s + k < limit:
                            feed(eng, group0 + i + (at + s + k) // 4, (at + s + k) % 4)
                    drain(group0 + i + (at + s + 1) // 4, (at + s + 1) % 4, 2 * i + (at - p0 + s) // 2, s // 2)
            if n >= 8:
                with eng.Fori(0, n // 4) as i:
                    turn(p0, i, (0, 2))
                if n % 4:
                    turn(p0 + n - n % 4, 0, (0,))
            else:
                for s in range(0, n, 4):
                    turn(p0 + s, 0, (0, 2) if n - s >= 4 else (0,))

        def only_feed(eng, group0, p0, p1, feed):
            n = (p1 - p0) // 4
            with eng.Fori(0, n) as i:
                for s in range(4):
                    feed(eng, group0 + i + (p0 + s) // 4, (p0 + s) % 4)
            for p in range(p0 + 4 * n, p1):
                feed(eng, group0 + p // 4, p % 4)

        def multiply(pe, out, at, m, k, s, rhs_hi, rhs_lo, start, stop, skip=False):
            hi, lo = w_hi[:, s, at:at + m], w_lo[:, s, at:at + m]
            nc.tensor.matmul(out, hi, rhs_hi, start=start, stop=False, skip_group_check=skip)
            nc.tensor.matmul(out, hi, rhs_lo, start=False, stop=False, skip_group_check=skip)
            return nc.tensor.matmul(out, lo, rhs_hi, start=False, stop=stop, skip_group_check=skip)

        def spread(n, slots):
            return [[j for j in range(n) if j * slots // n == t] for t in range(slots)]

        def beside(pe, group0, p0, n, pair0, rhs_hi, rhs_lo, slots):
            plan = spread(n, slots)

            def fill(t):
                for j in plan[t] if t < slots else ():
                    s = (p0 + j) % 4
                    if j == 0:
                        pe.wait_ge(pair_out, pair0 + 2)
                    elif j % 2 == 0:
                        pe.wait_ge(pair_out, pair0 + j // 2 + 1)
                    pe.wait_ge(lo_done, 4 * (group0 + (p0 + j) // 4) + (s + 1))
                    for k in range(DC):
                        ins = multiply(pe, ps[:, j // 2 % 2, j % 2 * T:(j % 2 + 1) * T], k * P, P, k, s,
                                       rhs_hi[:, k, :], rhs_lo[:, k, :], k == 0, k == DC - 1)
                    ins.then_inc(panel_used, 1)
            return fill

        def feed_beside(eng, group0, p0, n, feed, slots, limit):
            plan = spread(n, slots)

            def fill(t):
                for j in plan[t] if t < slots else ():
                    if p0 + j + 2 < limit:
                        feed(eng, group0 + (p0 + j + 2) // 4, (p0 + j + 2) % 4)
            return fill

        def drain_beside(act, group0, p0, n, slots, drain):
            plan = spread(n, slots)

            def fill(t):
                for j in plan[t] if t < slots else ():
                    if j % 2:
                        act.wait_ge(panel_used, 4 * (group0 + (p0 + j) // 4) + ((p0 + j) % 4 + 5))
                        drain(j // 2, ps[:, j // 2 % 2, :].rearrange("p (n w) -> p n w", w=T))
            return fill

        def nothing(t):
            pass

        def first_pair(pe, group0, p0, pair0, rhs_hi, rhs_lo, split_by, split0):
            pe.wait_ge(pair_out, pair0 + 2)
            for p in (p0, p0 + 1):
                pe.wait_ge(lo_done, 4 * (group0 + p // 4) + (p % 4 + 1))
            for k in range(DC):
                if k % 2 == 0:
                    pe.wait_ge(split_by, split0 + k // 2 + 1)
                for half in range(2):
                    ins = multiply(pe, ps[:, 0, half * T:(half + 1) * T], k * P, P, k, (p0 + half) % 4,
                                   rhs_hi[:, k, :], rhs_lo[:, k, :], k == 0 and half == 0, k == DC - 1, True)
                    if k == DC - 1:
                        ins.then_inc(panel_used, 1)

        def project(pe, group0, p0, n, pair0, rhs_hi, rhs_lo, chunks, m=P, per_panel=1, split0=None, split_by=x_split, done=0):
            if split0 is not None:
                first_pair(pe, group0, p0, pair0, rhs_hi, rhs_lo, split_by, split0)
                done = 2
            elif not done:
                pe.wait_ge(pair_out, pair0 + 2)
                pe.sem_inc(pe_turn, 1)

            def panel(at, i, s_at):
                s = at % 4
                pe.wait_ge(lo_done, 4 * (group0 + i + at // 4) + (s + 1))
                for o in range(per_panel):
                    use = (s_at * per_panel + o) // 2
                    half = (s_at * per_panel + o) % 2
                    if half == 0:
                        uses = 2 * per_panel * i + use
                        pe.wait_ge(pair_out, pair0 + uses + 1)
                    out = ps[0:m, use % 2, half * T:(half + 1) * T]
                    for k in range(chunks):
                        ins = multiply(pe, out, (k * per_panel + o) * m, m, k, s, rhs_hi[:, k, :], rhs_lo[:, k, :],
                                       k == 0, k == chunks - 1)
                ins.then_inc(panel_used, 1)
            loops = (n - done) // 4 if n >= 8 else 0
            if loops:
                with pe.Fori(0, loops) as i:
                    for s in range(done, done + 4):
                        panel(p0 + s, i, s)
            for s in range(done + 4 * loops, n):
                panel(p0 + s, 0, s)

        def down(pe, group0, p0, run):
            pe.wait_ge(ffn_dve, run * 2 * FC + 2 * FC - 2)
            pe.wait_ge(down_out, 4 * run + 1)

            def panel(at, i, k, start, stop):
                s = at % 4
                pe.wait_ge(lo_done, 4 * (group0 + i + at // 4) + (s + 1))
                for m in range(DC):
                    ins = multiply(pe, ps[:, 4 + m // 2, (m % 2) * T:(m % 2 + 1) * T], m * P, P, k, s,
                                   hid_hi[:, k, :], hid_lo[:, k, :], start and m % 2 == 0, stop, True)
                ins.then_inc(panel_used, 1)
                return ins
            panel(p0, 0, 0, True, False)
            with pe.Fori(0, (FC - 2) // 4) as i:
                for s in range(4):
                    panel(p0 + 1 + s, i, 4 * i + (s + 1), False, False)
            pe.wait_ge(ffn_dve, run * 2 * FC + 2 * FC)
            panel(p0 + FC - 1, 0, FC - 1, False, True)

        def pe_attention(pe, head0, n, q, k, extra, v, rows, ready, fill=nothing):
            ready(pe)
            for t in range(n + 2):
                if t < n:
                    pe.wait_ge(at_stt, head0 + t + 1)
                    for tile in range(2):
                        out = ps[:, 2 + t % 2, tile * T:(tile + 1) * T]
                        ins = nc.tensor.matmul(out, q(t, tile), k(t), start=True, stop=extra is None)
                        if extra is not None:
                            ins = nc.tensor.matmul(out, extra[0](t, tile), extra[1], start=False, stop=True)
                    ins.then_inc(at_s, 1)
                fill(t)
                if 1 <= t <= n:
                    h = t - 1
                    pe.wait_ge(at_p, head0 + h + 1)
                    pe.wait_ge(at_pt, head0 + h + 1)
                    for kt in range(2):
                        for tile in range(2):
                            ins = nc.tensor.transpose(
                                ps[:, 4 + h % 2, kt * T + tile * P:kt * T + (tile + 1) * P],
                                prob[:, h % 2, tile * T + kt * P:tile * T + (kt + 1) * P], ident)
                    ins.then_inc(at_t, 1)
                if t >= 2:
                    h = t - 2
                    pe.wait_ge(at_pt, head0 + h + 3)
                    pe.wait_ge(at_ol, head0 + h + 1)
                    for kt in range(2):
                        ins = nc.tensor.matmul(ps[rows(h), 6 + h % 2, 0:T], v(h, kt),
                                               prob_t[:, h % 2, kt * T:(kt + 1) * T], start=kt == 0, stop=kt == 1)
                    ins.then_inc(at_o, 1)

        def act_attention(act, head0, n, rows, out_hi, reverse=False, bias_dma=None, fill=nothing, drain=nothing):
            for t in range(n + 2):
                if t < n:
                    act.wait_ge(at_max, head0 + t + 1)
                    for tile in range(2):
                        s = prob[:, t % 2, tile * T:(tile + 1) * T]
                        ins = nc.scalar.activation(s, s, ACT.Exp, bias=neg_max[:, t % 2, tile:tile + 1],
                                                   accum_out=den[:, t % 2, tile:tile + 1])
                        ins.then_inc(at_exp, 1)
                    if bias_dma is not None and t + 2 < n:
                        bias_dma(act, t + 2)
                fill(t)
                drain(t)
                if 1 <= t <= n:
                    h = t - 1
                    act.wait_ge(at_t, head0 + h + 3)
                    act.wait_ge(at_o, head0 + h + 1)
                    src = ps[:, 4 + h % 2, :].rearrange("p (k q) -> p k q", k=2)
                    if reverse:
                        src = src[:, :, ::-1]
                    nc.scalar.activation(prob_t[:, h % 2, :].rearrange("p (k q) -> p k q", k=2), src,
                                         ACT.Copy).then_inc(at_pt, 1)
                if t >= 2:
                    h = t - 2
                    act.wait_ge(at_o, head0 + h + 3)
                    nc.scalar.activation(out_hi(h)[rows(h), :], ps[rows(h), 6 + h % 2, 0:T],
                                         ACT.Copy).then_inc(at_oh, 1)

        def dve_attention(dve, head0, n, rows, out_hi, out_lo, scale, bias_of, bias_wait=None, fill=nothing):
            for t in range(n + 3):
                if t < n:
                    if bias_wait is not None:
                        bias_wait(dve, t)
                    dve.wait_ge(at_s, head0 + t + 1)
                    dve.wait_ge(at_t, head0 + t + 1)
                    if bias_of is None:
                        nc.vector.tensor_scalar(prob[:, t % 2, :], ps[:, 2 + t % 2, :], scale, None,
                                                ALU.mult).then_inc(at_stt, 1)
                    else:
                        nc.vector.scalar_tensor_tensor(out=prob[:, t % 2, :], in0=ps[:, 2 + t % 2, :], scalar=scale,
                                                       in1=bias_of(t), op0=ALU.mult, op1=ALU.add).then_inc(at_stt, 1)
                    dve.wait_ge(at_stt, head0 + t + 3)
                    nc.vector.tensor_reduce(neg_max[:, t % 2, :], prob[:, t % 2, :].rearrange("p (t k) -> p t k", t=2),
                                            AX.X, ALU.max, negate=True).then_inc(at_max, 1)
                if 1 <= t <= n:
                    h = t - 1
                    dve.wait_ge(at_exp, 2 * (head0 + h) + 2)
                    nc.vector.reciprocal(den[:, h % 2, :], den[:, h % 2, :]).then_inc(at_rc, 1)
                    dve.wait_ge(at_rc, head0 + h + 1)
                    view = prob[:, h % 2, :].rearrange("p (t k) -> p t k", t=2)
                    nc.vector.tensor_tensor(view, view, den[:, h % 2, :].rearrange("p (t o) -> p t o", o=1)
                                            .broadcast_to([P, 2, T]), ALU.mult).then_inc(at_p, 1)
                if t >= 3:
                    h = t - 3
                    dve.wait_ge(at_oh, head0 + h + 1)
                    nc.vector.tensor_tensor(out_lo(h)[rows(h), :], ps[rows(h), 6 + h % 2, 0:T],
                                            out_hi(h)[rows(h), :].bitcast(F32), ALU.subtract).then_inc(at_ol, 1)
                fill(t)

        def pe_turn_v(pe, run, src, chunks=range(4)):
            for tile in range(2):
                for at, c in enumerate(chunks):
                    ins = nc.tensor.transpose(ps[:, 6 + tile, at * P:(at + 1) * P],
                                              src[:, c, tile * P:(tile + 1) * P], ident)
                ins.then_inc(vt_pe, 1)

        def dve_turn_v(dve, run, v_nat=v_nat):
            for tile in range(2):
                dve.wait_ge(vt_pe, 2 * run + (tile + 1))
                nc.vector.tensor_copy(v_nat[:, tile * 512:(tile + 1) * 512], ps[:, 6 + tile, :]).then_inc(vt_dve, 1)

        def even_odd(h):
            return slice(64 * (h % 2), 64 * (h % 2) + 64)

        def whole(h):
            return slice(0, P)

        def pe_sums(pe, of_x, base, sem_in, both=True):
            for q in range(4):
                pe.wait_ge(sem_in, base + q + 1)
                for c in (2 * q, 2 * q + 1):
                    if both:
                        nc.tensor.matmul(ps[:, 2, 0:T], ones, x[:, c, :], start=c == 0, stop=c == DC - 1,
                                         skip_group_check=True)
                    ins = nc.tensor.matmul(ps[:, 2, T:2 * T], ones, of_x[:, c, :], start=not both and c == 0,
                                           stop=c == DC - 1, skip_group_check=True)
            return ins

        def pe_norm(pe, run, between=None):
            pe_sums(pe, sq, run * NA, n_act).then_inc(n_pe, 1)
            if between is not None:
                between()

        def over(v, n, rows=P):
            return v.rearrange("p (o t) -> p o t", o=1).broadcast_to([rows, n, T])

        def dve_norm(dve, run, gain, between=nothing):
            base = run * ND
            dve.wait_ge(n_pe, run + 1)
            nc.vector.tensor_scalar(mean[:], ps[:, 2, 0:T], 1.0 / D, None, ALU.mult).then_inc(n_dve, 1)
            dve.wait_ge(n_dve, base + 1)
            nc.vector.tensor_tensor(rstd[:, 1, :], mean[:], mean[:], ALU.mult).then_inc(n_dve, 1)
            dve.wait_ge(n_dve, base + 2)
            nc.vector.scalar_tensor_tensor(out=rstd[:, 0, :], in0=ps[:, 2, T:2 * T], scalar=1.0 / D,
                                           in1=rstd[:, 1, :], op0=ALU.mult, op1=ALU.subtract).then_inc(n_dve, 1)
            dve.wait_ge(n_dve, base + 3)
            nc.vector.tensor_scalar(rstd[:, 0, :], rstd[:, 0, :], 0.0, 1e-5, ALU.max, ALU.add).then_inc(n_dve, 1)
            nc.vector.tensor_tensor(x[:], x[:], over(mean[:], DC), ALU.subtract).then_inc(n_dve, 1)
            between(0)
            dve.wait_ge(n_act, run * NA + 6)
            dve.wait_ge(n_dve, base + 5)
            for q in range(5):
                if q < 4:
                    pair = x[:, 2 * q:2 * q + 2, :]
                    nc.vector.tensor_tensor(pair, pair, over(rstd[:, 0, :], 2), ALU.mult).then_inc(n_dve, 1)
                    dve.wait_ge(n_dve, base + 3 * q + 6)
                    for c in (2 * q, 2 * q + 1):
                        nc.vector.tensor_scalar(x[:, c, :], x[:, c, :], par[:, gain + c:gain + c + 1],
                                                par[:, gain + DC + c:gain + DC + c + 1], ALU.mult, ALU.add)\
                            .then_inc(n_dve, 1)
                if q:
                    pair = slice(2 * q - 2, 2 * q)
                    dve.wait_ge(x_split_hi, 4 * run + q + 4)
                    nc.vector.tensor_tensor(x_lo[:, pair, :], x[:, pair, :], x_hi[:, pair, :].bitcast(F32),
                                            ALU.subtract).then_inc(x_split, 1)
                between(1 + q)

        def pin(act, name="natural_log_exp_and_others"):
            nc.scalar.preload_act_table_set(name)

        def act_norm(act, run, whole_pair, between=nothing):
            base = run * NA
            pin(act)
            for q in range(4):
                whole_pair(q)
                nc.scalar.activation(sq[:, 2 * q:2 * q + 2, :], x[:, 2 * q:2 * q + 2, :], ACT.Square)\
                    .then_inc(n_act, 1)
            between(0)
            act.wait_ge(n_dve, run * ND + 4)
            nc.scalar.activation(rstd[:, 0, :], rstd[:, 0, :], ACT.Ln).then_inc(n_act, 1)
            act.wait_ge(n_act, base + 5)
            nc.scalar.activation(rstd[:, 0, :], rstd[:, 0, :], ACT.Exp, scale=-0.5).then_inc(n_act, 1)
            between(1)
            for q in range(4):
                pair = slice(2 * q, 2 * q + 2)
                act.wait_ge(n_dve, run * ND + 3 * q + 8)
                nc.scalar.activation(x_hi[:, pair, :], x[:, pair, :], ACT.Copy).then_inc(x_split_hi, 1)
                between(2 + q)

        def act_ffn(act, group0, p0, run, limit):
            def drain(group, s, q, b):
                act.wait_ge(panel_used, 4 * group + (s + 5))
                nc.scalar.activation(ffn_s[:, b, :], ps[:, b, 0:T], ACT.Silu).then_inc(ffn_act, 1)
                act.wait_ge(ffn_dve, 2 * FC * run + 2 * q + 1)
                nc.scalar.activation(hid_hi[:, q, :], ffn_h[:, b, :], ACT.Copy).then_inc(ffn_act, 1)
            nc.scalar.preload_act_table(ACT.Silu)
            panels(act, group0, p0, 2 * FC, feed_hi, drain, limit)

        def dve_ffn(dve, group0, p0, run, pair0, limit):
            def drain(group, s, q, b):
                dve.wait_ge(ffn_act, 2 * FC * run + 2 * q + 1)
                nc.vector.tensor_tensor(ffn_h[:, b, :], ps[:, b, T:2 * T], ffn_s[:, b, :], ALU.mult)\
                    .then_inc(ffn_dve, 1)
                dve.wait_ge(ffn_act, 2 * FC * run + 2 * q + 2)
                nc.vector.tensor_tensor(hid_lo[:, q, :], ffn_h[:, b, :], hid_hi[:, q, :].bitcast(F32), ALU.subtract)\
                    .then_inc(ffn_dve, 1)
                dve.sem_inc(pair_out, 1)
            panels(dve, group0, p0, 2 * FC, feed_lo, drain, limit)

        def chunk_c(c):
            return slice(64 * (c % 2), 64 * (c % 2) + 64)

        def pe_mod(pe, visit):
            pe.wait_ge(mod_sum, visit + 1)
            for j in range(MOD_STEP):
                ins = nc.tensor.matmul(ps[:, 3, j:j + 1], mod_acc[:, j, :], ones[:, 0:1], start=True, stop=True)
            ins.then_inc(mod_taken, 1)

        def dve_mod(dve, visit):
            dve.wait_ge(mod_taken, visit + 2)
            nc.vector.tensor_copy(modv[:, bass.ds(visit * MOD_STEP, MOD_STEP)], ps[:, 3, 0:MOD_STEP])\
                .then_inc(mod_out, 1)

        def f_tile(t, tile):
            return fl[0:16, t, tile * P:(tile + 1) * P]

        @block.tensor
        def _(pe):
            pe.sem_inc(panel_used, RING)
            pe.sem_inc(pair_out, 2)
            pe.sem_inc(mod_taken, 1)
            pe.sem_inc(down_out, 1)
            for s_ in (at_stt, at_pt, at_t, at_o, at_ol):
                pe.sem_inc(s_, 2)
            with pe.Fori(0, L) as l:
                g0, q0, h0 = l * GROUPS1, l * PAIRS1, l * HEADS1
                project(pe, g0, B_COLS, 6, q0 + Q_B, x_hi, x_lo, DC, split0=12 * l)
                pe.wait_ge(consts_in, 64)
                pe.wait_ge(pair_out, q0 + Q_AQ + 2)
                pe.sem_inc(pe_turn, 1)
                nc.tensor.matmul(ps[64:96, 3, 0:T], c_("rot32")[64:96, :], c_all[64:96, 5, :],
                                 start=True, stop=True).then_inc(b_pe, 1)
                pe.wait_ge(b_act, l * BA + 1)
                for c in range(3):
                    nc.tensor.matmul(ps[:, 2, 0:T], ones, sq_b[:, c, :], start=c == 0, stop=c == 2)
                for c in range(2):
                    ins = nc.tensor.matmul(ps[:, 2, T:2 * T], ones, sq_b[:, 3 + c, :], start=c == 0, stop=c == 1)
                ins.then_inc(b_pe, 1)
                a_queries = beside(pe, g0, A_Q, 4, q0 + Q_AQ, x_hi, x_lo, 4)
                for t in range(4):
                    a_queries(t)
                pe.wait_ge(b_dve, l * BD + 11)
                project(pe, g0, B_UQ, 4, q0 + Q_UQ, cn_hi, cn_lo, 3, m=96, per_panel=2)
                project(pe, g0, B_UKV, 4, q0 + Q_UKV, cn_hi[:, 3:5, :], cn_lo[:, 3:5, :], 2, per_panel=2)
                pe.wait_ge(pair_out, q0 + Q_A + 2)
                pe.sem_inc(pe_turn, 1)
                for h in range(0, 8, 2):
                    ins = nc.tensor.matmul(ps[64:96, 2 + h // 2, :], c_("rot32")[64:96, :],
                                           q_b[64:96, h:h + 2, :], start=True, stop=True)
                ins.then_inc(b_pe, 1)
                for tile in range(2):
                    for h in range(8):
                        ins = nc.tensor.transpose(ps[:, 6 + tile, 64 * h:64 * h + 64],
                                                  kv_b[64:128, h, tile * P:(tile + 1) * P], ident[64:128, 64:128])
                ins.then_inc(b_pe, 1)

                def b_ready(pe):
                    pe.wait_ge(b_dve, l * BD + 17)
                    pe.wait_ge(b_key, l + 1)
                b_panels = beside(pe, g0, A_KV, 8, q0 + Q_A, x_hi, x_lo, 10)

                def b_fill(t):
                    b_panels(t)
                    if t % 2 and t < 7:
                        pe.wait_ge(b_dve, l * BD + 17 + t + 1)
                    if t == 1:
                        pe.wait_ge(b_v, 2 * l + 2)
                pe_attention(pe, h0, 8, lambda h, t: q_b[0:96, h, t * P:(t + 1) * P], lambda h: kv_b[0:96, h, :], None,
                             lambda h, kt: v_nat[:, kt * 512 + 64 * h:kt * 512 + 64 * h + 64], even_odd, b_ready, b_fill)
                pe.wait_ge(at_stt, h0 + 8 + 2)
                pe_mod(pe, 4 * l)
                pe.wait_ge(c_dve, l * CD + 3)
                pe.sem_inc(pe_turn, 1)
                for tile in range(2):
                    ins = nc.tensor.transpose(ps[:, 2, 8 * tile:8 * tile + 8], flog[0:8, tile * P:(tile + 1) * P],
                                              ident[0:8, 0:8])
                ins.then_inc(c_pe, 1)
                pe.wait_ge(pair_out, q0 + Q_C + 2)
                pe.wait_ge(at_ol, h0 + 8 + 2)
                pe_turn_v(pe, 3 * l, v_a)
                pe.wait_ge(c_dve, l * CD + 5)
                for tile in range(2):
                    ins = nc.tensor.matmul(ps[0:16, 2, T:2 * T], f_nat[:, tile, :],
                                           c_("tri")[:, tile * T:(tile + 1) * T], start=tile == 0, stop=tile == 1)
                ins.then_inc(c_pe, 1)

                def a_ready(pe):
                    pe.wait_ge(vt_dve, 6 * l + 2)
                    pe.wait_ge(mod_out, 4 * l + 1)
                    pe.wait_ge(c_dve, l * CD + 7)
                pe_attention(pe, h0 + 8, 8, lambda h, t: qk_a[chunk_c(h), h // 2, t * P:(t + 1) * P],
                             lambda h: qk_a[chunk_c(h), 4 + h // 2, :], None,
                             lambda h, kt: v_nat[:, kt * 512 + 64 * h:kt * 512 + 64 * h + 64], even_odd, a_ready,
                             beside(pe, g0, C_QKV, 12, q0 + Q_C, x_hi, x_lo, 10))
                pe.wait_ge(pair_out, q0 + Q_G + 2)
                pe.wait_ge(at_ol, h0 + 16 + 2)
                pe_turn_v(pe, 3 * l + 1, v_t)

                def c_ready(pe):
                    pe.wait_ge(vt_dve, 6 * l + 4)
                    pe.wait_ge(c_dve, l * CD + CD)
                pe_attention(pe, h0 + 16, 8, lambda h, t: qk[chunk_c(h), h // 2, t * P:(t + 1) * P],
                             lambda h: qk[chunk_c(h), 4 + h // 2, :], (f_tile, fr),
                             lambda h, kt: v_nat[:, kt * 512 + 64 * h:kt * 512 + 64 * h + 64], even_odd, c_ready,
                             beside(pe, g0, GATE, 12, q0 + Q_G, x_hi, x_lo, 10))
                pe.wait_ge(at_ol, h0 + 24 + 2)
                project(pe, g0, GATE + 12, 12, q0 + Q_G + 6, x_hi, x_lo, DC)
                for n in range(3):
                    project(pe, g0, BRANCH + 4 * n, 4, q0 + Q_BR + 4 * n, br_hi[:, 4 * n:4 * n + 4, :],
                            br_lo[:, 4 * n:4 * n + 4, :], 4, per_panel=2)
                pe_mod(pe, 4 * l + 1)
                project(pe, g0, OUT1, 8, q0 + Q_OUT, mg_hi, mg_lo, DC, split0=4 * l, split_by=mg_l)
                pe.wait_ge(mem_l, 2 * l + 2)
                memory_part = beside(pe, g0, X_KV, 8, q0 + Q_XKV, mem_hi, mem_lo, 8)
                pe_norm(pe, 3 * l, lambda: [memory_part(t) for t in range(8)])
                project(pe, g0, X_Q, 2, q0 + Q_XQ, x_hi, x_lo, DC, split0=12 * l + 4)
                pe_turn_v(pe, 3 * l + 2, v_t)

                x_panels = beside(pe, g0, X_Q + 2, 2, q0 + Q_XQ + 1, x_hi, x_lo, 2)

                def x_query(h, t):
                    if h == 2 and t == 0:
                        pe.wait_ge(pair_out, q0 + Q_XO + 2)
                    return qk[:, h, t * P:(t + 1) * P]

                def x_ready(pe):
                    pe.wait_ge(pair_out, q0 + Q_XQ + 1 + 2)
                    pe.wait_ge(vt_dve, 6 * l + 6)
                    pe.wait_ge(mod_out, 4 * l + 2)
                pe_attention(pe, h0 + 24, 4, x_query, lambda h: qk[:, 4 + h, :], None,
                             lambda h, kt: v_nat[:, kt * 512 + P * h:kt * 512 + P * h + P], whole, x_ready,
                             x_panels)
                pe.wait_ge(at_ol, h0 + 28 + 2)
                project(pe, g0, X_O, 4, q0 + Q_XO, xo_hi, xo_lo, 4, per_panel=2)
                pe_norm(pe, 3 * l + 1, lambda: pe_mod(pe, 4 * l + 2))
                project(pe, g0, GU1, 2 * FC, q0 + Q_GU, x_hi, x_lo, DC, split0=12 * l + 8)
                down(pe, g0, DOWN1, l)
                pe_norm(pe, 3 * l + 2, lambda: pe_mod(pe, 4 * l + 3))

            pe.sem_inc(hg_s, 1)
            with pe.Fori(0, L) as l:
                g0, q0, h0 = L * GROUPS1 + l * GROUPS2, L * PAIRS1 + l * PAIRS2, L * HEADS1 + 4 * l

                def norm2(k):
                    pe_sums(pe, sq2, 6 * (3 * l + k), rn_act, both=False).then_inc(rn_pe, 1)
                norm2(0)
                project(pe, g0, GU2A, 2 * FC, q0 + R_GUA, x_hi, x_lo, DC, split0=12 * (L + l) + 4)
                down(pe, g0, DOWN2A, L + 2 * l)
                norm2(1)
                project(pe, g0, IN2, 12, q0 + R_IN, x_hi, x_lo, DC, split0=12 * (L + l) + 8)
                fills = [beside(pe, g0, IN2 + p, n, q0 + R_IN + p // 2, x_hi, x_lo, slots)
                         for p, n, slots in IN2_PARTS]
                pe.wait_ge(pair_out, q0 + R_IN + 6 + 2)
                pe.wait_ge(consts2_in, 16)
                pe_turn_v(pe, 0, h_all, (4, 5, 10, 11))
                for t in range(6):
                    if t < 4:
                        for kt in range(2):
                            ins = nc.tensor.matmul(ps[:, 2 + t % 2, kt * T:(kt + 1) * T],
                                                   h_all[chunk_c(t), 2 + t // 2, kt * P:(kt + 1) * P],
                                                   h_all[chunk_c(t), t // 2, :], start=True, stop=True)
                        ins.then_inc(sb_z, 1)
                    fills[0](t)
                    if 1 <= t <= 4:
                        h = t - 1
                        bank, b = ps[:, 4 + h % 2, :], h % 2
                        pe.wait_ge(sb_l, 4 * l + h + 1)
                        nc.tensor.matmul(bank[:, 0:T], c2("suffix"), prob_t[:, b, 0:T], start=True, stop=False)
                        nc.tensor.matmul(bank[:, 0:T], ones, prob_t[:, b, T:2 * T], start=False, stop=True)
                        nc.tensor.matmul(bank[:, T:2 * T], c2("suffix"), prob_t[:, b, T:2 * T],
                                         start=True, stop=True).then_inc(sb_t, 1)
                    if t >= 2:
                        h = t - 2
                        pe.wait_ge(sb_w, 4 * l + h + 1)
                        if h == 0:
                            pe.wait_ge(vt_dve, 2 * (3 * L + 2 * l) + 2)
                        if h >= 2:
                            pe.wait_ge(sb_ol, 4 * l + h - 1)
                        for kt in range(2):
                            ins = nc.tensor.matmul(ps[even_odd(h), 6 + h % 2, 0:T],
                                                   v_nat[:, kt * 512 + 64 * h:kt * 512 + 64 * h + 64],
                                                   prob[:, h % 2, kt * T:(kt + 1) * T], start=kt == 0, stop=kt == 1)
                        ins.then_inc(sb_o, 1)
                pe.wait_ge(dl_act, 3 * l + 1)
                for n in range(2):
                    ins = nc.tensor.matmul(ps[:, 2 + n, :], c2("block64"), rot_tmp[:, 2 * n:2 * n + 2, :],
                                           start=True, stop=True)
                ins.then_inc(dl_pe, 1)
                fills[1](0)
                fills[1](1)
                pe.wait_ge(dl_dve, 9 * l + 4)
                for n in range(2):
                    ins = nc.tensor.matmul(ps[:, 2 + n, :], c2("rot64"), h_all[:, 6 + 2 * n:8 + 2 * n, :],
                                           start=True, stop=True)
                ins.then_inc(dl_pe, 1)

                def d_ready(pe):
                    pe.wait_ge(dl_dve, 9 * l + 9)
                    pe.wait_ge(sb_ol, 4 * l + 4)
                pe_attention(pe, h0, 4, lambda h, t: h_all[chunk_c(h), 6 + h // 2, t * P:(t + 1) * P],
                             lambda h: h_all[chunk_c(h), 8 + h // 2, :], None,
                             lambda h, kt: v_nat[:, kt * 512 + 256 + 64 * h:kt * 512 + 256 + 64 * h + 64],
                             even_odd, d_ready, fills[2])
                for t in range(4):
                    fills[3](t)
                pe.wait_ge(hg_dve, HG * l + 11)
                pe.wait_ge(at_ol, h0 + 4 + 2)
                for tile in range(2):
                    for h in range(4):
                        ins = nc.tensor.transpose(ps[:, 2 + tile, h * P:(h + 1) * P],
                                                  logf[:, h, tile * P:(tile + 1) * P], ident)
                ins.then_inc(hg_pe, 1)
                pe_turn_v(pe, 0, h_all, (20, 21, 22, 23))
                pe.wait_ge(hg_dve, HG * l + 13)
                pe.wait_ge(vt_dve, 2 * (3 * L + 2 * l) + 4)

                def sums(level):
                    if level:
                        pe.wait_ge(hg_exp, 8 * l + level)
                    for tile in range(2):
                        span = level if level < 7 else 7 + tile
                        for h in range(4):
                            ins = nc.tensor.matmul(ps[:, 2 + tile, h * P:(h + 1) * P],
                                                   logf_nat[:, tile * 512 + h * P:tile * 512 + (h + 1) * P],
                                                   c2("spans")[:, span * P:(span + 1) * P], start=True, stop=True)
                    ins.then_inc(hg_d, 1)
                sums(0)
                for level in range(9):
                    if level < 7:
                        sums(level + 1)
                    if level < 8:
                        pe.wait_ge(hg_qe, 8 * l + level + 1)
                        pe.wait_ge(hg_ke, 8 * l + level + 1)
                    if level > 1:
                        pe.wait_ge(hg_m, 9 * l + level - 1)
                    b = level % 2
                    bank = 4 + 2 * b
                    if level == 7:
                        for h in range(4):
                            ins = nc.tensor.matmul(ps[:, bank, h * P:(h + 1) * P], h_ke[b][:, 0, h, :],
                                                   h_qe[b][:, 1, h, :], start=True, stop=True)
                    else:
                        keys, queries = (h_ke[b], h_qe[b]) if level < 8 else (k_h, q_h)
                        for tile in range(2):
                            for h in range(4):
                                ins = nc.tensor.matmul(ps[:, bank + tile, h * P:(h + 1) * P], keys[:, tile, h, :],
                                                       queries[:, tile, h, :], start=True, stop=True)
                    ins.then_inc(hg_s, 1)
                pe.wait_ge(hg_m, 9 * l + 9)
                pe.wait_ge(hg_dve, HG * l + 14)
                for h in range(4):
                    out = ps[:, 6 + h // 2, :]
                    at = (h % 2) * T
                    nc.tensor.matmul(out[:, at:at + P], v_h[:, h * P:(h + 1) * P], scores[:, 0, h, :],
                                     start=True, stop=True)
                    nc.tensor.matmul(out[:, at + P:at + T], v_h[:, h * P:(h + 1) * P], cross[:, h * P:(h + 1) * P],
                                     start=True, stop=False)
                    ins = nc.tensor.matmul(out[:, at + P:at + T], v_h[:, 512 + h * P:512 + (h + 1) * P],
                                           scores[:, 1, h, :], start=False, stop=True)
                ins.then_inc(hg_pe, 1)
                pe.wait_ge(pair_out, q0 + R_OUT + 2)
                for p in (OUT2, OUT2 + 1):
                    pe.wait_ge(lo_done, 4 * (g0 + p // 4) + (p % 4 + 1))

                def out_part(chunks):
                    for half in range(2):
                        for k in chunks:
                            ins = multiply(pe, ps[:, 0, half * T:(half + 1) * T], k * P, P, k, (OUT2 + half) % 4,
                                           mix_hi[:, k, :], mix_lo[:, k, :], k == 0 and half == 0, k == DC - 1, True)
                            if k == DC - 1:
                                ins.then_inc(panel_used, 1)
                pe.wait_ge(at_ol, h0 + 4 + 2)
                out_part(range(4))
                pe.wait_ge(hg_act, HA * l + 7)
                for n in range(2):
                    ins = nc.tensor.matmul(ps[:, 2 + n, :], ones, sq2[:, 2 * n:2 * n + 2, :], start=True, stop=True)
                ins.then_inc(hg_pe, 1)
                pe.wait_ge(hg_dve, HG * l + HG)
                out_part(range(4, DC))
                project(pe, g0, OUT2, 8, q0 + R_OUT, mix_hi, mix_lo, DC, done=2)
                norm2(2)
                project(pe, g0, GU2B, 2 * FC, q0 + R_GUB, x_hi, x_lo, DC, split0=12 * (L + l) + 12)
                down(pe, g0, DOWN2B, L + 2 * l + 1)

        @block.scalar
        def _(act):
            act.dma_start(silu_c[:], io["c"]).then_inc(c_in, 16)
            for q in range(4):
                pair = slice(2 * q, 2 * q + 2)
                act.wait_ge(x_in[q], 16)
                nc.scalar.activation(x_hi[:, pair, :], x[:, pair, :], ACT.Copy).then_inc(x_split_hi, 1)
                if q < 2:
                    feed_hi(act, 0, q)
            act.wait_ge(c_in, 16)
            nc.scalar.activation(silu_c[:], silu_c[:], ACT.Silu).then_inc(silu_done, 1)
            act.wait_ge(consts_in, 64)
            for n in range(2):
                dst = (rope_sin, rope_cos)[n]
                act.wait_ge(rope_dve, 10 * (n + 1))
                nc.scalar.activation(dst[64:96, :], dst[64:96, :], ACT.Sin).then_inc(rope_act, 1)

            with act.Fori(0, L) as l:
                g0, q0, h0 = l * GROUPS1, l * PAIRS1, l * HEADS1
                act.wait_ge(par_set, l + 1)

                def copy_pair(dst):
                    def drain(group, s, q, b):
                        act.wait_ge(panel_used, 4 * group + (s + 5))
                        nc.scalar.activation(dst(q), ps[:, b, :].rearrange("p (n w) -> p n w", w=T),
                                             ACT.Copy).then_inc(pair_out, 1)
                    return drain

                def feeds(p0, p1):
                    for p in range(p0, p1):
                        feed_hi(act, g0 + p // 4, p % 4)
                panels(act, g0, B_COLS, 6, feed_hi, copy_pair(lambda q: c_all[:, 2 * q:2 * q + 2, :]), PANELS1)
                act.wait_ge(pair_out, q0 + Q_AQ + 2)
                nc.scalar.activation(sq_b[:], c_all[:, 0:5, :], ACT.Square).then_inc(b_act, 1)
                feeds(A_Q + 2, A_Q + 4)
                act.wait_ge(b_dve, l * BD + 2)
                nc.scalar.activation(rstd[:], rstd[:], ACT.Ln).then_inc(b_act, 1)
                act.wait_ge(b_act, l * BA + 2)
                nc.scalar.activation(rstd[:], rstd[:], ACT.Exp, scale=-0.5).then_inc(b_act, 1)
                act.wait_ge(b_dve, l * BD + 10)
                nc.scalar.activation(cn_hi[:], c_all[:, 0:5, :], ACT.Copy).then_inc(b_act, 1)

                def keep_a(q, src):
                    dst = qk_a[:, 2 * q:2 * q + 2, :] if q < 4 else v_a[:, 2 * q - 8:2 * q - 6, :]
                    nc.scalar.activation(dst, src[:, :, ::-1] if q < 2 else src, ACT.Copy).then_inc(pair_out, 1)
                for q in range(2):
                    feeds(B_UQ + q, B_UQ + q + 1)
                    act.wait_ge(panel_used, 4 * g0 + A_Q + 2 * q + 1 + 5)
                    keep_a(q, ps[:, q, :].rearrange("p (n w) -> p n w", w=T))
                for j in range(4):
                    for p in (2 * j + B_UQ + 2, 2 * j + B_UQ + 3):
                        if p < A_KV:
                            feed_hi(act, g0 + p // 4, p % 4)
                    for p in (B_UQ + 2 * j, B_UQ + 2 * j + 1):
                        act.wait_ge(panel_used, 4 * g0 + p + 5)
                        b = (p - B_UQ) % 2
                        m, dst = (96, q_b) if p < B_UKV else (P, kv_b)
                        h = 2 * ((p - B_UQ) % 4)
                        nc.scalar.activation(dst[0:m, h:h + 2, :], ps[0:m, b, :].rearrange("p (n w) -> p n w", w=T),
                                             ACT.Copy).then_inc(pair_out, 1)
                act.sem_inc(b_act, 1)

                def keep_c(q, src):
                    dst = qk[:, 2 * q:2 * q + 2, :] if q < 4 else v_t[:, 2 * q - 8:2 * q - 6, :]
                    nc.scalar.activation(dst, src, ACT.Copy).then_inc(pair_out, 1)

                def keep_gate(q, src):
                    for o in range(2):
                        c = 2 * q + o
                        ins = nc.scalar.activation(gates[:, c, :], src[:, o, :], ACT.Identity,
                                                   bias=par[:, P_GATE + c:P_GATE + c + 1])
                    ins.then_inc(pair_out, 1)

                pin(act)
                feeds(A_KV, A_KV + 2)
                act.wait_ge(b_dve, l * BD + 5)
                act.wait_ge(b_pe, l * BP + 4)
                nc.scalar.activation(kv_b[64:96, :, :], over(c_all[64:96, 5, :], 8, 32), ACT.Copy).then_inc(b_key, 1)
                b_feed = feed_beside(act, g0, A_KV, 8, feed_hi, 10, PANELS1)

                def b_fill(t):
                    b_feed(t)
                    if t == 3:
                        act.wait_ge(c_dve, l * CD + 1)
                        nc.scalar.activation(fabs[0:8, :], flog[0:8, :], ACT.Abs).then_inc(c_act, 1)
                        act.wait_ge(c_act, l * CA + 1)
                        nc.scalar.activation(fabs[0:8, :], fabs[0:8, :], ACT.Exp, scale=-1.0).then_inc(c_act, 1)
                        act.wait_ge(c_act, l * CA + 2)
                        nc.scalar.activation(fabs[0:8, :], fabs[0:8, :], ACT.Ln, bias=1.0).then_inc(c_act, 1)
                act_attention(act, h0, 8, even_odd, lambda h: br_hi[:, 4 + h // 2, :], False, None, b_fill,
                              drain_beside(act, g0, A_KV, 8, 10, lambda q, src: keep_a(q + 2, src)))

                def bias_dma(act, h):
                    act.wait_ge(at_stt, h0 + 8 + h + 1)
                    for blk in range(4):
                        rows = slice(64 * (blk % 2), 64 * (blk % 2) + 64)
                        at = (blk // 2) * T
                        n = T - 64 * blk
                        src = io["rel"][l][h, blk, :, 0:n]
                        act.dma_start(bias[rows, h % 2, at:at + n], src).then_inc(bias_in[h % 2], 16)
                act.wait_ge(init_done, 1)
                bias_dma(act, 0)
                bias_dma(act, 1)
                act_attention(act, h0 + 8, 8, even_odd, lambda h: br_hi[:, h // 2, :], True, bias_dma,
                              feed_beside(act, g0, C_QKV, 12, feed_hi, 10, PANELS1),
                              drain_beside(act, g0, C_QKV, 12, 10, keep_c))
                act_attention(act, h0 + 16, 8, even_odd, lambda h: br_hi[:, 8 + h // 2, :], False, None,
                              feed_beside(act, g0, GATE, 12, feed_hi, 10, PANELS1),
                              drain_beside(act, g0, GATE, 12, 10, keep_gate))
                act.dma_start(mem[:], io["memT"]).then_inc(mem_in, 16)
                for q in range(6):
                    feeds(GATE + 12 + 2 * q + 2, GATE + 12 + 2 * q + 4)
                    act.wait_ge(panel_used, 4 * g0 + GATE + 12 + 2 * q + 1 + 5)
                    keep_gate(6 + q, ps[:, q % 2, :].rearrange("p (n w) -> p n w", w=T))
                act.wait_ge(pair_out, q0 + Q_BR + 2)
                nc.scalar.activation(gates[:], gates[:], ACT.Sigmoid).then_inc(gate_done, 1)
                only_feed(act, g0, BRANCH + 2, BRANCH + 12, feed_hi)
                feeds(OUT1, OUT1 + 2)
                for q in range(4):
                    pair = slice(2 * q, 2 * q + 2)
                    act.wait_ge(br_dve, l * 20 + 14 + 2 * q)
                    nc.scalar.activation(mg_hi[:, pair, :], merged[:, pair, :], ACT.Copy).then_inc(mg_h, 1)
                feeds(OUT1 + 2, OUT1 + 4)
                act.wait_ge(mem_in, 16 * l + 16)
                nc.scalar.activation(mem_hi[:], mem[:], ACT.Copy).then_inc(mem_h, 1)
                feeds(OUT1 + 4, X_KV + 2)

                def keep_mem(q, src):
                    dst = qk[:, 4 + 2 * q:6 + 2 * q, :] if q < 2 else v_t[:, 2 * q - 4:2 * q - 2, :]
                    nc.scalar.activation(dst, src, ACT.Copy).then_inc(pair_out, 1)
                mem_feed = feed_beside(act, g0, X_KV, 8, feed_hi, 8, PANELS1)
                mem_drain = drain_beside(act, g0, X_KV, 8, 8, keep_mem)

                def mem_steps(at):
                    for t in ((0, 1), (2, 3), (4,), (5,), (6,), (7,))[at]:
                        mem_feed(t)
                        mem_drain(t)
                act_norm(act, 3 * l, lambda q: act.wait_ge(pair_out, q0 + Q_OUT + q + 3), mem_steps)
                def keep_xq(q, src):
                    nc.scalar.activation(qk[:, 2 * q:2 * q + 2, :], src, ACT.Copy).then_inc(pair_out, 1)
                feeds(X_Q + 2, X_O)
                act.wait_ge(panel_used, 4 * g0 + X_Q + 1 + 5)
                keep_xq(0, ps[:, 0, :].rearrange("p (n w) -> p n w", w=T))
                act_attention(act, h0 + 24, 4, whole, lambda h: xo_hi[:, h, :], False, None,
                              feed_beside(act, g0, X_O - 2, 4, feed_hi, 4, PANELS1),
                              drain_beside(act, g0, X_Q + 2, 2, 2, lambda q, src: keep_xq(1, src)))
                act_norm(act, 3 * l + 1, lambda q: act.wait_ge(pair_out, q0 + Q_XO + q + 3),
                         lambda at: feeds(GU1 + at, GU1 + at + 1) if at < 2 else None)
                act_ffn(act, g0, GU1, l, PANELS1)
                only_feed(act, g0, DOWN1 + 2, PANELS1 + 2, feed_hi)
                act_norm(act, 3 * l + 2, lambda q: act.wait_ge(down_out, 4 * l + q + 2))

            act.wait_ge(mod_end, 1)
            act.wait_ge(mod_taken, 9)
            act.dma_start(side[:, 0:N_CONST2], io["const2"]).then_inc(consts2_in, 16)
            act.wait_ge(lb_dve, 1)
            nc.scalar.activation(lb_t[:, 0:2, :], lb_t[:, 0:2, :], ACT.Exp).then_inc(lb_act, 1)
            with act.Fori(0, L) as l:
                g0, q0, h0 = L * GROUPS1 + l * GROUPS2, L * PAIRS1 + l * PAIRS2, L * HEADS1 + 4 * l

                def norm2(k):
                    run = 3 * l + k
                    pin(act)
                    for q in range(4):
                        pair = slice(2 * q, 2 * q + 2)
                        act.wait_ge(res2, 4 * run + q + 1)
                        nc.scalar.activation(sq2[:, pair, :], x[:, pair, :], ACT.Square).then_inc(rn_act, 1)
                    act.wait_ge(rn_dve, 9 * run + 1)
                    nc.scalar.activation(rstd[:, 0, :], rstd[:, 0, :], ACT.Ln).then_inc(rn_act, 1)
                    act.wait_ge(rn_act, 6 * run + 5)
                    nc.scalar.activation(rstd[:, 0, :], rstd[:, 0, :], ACT.Exp, scale=-0.5).then_inc(rn_act, 1)
                    for q in range(4):
                        pair = slice(2 * q, 2 * q + 2)
                        act.wait_ge(rn_dve, 9 * run + 2 * q + 3)
                        for c in (2 * q, 2 * q + 1):
                            ins = nc.scalar.activation(x_hi[:, c, :], normed[:, c, :], ACT.Identity,
                                                       bias=modl[:, 24 * k + c:24 * k + c + 1])
                        ins.then_inc(x_split_hi, 1)

                def feeds(p0, p1):
                    for p in range(p0, p1):
                        feed_hi(act, g0 + p // 4, p % 4)
                norm2(0)
                act_ffn(act, g0, GU2A, L + 2 * l, PANELS2)
                only_feed(act, g0, DOWN2A + 2, IN2 + 2, feed_hi)
                norm2(1)

                def keep(group, s, q, b):
                    act.wait_ge(panel_used, 4 * group + (s + 5))
                    nc.scalar.activation(h_all[:, bass.ds(2 * q, 2), :], ps[:, b, :].rearrange("p (n w) -> p n w", w=T),
                                         ACT.Copy).then_inc(pair_out, 1)
                panels(act, g0, IN2, 12, feed_hi, keep, PANELS2)

                def keep_at(first):
                    def drain(q, src):
                        nc.scalar.activation(h_all[:, first + 2 * q:first + 2 * q + 2, :], src, ACT.Copy)\
                            .then_inc(pair_out, 1)
                    return drain
                fills = [feed_beside(act, g0, IN2 + p, n, feed_hi, slots, PANELS2) for p, n, slots in IN2_PARTS]
                drains = [drain_beside(act, g0, IN2 + p, n, slots, keep_at(p)) for p, n, slots in IN2_PARTS]
                pin(act)
                for t in range(6):
                    fills[0](t)
                    if t < 4:
                        s_, buf = 3 * (4 * l + t), prob_t[:, t % 2, :]
                        act.wait_ge(sb_d, 2 * (4 * l + t) + 1)
                        nc.scalar.activation(buf, prob[:, t % 2, :], ACT.Abs).then_inc(sb_a, 1)
                        act.wait_ge(sb_a, s_ + 1)
                        nc.scalar.activation(buf, buf, ACT.Exp, scale=-1.0).then_inc(sb_a, 1)
                        act.wait_ge(sb_a, s_ + 2)
                        nc.scalar.activation(buf, buf, ACT.Ln, bias=1.0).then_inc(sb_a, 1)
                    drains[0](t)
                    if 1 <= t <= 4:
                        h = t - 1
                        act.wait_ge(sb_lw, 4 * l + h + 1)
                        nc.scalar.activation(prob[:, h % 2, :], prob[:, h % 2, :], ACT.Exp).then_inc(sb_e, 1)
                    if t >= 2:
                        h = t - 2
                        act.wait_ge(sb_o, 4 * l + h + 1)
                        nc.scalar.activation(mix_hi[even_odd(h), h // 2, :], ps[even_odd(h), 6 + h % 2, 0:T],
                                             ACT.Copy).then_inc(sb_oh, 1)
                nc.scalar.activation(rot_tmp[:], h_all[:, 6:10, :], ACT.Square).then_inc(dl_act, 1)
                fills[1](0)
                act.wait_ge(dl_dve, 9 * l + 2)
                nc.scalar.activation(rs4[:], rs4[:], ACT.Ln).then_inc(dl_act, 1)
                act.wait_ge(dl_act, 3 * l + 2)
                nc.scalar.activation(rs4[:], rs4[:], ACT.Exp, scale=-0.5).then_inc(dl_act, 1)
                fills[1](1)
                drains[1](1)
                act_attention(act, h0, 4, even_odd, lambda h: mix_hi[:, 2 + h // 2, :], False, None,
                              fills[2], drains[2])
                ha = HA * l
                for t in range(2):
                    fills[3](t)
                act.wait_ge(pair_out, q0 + R_IN + 12 + 2)
                nc.scalar.activation(logf[:], h_all[:, 16:20, :], ACT.Sigmoid).then_inc(hg_act, 1)
                act.wait_ge(hg_act, ha + 1)
                nc.scalar.activation(h_all[:, 16:20, :], h_all[:, 16:20, :], ACT.Sigmoid, scale=-1.0)\
                    .then_inc(hg_act, 1)
                nc.scalar.activation(h_all[:, 12:16, :], h_all[:, 12:16, :], ACT.Silu).then_inc(hg_act, 1)
                pin(act)
                drains[3](1)
                act.wait_ge(hg_dve, HG * l + 10)
                nc.scalar.activation(logf[:], logf[:], ACT.Ln).then_inc(hg_act, 1)
                nc.scalar.activation(logf_b[:], logf_b[:], ACT.Ln).then_inc(hg_act, 1)
                for t in range(2, 4):
                    fills[3](t)
                    drains[3](t)
                for level in range(8):
                    act.wait_ge(hg_d, 8 * l + level + 1)
                    if level > 1:
                        act.wait_ge(hg_qe, 8 * l + level - 1)
                        act.wait_ge(hg_ke, 8 * l + level - 1)
                    e = F[:, 4096 * (level % 2):4096 * (level % 2) + 1024]
                    nc.scalar.activation(e.rearrange("p (b c) -> p b c", b=2), ps[:, 2:4, :],
                                         ACT.Exp).then_inc(hg_exp, 1)
                act.wait_ge(pair_out, q0 + R_OUT + 2)
                nc.scalar.activation(h_all[:, 24:28, :], h_all[:, 24:28, :], ACT.Silu).then_inc(hg_act, 1)
                pin(act)
                act.wait_ge(hg_pe, 3 * l + 2)
                act.wait_ge(hg_ke, 8 * l + 8)
                act.wait_ge(hg_qe, 8 * l + 8)
                nc.scalar.activation(F[:, 0:1024].rearrange("p (b c) -> p b c", b=2), ps[:, 6:8, :],
                                     ACT.Square).then_inc(hg_act, 1)
                act.wait_ge(hg_dve, HG * l + 18)
                nc.scalar.activation(h_qe[0], h_qe[0], ACT.Ln).then_inc(hg_act, 1)
                act.wait_ge(hg_act, ha + 8)
                nc.scalar.activation(h_qe[0], h_qe[0], ACT.Exp, scale=-0.5).then_inc(hg_act, 1)
                act.wait_ge(hg_dve, HG * l + 20)
                nc.scalar.activation(mix_hi[:, 4:8, :], o_h[:], ACT.Copy).then_inc(hg_hi, 1)
                feeds(OUT2 + 2, GU2B + 2)
                norm2(2)
                act_ffn(act, g0, GU2B, L + 2 * l + 1, PANELS2)
                only_feed(act, g0, DOWN2B + 2, PANELS2 + 2, feed_hi)
            act.wait_ge(res2, 4 * (3 * L + 1))
            act.dma_start(io["out"], x[:]).then_inc(out_in, 16)
            act.wait_ge(out_in, 16)

        @block.vector
        def _(dve):
            nc.vector.memset(bias[:], NEG).then_inc(init_done, 1)
            for q in range(4):
                pair = slice(2 * q, 2 * q + 2)
                dve.wait_ge(x_split_hi, q + 1)
                nc.vector.tensor_tensor(x_lo[:, pair, :], x[:, pair, :], x_hi[:, pair, :].bitcast(F32),
                                        ALU.subtract).then_inc(x_split, 1)
                if q < 2:
                    feed_lo(dve, 0, q)
            two_pi = 2.0 * np.pi
            hi = float(np.float32(np.round(two_pi * 256) / 256))
            mid = float(np.float32(np.round((two_pi - hi) * 2 ** 20) / 2 ** 20))
            low = float(np.float32(two_pi - hi - mid))
            magic = 12582912.0
            edge = 3.1415925
            rows = slice(64, 96)
            ang, turns = F[rows, 4096:4352], F[rows, 4352:4608]
            step = 0

            def chain(ins):
                nonlocal step
                ins.then_inc(rope_dve, 1)
                step += 1
                dve.wait_ge(rope_dve, step)
            dve.wait_ge(consts_in, 64)
            for n in range(2):
                out = (rope_sin, rope_cos)[n][rows, :]
                nc.vector.tensor_copy(ang, pos_i[rows, :]).then_inc(rope_dve, 1)
                step += 1
                dve.wait_ge(rope_dve, step)
                chain(nc.vector.tensor_scalar(ang, ang, c_("invf")[rows, :], None, ALU.mult))
                chain(nc.vector.tensor_scalar(turns, ang, 1.0 / two_pi, 0.25 * n, ALU.mult, ALU.add))
                chain(nc.vector.tensor_scalar(turns, turns, magic, None, ALU.add))
                chain(nc.vector.tensor_scalar(turns, turns, -magic, None, ALU.add))
                chain(nc.vector.scalar_tensor_tensor(out=ang, in0=turns, scalar=-hi, in1=ang,
                                                     op0=ALU.mult, op1=ALU.add))
                chain(nc.vector.scalar_tensor_tensor(out=ang, in0=turns, scalar=-mid, in1=ang,
                                                     op0=ALU.mult, op1=ALU.add))
                chain(nc.vector.scalar_tensor_tensor(out=ang, in0=turns, scalar=-low, in1=ang,
                                                     op0=ALU.mult, op1=ALU.add))
                chain(nc.vector.tensor_scalar(out, ang, 0.5 * np.pi * n, edge, ALU.add, ALU.min))
                chain(nc.vector.tensor_scalar(out, out, -edge, None, ALU.max))

            with dve.Fori(0, L) as l:
                g0, q0, h0 = l * GROUPS1, l * PAIRS1, l * HEADS1
                nc.vector.tensor_copy(par[:], par_all[:, l, :]).then_inc(par_set, 1)
                bd = l * BD

                def feeds(p0, p1):
                    for p in range(p0, p1):
                        feed_lo(dve, g0 + p // 4, p % 4)
                feeds(2, 8)
                dve.wait_ge(b_pe, l * BP + 2)
                nc.vector.tensor_scalar(rstd[:, 0, :], ps[:, 2, 0:T], 1.0 / 384, 1e-6, ALU.mult, ALU.add)\
                    .then_inc(b_dve, 1)
                nc.vector.tensor_scalar(rstd[:, 1, :], ps[:, 2, T:2 * T], 1.0 / 256, 1e-6, ALU.mult, ALU.add)\
                    .then_inc(b_dve, 1)
                feeds(A_Q + 2, A_Q + 4)
                dve.wait_ge(rope_act, 2)
                dve.wait_ge(pair_out, q0 + Q_AQ + 2)
                turned = rot_b[rows, 0, :]
                nc.vector.tensor_tensor(turned, ps[rows, 3, 0:T], rope_sin[rows, :], ALU.mult).then_inc(b_dve, 1)
                nc.vector.tensor_tensor(c_all[rows, 5, :], c_all[rows, 5, :], rope_cos[rows, :], ALU.mult)\
                    .then_inc(b_dve, 1)
                dve.wait_ge(b_dve, bd + 4)
                nc.vector.tensor_tensor(c_all[rows, 5, :], c_all[rows, 5, :], turned, ALU.add).then_inc(b_dve, 1)
                dve.wait_ge(b_act, l * BA + 3)
                dve.wait_ge(par_set, l + 1)
                for c in range(5):
                    nc.vector.scalar_tensor_tensor(out=c_all[:, c, :], in0=c_all[:, c, :],
                                                   scalar=par[:, P_QN + c:P_QN + c + 1], in1=rstd[:, c // 3, :],
                                                   op0=ALU.mult, op1=ALU.mult).then_inc(b_dve, 1)
                dve.wait_ge(b_act, l * BA + 4)
                nc.vector.tensor_tensor(cn_lo[:], c_all[:, 0:5, :], cn_hi[:].bitcast(F32), ALU.subtract)\
                    .then_inc(b_dve, 1)
                feeds(B_UQ, A_KV)
                dve.wait_ge(b_act, l * BA + 5)
                dve.wait_ge(pair_out, q0 + Q_A + 2)
                dve.wait_ge(b_pe, l * BP + 3)
                for h in range(0, 8, 2):
                    nc.vector.tensor_tensor(rot_b[rows, h:h + 2, :],
                                            ps[rows, 2 + h // 2, :].rearrange("p (n w) -> p n w", w=T),
                                            over(rope_sin[rows, :], 2, 32), ALU.mult).then_inc(b_dve, 1)

                def turn_q(pair):
                    h = slice(2 * pair, 2 * pair + 2)
                    nc.vector.tensor_tensor(q_b[rows, h, :], q_b[rows, h, :], over(rope_cos[rows, :], 2, 32),
                                            ALU.mult).then_inc(b_dve, 1)
                    dve.wait_ge(b_dve, bd + 16 + 2 * pair)
                    nc.vector.tensor_tensor(q_b[rows, h, :], q_b[rows, h, :], rot_b[rows, h, :], ALU.add)\
                        .then_inc(b_dve, 1)
                turn_q(0)
                dve.wait_ge(b_pe, l * BP + 4)
                for tile in range(2):
                    nc.vector.tensor_copy(v_nat[:, tile * 512:(tile + 1) * 512], ps[:, 6 + tile, :])\
                        .then_inc(b_v, 1)
                feeds(A_KV, A_KV + 2)
                b_feed = feed_beside(dve, g0, A_KV, 8, feed_lo, 10, PANELS1)

                def b_fill(t):
                    b_feed(t)
                    if t < 3:
                        turn_q(t + 1)
                    if t == 3:
                        nc.vector.tensor_scalar(flog[0:8, :], c_all[0:8, 5, :], par[0:8, P_BF:P_BF + 1], None,
                                                ALU.add).then_inc(c_dve, 1)
                    if t == 5:
                        dve.wait_ge(c_act, l * CA + 3)
                        dve.wait_ge(c_dve, l * CD + 1)
                        nc.vector.tensor_scalar(flog[0:8, :], flog[0:8, :], 0.0, None, ALU.min).then_inc(c_dve, 1)
                        dve.wait_ge(c_dve, l * CD + 2)
                        nc.vector.tensor_tensor(flog[0:8, :], flog[0:8, :], fabs[0:8, :], ALU.subtract)\
                            .then_inc(c_dve, 1)
                dve_attention(dve, h0, 8, even_odd, lambda h: br_hi[:, 4 + h // 2, :],
                              lambda h: br_lo[:, 4 + h // 2, :], 96.0 ** -0.5, lambda t: c_("chunk_mask"), None,
                              b_fill)
                dve.wait_ge(c_pe, l * CP + 1)
                f_src = ps[:, 2, 0:16].rearrange("p (t c) -> p t c", t=2)
                nc.vector.tensor_scalar(f_nat[:, :, 0:8], f_src, 8.0, None, ALU.mult).then_inc(c_dve, 1)
                nc.vector.tensor_scalar(f_nat[:, :, 8:16], f_src, -8.0, None, ALU.mult).then_inc(c_dve, 1)
                dve_mod(dve, 4 * l)
                dve_turn_v(dve, 3 * l)
                dve.wait_ge(c_pe, l * CP + 2)
                nc.vector.tensor_scalar(fl0[:], ps[0:16, 2, T:2 * T], c_("is_f")[0:16, :], c_("is_one")[0:16, :],
                                        ALU.mult, ALU.add).then_inc(c_dve, 1)
                nc.vector.tensor_scalar(fr[:], ps[0:16, 2, T:2 * T], c_("is_one")[0:16, :], c_("is_f")[0:16, :],
                                        ALU.mult, ALU.add).then_inc(c_dve, 1)

                def bias_wait(dve, h):
                    dve.wait_ge(bias_in[h % 2], 64 * (4 * l + h // 2 + 1))
                dve_attention(dve, h0 + 8, 8, even_odd, lambda h: br_hi[:, h // 2, :],
                              lambda h: br_lo[:, h // 2, :], 0.125, lambda h: bias[:, h % 2, :], bias_wait,
                              feed_beside(dve, g0, C_QKV, 12, feed_lo, 10, PANELS1))
                dve.wait_ge(c_dve, l * CD + 7)
                nc.vector.tensor_tensor(fl[0:16, :, :], fl0[:].rearrange("p (o t) -> p o t", o=1)
                                        .broadcast_to([16, 8, T]),
                                        c_("head")[0:16, :].rearrange("p (h o) -> p h o", o=1)
                                        .broadcast_to([16, 8, T]), ALU.mult).then_inc(c_dve, 1)
                dve_turn_v(dve, 3 * l + 1)
                dve_attention(dve, h0 + 16, 8, even_odd, lambda h: br_hi[:, 8 + h // 2, :],
                              lambda h: br_lo[:, 8 + h // 2, :], 0.125, lambda t: c_("causal_mask"), None,
                              feed_beside(dve, g0, GATE, 12, feed_lo, 10, PANELS1))
                feeds(GATE + 14, BRANCH + 2)

                def split_merged(q):
                    pair = slice(2 * q, 2 * q + 2)
                    dve.wait_ge(mg_h, 4 * l + q + 1)
                    nc.vector.tensor_tensor(mg_lo[:, pair, :], merged[:, pair, :], mg_hi[:, pair, :].bitcast(F32),
                                            ALU.subtract).then_inc(mg_l, 1)
                step = 0
                for j in range(12):
                    p = BRANCH + j + 2
                    feeds(p, p + 1)
                    n, c = j // 4, 2 * (j % 4)
                    dve.wait_ge(panel_used, 4 * g0 + BRANCH + j + 5)
                    dve.wait_ge(gate_done, l + 1)
                    gate = gates[:, 8 * n + c:8 * n + c + 2, :]
                    src = ps[:, j % 2, :].rearrange("p (n w) -> p n w", w=T)
                    tmp = gate_tmp.rearrange("p (n w) -> p n w", w=T)
                    dst = merged[:, c:c + 2, :] if n == 0 else tmp
                    nc.vector.tensor_tensor(dst, src, gate, ALU.mult).then_inc(br_dve, 1)
                    step += 1
                    dve.wait_ge(br_dve, l * 20 + step)
                    dve.sem_inc(pair_out, 1)
                    if n:
                        nc.vector.tensor_tensor(merged[:, c:c + 2, :], merged[:, c:c + 2, :], tmp, ALU.add)\
                            .then_inc(br_dve, 1)
                        step += 1
                        dve.wait_ge(br_dve, l * 20 + step)
                    if j > 8:
                        split_merged(j - 9)
                split_merged(3)
                dve_mod(dve, 4 * l + 1)

                def residual(p0, n_pairs, per_panel):
                    for q in range(n_pairs):
                        last = p0 + (2 * q + 1 if per_panel == 1 else q)
                        dve.wait_ge(panel_used, 4 * g0 + last + 5)
                        dst = x[:, 2 * q:2 * q + 2, :]
                        nc.vector.scalar_tensor_tensor(out=dst, in0=dst, scalar=ALPHA,
                                                       in1=ps[:, q % 2, :].rearrange("p (n w) -> p n w", w=T),
                                                       op0=ALU.mult, op1=ALU.add).then_inc(pair_out, 1)
                        if per_panel == 1:
                            feeds(last + 3, min(last + 5, p0 + 10))
                        if p0 == OUT1 and q in (1, 2):
                            half = slice(4 * q - 4, 4 * q)
                            dve.wait_ge(mem_h, l + 1)
                            nc.vector.tensor_tensor(mem_lo[:, half, :], mem[:, half, :],
                                                    mem_hi[:, half, :].bitcast(F32), ALU.subtract).then_inc(mem_l, 1)
                feeds(OUT1 + 2, OUT1 + 4)
                residual(OUT1, 4, 1)
                mem_feed = feed_beside(dve, g0, X_KV, 8, feed_lo, 8, PANELS1)
                dve_norm(dve, 3 * l, P_MIXG,
                         lambda at: [mem_feed(t) for t in ((0, 1), (2,), (3,), (4,), (5,), (6, 7))[at]])
                feeds(X_Q + 2, X_O)
                dve_turn_v(dve, 3 * l + 2)
                dve_attention(dve, h0 + 24, 4, whole, lambda h: xo_hi[:, h, :], lambda h: xo_lo[:, h, :],
                              128.0 ** -0.5, None, None, feed_beside(dve, g0, X_O - 2, 4, feed_lo, 4, PANELS1))
                residual(X_O, 4, 2)
                dve_norm(dve, 3 * l + 1, P_XAG, lambda at: feeds(GU1 + at, GU1 + at + 1) if at < 2 else None)
                dve_mod(dve, 4 * l + 2)
                dve_ffn(dve, g0, GU1, l, q0 + Q_GU, PANELS1)
                only_feed(dve, g0, DOWN1 + 2, PANELS1 + 2, feed_lo)
                dve.wait_ge(panel_used, 4 * g0 + PANELS1 + 4)
                for q in range(4):
                    dst = x[:, 2 * q:2 * q + 2, :]
                    nc.vector.scalar_tensor_tensor(out=dst, in0=dst, scalar=ALPHA,
                                                   in1=ps[:, 4 + q, :].rearrange("p (n w) -> p n w", w=T),
                                                   op0=ALU.mult, op1=ALU.add).then_inc(down_out, 1)
                dve_norm(dve, 3 * l + 2, P_FFG)
                dve_mod(dve, 4 * l + 3)

            for q in range(4):
                dve.sem_inc(res2, 1)
            dve.wait_ge(lbl_in, 16)
            nc.vector.tensor_tensor(lb_t[:, 2, :], lbl[:, 0, :], lbl[:, 1, :], ALU.max).then_inc(lb_c, 1)
            dve.wait_ge(lb_c, 1)
            nc.vector.tensor_tensor(lb_t[:, 0:2, :], lbl[:], lb_t[:, 2:3, :].broadcast_to([P, 2, 4]),
                                    ALU.subtract).then_inc(lb_dve, 1)
            dve.wait_ge(lb_act, 1)
            nc.vector.tensor_tensor(lb_t[:, 2, :], lb_t[:, 0, :], lb_t[:, 1, :], ALU.add).then_inc(lb_c, 1)
            dve.wait_ge(lb_c, 2)
            nc.vector.reciprocal(lb_t[:, 2, :], lb_t[:, 2, :]).then_inc(lb_c, 1)
            dve.wait_ge(lb_c, 3)
            nc.vector.tensor_tensor(lb_t[:, 0:2, :], lb_t[:, 0:2, :], lb_t[:, 2:3, :].broadcast_to([P, 2, 4]),
                                    ALU.mult).then_inc(lb_c, 1)
            dve.wait_ge(lb_c, 4)
            nc.vector.tensor_tensor(lb[:, 0, :], lb_t[:, 0, :], lb_t[:, 0, :], ALU.subtract).then_inc(lb_c, 1)
            nc.vector.tensor_tensor(lb_t[:, 2, :], lb_t[:, 0, :], lb_t[:, 1, :], ALU.add).then_inc(lb_c, 1)
            dve.wait_ge(lb_c, 6)
            nc.vector.tensor_tensor(lb[:, 1, :], lb_t[:, 2, :], lb_t[:, 0, :], ALU.subtract).then_inc(lb_c, 1)
            dve.wait_ge(lb_c, 7)
            nc.vector.tensor_scalar(lb[:], lb[:], 0.0, 1.0 - 1e-6, ALU.max, ALU.min).then_inc(lb_c, 1)
            dve.wait_ge(lb_c, 8)
            dve.wait_ge(mod_out, 8)
            with dve.Fori(0, L) as l:
                g0, q0, h0 = L * GROUPS1 + l * GROUPS2, L * PAIRS1 + l * PAIRS2, L * HEADS1 + 4 * l
                nc.vector.tensor_copy(par2[:], par2_all[:, l, :]).then_inc(mod_set, 1)
                nc.vector.tensor_tensor(modl[:], modv[:, bass.ds(l * MOD_CHUNKS, MOD_CHUNKS)],
                                        par2_all[:, l, 0:MOD_CHUNKS], ALU.add).then_inc(mod_set, 1)
                nc.vector.tensor_copy(lbc[:, 0, :], lb[:, l, :]).then_inc(mod_set, 1)
                dve.wait_ge(mod_set, 10 * l + 3)
                nc.vector.tensor_scalar(lbc[:, 1, :], lbc[:, 0, :], 1e-30, None, ALU.max).then_inc(mod_set, 1)
                dve.wait_ge(mod_set, 10 * l + 4)
                nc.vector.tensor_scalar(lbc[:, 0, :], lbc[:, 0, :], -1.0, 1.0, ALU.mult, ALU.add).then_inc(mod_set, 1)
                for at in (8, 32, 56):
                    nc.vector.tensor_scalar(modl[:, at:at + 8], modl[:, at:at + 8], 1.0, None, ALU.add)\
                        .then_inc(mod_set, 1)
                for at in (16, 64):
                    nc.vector.tensor_scalar(modl[:, at:at + 8], modl[:, at:at + 8], 0.5, None, ALU.mult)\
                        .then_inc(mod_set, 1)
                dve.wait_ge(mod_set, 10 * l + 10)

                def norm2(k):
                    run = 3 * l + k
                    dve.wait_ge(rn_pe, run + 1)
                    nc.vector.tensor_scalar(rstd[:, 0, :], ps[:, 2, T:2 * T], 1.0 / D, 1e-6, ALU.mult, ALU.add)\
                        .then_inc(rn_dve, 1)
                    dve.wait_ge(rn_act, 6 * run + 6)
                    for q in range(5):
                        if q < 4:
                            for c in (2 * q, 2 * q + 1):
                                at = 24 * k + 8 + c
                                nc.vector.scalar_tensor_tensor(
                                    out=normed[:, c, :], in0=x[:, c, :], scalar=modl[:, at:at + 1],
                                    in1=rstd[:, 0, :], op0=ALU.mult, op1=ALU.mult).then_inc(rn_dve, 1)
                        if q:
                            dve.wait_ge(x_split_hi, 12 * L + 4 * run + q + 4)
                            for c in (2 * q - 2, 2 * q - 1):
                                ins = nc.vector.scalar_tensor_tensor(
                                    out=x_lo[:, c, :], in0=normed[:, c, :], scalar=modl[:, 24 * k + c:24 * k + c + 1],
                                    in1=x_hi[:, c, :].bitcast(F32), op0=ALU.add, op1=ALU.subtract)
                            ins.then_inc(x_split, 1)

                def feeds(p0, p1):
                    for p in range(p0, p1):
                        feed_lo(dve, g0 + p // 4, p % 4)

                def add_down(end, k):
                    dve.wait_ge(panel_used, 4 * g0 + end + 4)
                    for c in range(DC):
                        at = 24 * k + 16 + c
                        ins = nc.vector.scalar_tensor_tensor(
                            out=x[:, c, :], in0=ps[:, 4 + c // 2, (c % 2) * T:(c % 2 + 1) * T],
                            scalar=modl[:, at:at + 1], in1=x[:, c, :], op0=ALU.mult, op1=ALU.add)
                        ins.then_inc(down_out if c % 2 else rn_x, 1)
                        if c % 2:
                            dve.wait_ge(down_out, 4 * (L + 2 * l + k // 2) + (c // 2 + 2))
                            dve.sem_inc(res2, 1)
                norm2(0)
                dve_ffn(dve, g0, GU2A, L + 2 * l, q0 + R_GUA, PANELS2)
                only_feed(dve, g0, DOWN2A + 2, IN2 + 2, feed_lo)
                add_down(IN2, 0)
                norm2(1)
                feeds(IN2 + 2, IN2 + 14)
                fills = [feed_beside(dve, g0, IN2 + p, n, feed_lo, slots, PANELS2) for p, n, slots in IN2_PARTS]
                dve_turn_v(dve, 3 * L + 2 * l)
                dve.wait_ge(consts2_in, 16)
                for t in range(6):
                    fills[0](t)
                    if t < 4:
                        h, b = 4 * l + t, t % 2
                        dve.wait_ge(sb_z, h + 1)
                        if t >= 2:
                            dve.wait_ge(sb_o, h - 1)
                        nc.vector.tensor_scalar(prob[:, b, :], ps[:, 2 + b, :], 0.125, None, ALU.mult)\
                            .then_inc(sb_d, 1)
                        dve.wait_ge(sb_a, 3 * h + 3)
                        dve.wait_ge(sb_d, 2 * h + 1)
                        nc.vector.scalar_tensor_tensor(out=prob_t[:, b, :], in0=prob[:, b, :], scalar=0.0,
                                                       in1=prob_t[:, b, :], op0=ALU.max, op1=ALU.add)\
                            .then_inc(sb_d, 1)
                        dve.wait_ge(sb_d, 2 * h + 2)
                        nc.vector.scalar_tensor_tensor(out=prob_t[:, b, :], in0=prob_t[:, b, :], scalar=-1.0,
                                                       in1=c2("before"), op0=ALU.mult, op1=ALU.mult)\
                            .then_inc(sb_l, 1)
                    if 1 <= t <= 4:
                        h, b = 4 * l + t - 1, (t - 1) % 2
                        dve.wait_ge(sb_t, h + 1)
                        nc.vector.tensor_tensor(prob[:, b, :], prob[:, b, :], ps[:, 4 + b, :], ALU.add)\
                            .then_inc(sb_lw, 1)
                        dve.wait_ge(sb_e, h + 1)
                        nc.vector.scalar_tensor_tensor(out=prob[:, b, :], in0=prob[:, b, :], scalar=1.0,
                                                       in1=c2("before"), op0=ALU.min, op1=ALU.mult)\
                            .then_inc(sb_w, 1)
                    if t >= 2:
                        h = t - 2
                        dve.wait_ge(sb_oh, 4 * l + h + 1)
                        nc.vector.tensor_tensor(mix_lo[even_odd(h), h // 2, :], ps[even_odd(h), 6 + h % 2, 0:T],
                                                mix_hi[even_odd(h), h // 2, :].bitcast(F32), ALU.subtract)\
                            .then_inc(sb_ol, 1)
                dd = 9 * l
                dve.wait_ge(dl_pe, 2 * l + 1)
                for n in range(2):
                    nc.vector.tensor_scalar(rs4[:, 2 * n:2 * n + 2, :], ps[:, 2 + n, :]
                                            .rearrange("p (n w) -> p n w", w=T), 1.0 / 64, 1e-6, ALU.mult, ALU.add)\
                        .then_inc(dl_dve, 1)
                fills[1](0)
                dve.wait_ge(dl_act, 3 * l + 3)
                for n in range(2):
                    v = h_all[:, 6 + 2 * n:8 + 2 * n, :]
                    nc.vector.scalar_tensor_tensor(out=v, in0=v, scalar=par2[:, P2_QG + n:P2_QG + n + 1],
                                                   in1=rs4[:, 2 * n:2 * n + 2, :], op0=ALU.mult, op1=ALU.mult)\
                        .then_inc(dl_dve, 1)
                fills[1](1)
                dve.wait_ge(dl_pe, 2 * l + 2)
                for n in range(2):
                    nc.vector.tensor_tensor(rot_tmp[:, 2 * n:2 * n + 2, :],
                                            ps[:, 2 + n, :].rearrange("p (n w) -> p n w", w=T),
                                            over(c2("sin"), 2), ALU.mult).then_inc(dl_dve, 1)
                v = h_all[:, 6:10, :]
                nc.vector.tensor_tensor(v, v, over(c2("cos"), 4), ALU.mult).then_inc(dl_dve, 1)
                dve.wait_ge(dl_dve, dd + 7)
                nc.vector.tensor_tensor(v, v, rot_tmp[:], ALU.add).then_inc(dl_dve, 1)
                dve.wait_ge(dl_dve, dd + 8)
                dve.sem_inc(dl_dve, 1)
                dve_attention(dve, h0, 4, even_odd, lambda h: mix_hi[:, 2 + h // 2, :],
                              lambda h: mix_lo[:, 2 + h // 2, :], 0.125, lambda t: c2("dilated"), None, fills[2])
                hd = HG * l
                for t in range(2):
                    fills[3](t)
                dve.wait_ge(hg_act, HA * l + 3)
                for c in range(4):
                    nc.vector.tensor_scalar(logf[:, c, :], logf[:, c, :], lbc[:, 0, c:c + 1], lbc[:, 1, c:c + 1],
                                            ALU.mult, ALU.add).then_inc(hg_dve, 1)
                    nc.vector.tensor_scalar(h_all[:, 16 + c, :], h_all[:, 16 + c, :], lbc[:, 0, c:c + 1], None,
                                            ALU.mult).then_inc(hg_dve, 1)
                dve.wait_ge(hg_dve, hd + 8)
                nc.vector.tensor_scalar(logf_b[:], logf[:], 2.0 ** 50, 1.0, ALU.mult, ALU.min).then_inc(hg_dve, 1)
                dve.wait_ge(hg_dve, hd + 9)
                nc.vector.tensor_scalar(logf[:], logf[:], 2.0 ** -50, None, ALU.max).then_inc(hg_dve, 1)
                for t in range(2, 4):
                    fills[3](t)
                dve.wait_ge(hg_act, HA * l + 5)
                nc.vector.tensor_tensor(logf[:], logf[:], logf_b[:], ALU.add).then_inc(hg_dve, 1)
                dve.wait_ge(hg_pe, 3 * l + 1)
                for tile in range(2):
                    nc.vector.tensor_copy(logf_nat[:, tile * 512:(tile + 1) * 512], ps[:, 2 + tile, :])\
                        .then_inc(hg_dve, 1)
                dve_turn_v(dve, 3 * L + 2 * l + 1, v_h)

                def decay(level):
                    dve.wait_ge(hg_exp, 8 * l + level + 1)
                    if level > 2:
                        dve.wait_ge(hg_a, 6 * l + level - 2)
                    b, at = level % 2, slice(0, 2) if level < 7 else slice(1, 2)
                    nc.vector.tensor_tensor(h_qe[b][:, at], q_h[:, at], h_e[b][:, at], ALU.mult).then_inc(hg_qe, 1)
                decay(0)
                for level in range(9):
                    if level < 7:
                        decay(level + 1)
                    b = level % 2
                    bank = 4 + 2 * b
                    dve.wait_ge(hg_s, 9 * l + level + 2)
                    if level == 7:
                        nc.vector.tensor_copy(cross, ps[:, bank, :]).then_inc(hg_m, 1)
                        continue
                    at = level if level < 7 else 7
                    mask = c2("levels")[:, at * P:(at + 1) * P].rearrange("p (o t) -> p o t", o=1)
                    src = ps[:, bank:bank + 2, :].rearrange("p k (h t) -> p (k h) t", h=4)
                    flat = (lambda v: v.rearrange("p k h t -> p (k h) t"))
                    dst = scores if level == 0 else h_qe[b]
                    if level == 8:
                        dve.wait_ge(hg_a, 6 * l + 6)
                    nc.vector.tensor_tensor(flat(dst), src, mask.broadcast_to([P, 8, P]), ALU.mult).then_inc(hg_m, 1)
                    if level:
                        dve.wait_ge(hg_m, 9 * l + level + 1)
                        if level > 1:
                            dve.wait_ge(hg_a, 6 * l + min(level - 1, 6))
                        ins = nc.vector.tensor_tensor(flat(scores), flat(scores), flat(dst), ALU.add)
                        ins.then_inc(hg_a if level < 8 else hg_dve, 1)
                dve.wait_ge(hg_act, HA * l + 7)
                for n in range(2):
                    nc.vector.tensor_copy(o_h[:, 2 * n:2 * n + 2, :],
                                          ps[:, 6 + n, :].rearrange("p (n w) -> p n w", w=T)).then_inc(hg_dve, 1)
                dve.wait_ge(hg_pe, 3 * l + 3)
                for n in range(2):
                    nc.vector.tensor_scalar(F[:, 1024 + 512 * n:1536 + 512 * n], ps[:, 2 + n, :], 1.0 / P, 1e-6,
                                            ALU.mult, ALU.add).then_inc(hg_dve, 1)
                dve.wait_ge(hg_act, HA * l + 9)
                nc.vector.scalar_tensor_tensor(out=o_h[:], in0=o_h[:], scalar=par2[:, P2_HG:P2_HG + 1],
                                               in1=f(1024, 4), op0=ALU.mult, op1=ALU.mult).then_inc(hg_dve, 1)
                dve.wait_ge(hg_dve, hd + 19)
                nc.vector.tensor_tensor(o_h[:], o_h[:], h_all[:, 24:28, :], ALU.mult).then_inc(hg_dve, 1)
                dve.wait_ge(hg_hi, l + 1)
                nc.vector.tensor_tensor(mix_lo[:, 4:8, :], o_h[:], mix_hi[:, 4:8, :].bitcast(F32), ALU.subtract)\
                    .then_inc(hg_dve, 1)
                feeds(OUT2 + 2, OUT2 + 4)
                for q in range(4):
                    dve.wait_ge(panel_used, 4 * g0 + OUT2 + 2 * q + 1 + 5)
                    for c in (2 * q, 2 * q + 1):
                        ins = nc.vector.scalar_tensor_tensor(
                            out=x[:, c, :], in0=ps[:, q % 2, (c % 2) * T:(c % 2 + 1) * T],
                            scalar=modl[:, 40 + c:41 + c], in1=x[:, c, :], op0=ALU.mult, op1=ALU.add)
                        ins.then_inc(pair_out if c % 2 else rn_x, 1)
                    dve.wait_ge(pair_out, q0 + R_OUT + q + 3)
                    dve.sem_inc(res2, 1)
                    feeds(OUT2 + 2 * q + 4, min(OUT2 + 2 * q + 6, GU2B + 2))
                norm2(2)
                dve_ffn(dve, g0, GU2B, L + 2 * l + 1, q0 + R_GUB, PANELS2)
                only_feed(dve, g0, DOWN2B + 2, PANELS2 + 2, feed_lo)
                add_down(PANELS2, 2)


def constants():
    c = {}
    i = np.arange(P)
    t = np.arange(T)
    c["ident"] = np.eye(P)
    c["ones"] = np.ones((P, P))
    rot32 = np.zeros((P, 32))
    for m in range(16):
        rot32[64 + m + 16, m] = -1.0
        rot32[64 + m, m + 16] = 1.0
    c["rot32"] = rot32

    def tiles(a):
        return a.reshape(2, P, -1).transpose(1, 0, 2).reshape(P, -1)
    c["tri"] = tiles((t[:, None] <= t[None, :]).astype(np.float32))
    c["chunk_mask"] = tiles(np.where(t[None, :] // 64 <= t[:, None] // 64, 0.0, NEG))
    c["causal_mask"] = tiles(np.where(t[None, :] <= t[:, None], 0.0, NEG))
    invf = np.zeros((P, 1), np.float32)
    invf[64:96, 0] = np.tile(np.float32(10000.0) ** (-np.arange(16, dtype=np.float32) / np.float32(16)), 2)
    c["invf"] = invf
    c["is_f"] = (i < 8)[:, None] * 1.0
    c["is_one"] = ((i >= 8) & (i < 16))[:, None] * 1.0
    c["head"] = (i[:, None] % 8 == np.arange(8)[None, :]) * 1.0
    c["block64"] = (i[:, None] // 64 == i[None, :] // 64) * 1.0
    rot64 = np.zeros((P, P))
    for b in (0, 64):
        for m in range(32):
            rot64[b + m + 32, b + m] = -1.0
            rot64[b + m, b + m + 32] = 1.0
    c["rot64"] = rot64
    f64 = np.float32(10000.0) ** (-np.arange(32, dtype=np.float32) * np.float32(2.0) / np.float32(64))
    ang = t.astype(np.float32)[None, :] * np.tile(f64, 4)[:, None]
    c["cos"], c["sin"] = np.cos(ang), np.sin(ang)
    dist = t[:, None] - t[None, :]
    count = sum(((dist >= 0) & (dist % s == 0) & (dist // s <= P)).astype(int) for s in (1, 4, 16))
    c["dilated"] = tiles(np.where(count > 0, np.log(np.maximum(count, 1)), NEG))
    spans, levels = [], []
    for h in (1, 2, 4, 8, 16, 32, 64):
        base = i // (2 * h) * (2 * h)
        u, b, s = i[:, None], base[None, :], i[None, :]
        right = (s - b) >= h
        spans.append(np.where(right, (u >= b + h) & (u <= s), (u > s) & (u < b + h)) * 1.0)
        same = base[:, None] == base[None, :]
        levels.append((same & ((i - base)[:, None] < h) & ((i - base)[None, :] >= h)) * 1.0)
    spans.append((i[:, None] > i[None, :]) * 1.0)
    spans.append((i[:, None] <= i[None, :]) * 1.0)
    levels.append(np.eye(P))
    c["spans"], c["levels"] = np.concatenate(spans, 1), np.concatenate(levels, 1)
    c["before"] = tiles((t[:, None] < t[None, :]) * 1.0)
    c["suffix"] = (i[:, None] >= i[None, :]) * 1.0
    return [np.concatenate([np.asarray(c[n], np.float32).reshape(P, w) for n, (_, w) in which.items()], 1)
            for which in (CONSTS, CONSTS2)]


def k_panels(w, cols):
    k, n = w.shape
    a = w.reshape(k // P, P, n // cols, cols).transpose(2, 1, 0, 3).reshape(n // cols, P, -1)
    if a.shape[2] < W:
        a = np.pad(a, ((0, 0), (0, 0), (0, W - a.shape[2])))
    return a


def columns(v):
    return v.reshape(-1, P).T


def kernel(**inputs):
    import concourse.bacc as _bacc
    from concourse.bass_utils import run_bass_kernel_spmd as _run

    a = {n: np.asarray(v) for n, v in inputs.items()}
    stream = []
    for l in range(L):
        w_in = a["w_in"][l]
        b = w_in[:, 1536:2208]
        c_at, f_at, g_at = 2208, 3744, 3752
        z = np.zeros((D, 56), np.float32)
        odd = np.concatenate([w_in[:, f_at:f_at + 8], z, b[:, 640:672], z[:, :32]], 1)
        stream += [k_panels(np.concatenate([b[:, :640], odd], 1), P),
                   k_panels(w_in[:, :512], P), k_panels(a["b_w_uq"][l], 192), k_panels(a["b_w_ukv"][l], 256),
                   k_panels(w_in[:, 512:1536], P), k_panels(w_in[:, c_at:c_at + 1536], P),
                   k_panels(w_in[:, g_at:], P)]
        stream += [k_panels(a["w_branch"][l, n], 256) for n in range(3)]
        stream += [k_panels(a["w_mix_out"][l], P), k_panels(a["xa_w_kv"][l], P), k_panels(a["xa_w_q"][l], P),
                   k_panels(a["xa_w_o"][l], 256)]
        gu = k_panels(a["ffn_w_gu"][l], P)
        stream += [np.stack([gu[:FC], gu[FC:]], 1).reshape(2 * FC, P, W), a["ffn_w_down"][l].reshape(FC, P, W)]
    for l in range(L):
        def ffn(n):
            g, u = (k_panels(a[f"ffn{n}_w_{k}_2"][l], P) for k in ("gate", "up"))
            return [np.stack([g, u], 1).reshape(2 * FC, P, W), a[f"ffn{n}_w_down_2"][l].reshape(FC, P, W)]
        stream += ffn(1) + [k_panels(a["w_in_2"][l], P), k_panels(a["w_out_2"][l], P)] + ffn(2)
    stream.append(np.zeros((RING, P, W), np.float32))
    stream = np.concatenate(stream, 0)

    par1 = np.stack([np.concatenate(
        [columns(a[n][l]) for n in ("ln_mix_g", "ln_mix_b", "ln_xa_g", "ln_xa_b", "ln_ffn_g", "ln_ffn_b")]
        + [columns(a["b_gate"][l].reshape(-1)), columns(a["b_q_norm"][l]), columns(a["b_kv_norm"][l]),
           np.pad(a["b_forget"][l], (0, P - 8))[:, None]], 1) for l in range(L)], 1)
    par2 = np.stack([np.concatenate(
        [columns(a["b_mod_2"][l]), np.tile(a["q_norm_g_2"][l], 2)[:, None], np.tile(a["k_norm_g_2"][l], 2)[:, None],
         a["hgrn_norm_g_2"][l][:, None]], 1) for l in range(L)], 1)
    wmod = np.concatenate([k_panels(a["w_mod_2"][l], P) for l in range(L)], 0)
    wmod = np.concatenate([wmod, wmod[:2]], 0)
    rev = a["a_rel_bias"][:, :, ::-1]
    win = np.lib.stride_tricks.sliding_window_view(np.pad(rev, ((0, 0), (0, 0), (0, 256))), 256, axis=2)
    rel = np.stack([win[:, :, 1 + 64 * b:65 + 64 * b, :] for b in range(4)], 2)

    arrays = {
        "xT": a["x"][0].T.reshape(DC, P, T).transpose(1, 0, 2),
        "memT": a["mem"][0].T.reshape(DC, P, T).transpose(1, 0, 2),
        "pos": a["positions"].reshape(T),
        "c": columns(a["c_2"][0]),
        "lbl": a["hgrn_lb_logits_2"].reshape(L, 4, P).transpose(2, 0, 1),
        "w": stream, "wmod": wmod, "rel": rel, "par1": par1, "par2": par2, "const": constants()[0], "const2": constants()[1],
    }
    arrays = {n: np.ascontiguousarray(v) for n, v in arrays.items()}
    nc = _bacc.Bacc("TRN2", target_bir_lowering=False, num_devices=1)
    io = {n: nc.dram_tensor(f"in_{n}", v.shape, mybir.dt.from_np(v.dtype), kind="ExternalInput").ap()
          for n, v in arrays.items()}
    io["out"] = nc.dram_tensor("out", (P, DC, T), F32, kind="ExternalOutput").ap()
    build(nc, io)
    got = _run(nc, [{f"in_{n}": v for n, v in arrays.items()}], core_ids=[0])
    return got.results[0]["out"].transpose(2, 1, 0).reshape(1, T, D)
```
